# Optimizing a Trainium2 kernel written in Bass

```python
import math
import jax, jax.numpy as jnp
from jax import lax
import numpy as np

D_MODEL = 1024
BATCH = 1
SEQ = 1024
DEPTH = 2

N_ATTN_HEADS = 4
QK_NOPE_DIM = 128
QK_ROPE_DIM = 64
QK_HEAD_DIM = QK_NOPE_DIM + QK_ROPE_DIM
V_HEAD_DIM = 128
Q_RANK = 256
KV_RANK = 128
ATTN_WIDTH = N_ATTN_HEADS * V_HEAD_DIM
ROPE_THETA = 10000.0
Q_BLOCK = 128
CONV_CH = 512
CONV_WIDTH = 31
CONV_PAD = CONV_WIDTH // 2
D_MIX = ATTN_WIDTH + CONV_CH
IN_WIDTH = Q_RANK + KV_RANK + QK_ROPE_DIM + 2 * CONV_CH
N_EXPERTS = 16
CAPACITY_FACTOR = 2
EXPERT_FF = 1024
N_MOD = 6
EPS = 1e-6


def rms_norm(x, g):
    xf = x.astype(jnp.float32)
    y = xf * lax.rsqrt(jnp.mean(xf * xf, axis=-1, keepdims=True) + EPS)
    return (y * g.astype(jnp.float32)).astype(x.dtype)

def layer_norm(x, g, b):
    xf = x.astype(jnp.float32)
    mu = jnp.mean(xf, axis=-1, keepdims=True)
    var = jnp.mean(jnp.square(xf - mu), axis=-1, keepdims=True)
    y = (xf - mu) * lax.rsqrt(var + EPS)
    return (y * g.astype(jnp.float32) + b.astype(jnp.float32)).astype(x.dtype)

def rope_tables(positions):
    inv_freq = 1.0 / (ROPE_THETA ** (jnp.arange(0, QK_ROPE_DIM, 2, dtype=jnp.float32) / QK_ROPE_DIM))
    ang = positions.astype(jnp.float32)[..., None] * inv_freq
    return jnp.cos(ang), jnp.sin(ang)

def apply_rope(x, cos, sin):
    half = x.shape[-1] // 2
    x1 = x[..., :half].astype(jnp.float32)
    x2 = x[..., half:].astype(jnp.float32)
    c = cos[:, :, None, :]
    s = sin[:, :, None, :]
    return jnp.concatenate([x1 * c - x2 * s, x2 * c + x1 * s], axis=-1).astype(x.dtype)

def mla_group(c_q, c_kv, k_rope, cos, sin, q_latent_g, w_uq, kv_latent_g, w_ukv, q_head_g, k_head_g):
    B, S, _ = c_q.shape
    q = jnp.einsum('bsr,rk->bsk', rms_norm(c_q, q_latent_g), w_uq).reshape(B, S, N_ATTN_HEADS, QK_HEAD_DIM)
    kv = jnp.einsum('bsr,rk->bsk', rms_norm(c_kv, kv_latent_g), w_ukv).reshape(
        B, S, N_ATTN_HEADS, QK_NOPE_DIM + V_HEAD_DIM)
    k_nope, v = kv[..., :QK_NOPE_DIM], kv[..., QK_NOPE_DIM:]
    k_r = jnp.broadcast_to(k_rope[:, :, None, :], (B, S, N_ATTN_HEADS, QK_ROPE_DIM))
    k = jnp.concatenate([k_nope, k_r], axis=-1)
    q = rms_norm(q, q_head_g)
    k = rms_norm(k, k_head_g)
    q = jnp.concatenate([q[..., :QK_NOPE_DIM], apply_rope(q[..., QK_NOPE_DIM:], cos, sin)], axis=-1)
    k = jnp.concatenate([k[..., :QK_NOPE_DIM], apply_rope(k[..., QK_NOPE_DIM:], cos, sin)], axis=-1)
    scale = 1.0 / math.sqrt(QK_HEAD_DIM)
    n_blocks = S // Q_BLOCK
    qb = q.reshape(B, n_blocks, Q_BLOCK, N_ATTN_HEADS, QK_HEAD_DIM).transpose(1, 0, 3, 2, 4)
    kt = k.transpose(0, 2, 1, 3)
    vt = v.transpose(0, 2, 1, 3)

    def attend(q_blk):
        s = jnp.einsum('bhqd,bhkd->bhqk', q_blk, kt, preferred_element_type=jnp.float32) * scale
        p = jax.nn.softmax(s, axis=-1).astype(vt.dtype)
        return jnp.einsum('bhqk,bhkd->bhqd', p, vt)

    o = lax.map(attend, qb)
    return o.transpose(1, 0, 3, 2, 4).reshape(B, S, ATTN_WIDTH)

def conv_group(u, conv_w, conv_b, conv_norm_g, conv_norm_b):
    a, g = u[..., :CONV_CH], u[..., CONV_CH:]
    y = a * jax.nn.sigmoid(g)
    y = lax.conv_general_dilated(
        y, conv_w[:, None, :].astype(y.dtype), window_strides=(1,), padding=[(CONV_PAD, CONV_PAD)],
        dimension_numbers=('NWC', 'WIO', 'NWC'), feature_group_count=CONV_CH)
    y = y + conv_b
    return jax.nn.silu(layer_norm(y, conv_norm_g, conv_norm_b))

def expert_choice_ffn(h, w_router, w_gate, w_up, w_down):
    B, S, D = h.shape
    cap = CAPACITY_FACTOR * S // N_EXPERTS
    logits = jnp.einsum('bsd,de->bse', h, w_router).astype(jnp.float32)
    aff = jax.nn.softmax(logits, axis=-1)
    gate, idx = lax.top_k(aff.transpose(0, 2, 1), cap)
    xe = jax.vmap(lambda hb, ib: hb[ib])(h, idx)
    hid = jax.nn.silu(jnp.einsum('becd,edf->becf', xe, w_gate)) * jnp.einsum('becd,edf->becf', xe, w_up)
    ye = jnp.einsum('becf,efd->becd', hid, w_down) * gate[..., None].astype(h.dtype)
    return jax.vmap(lambda ib, yb: jnp.zeros((S, D), yb.dtype).at[ib.reshape(-1)].add(yb.reshape(-1, D)))(idx, ye)

def first_inputs(seed: int = 0) -> dict:
    key = jax.random.key(seed)
    ks = jax.random.split(key, 24)
    f32 = jnp.float32
    nrm = lambda k, shape, s: jax.random.normal(k, shape, f32) * s
    gain = lambda k, shape: 1.0 + 0.05 * jax.random.normal(k, shape, f32)
    L = DEPTH
    offset = jax.random.randint(ks[2], (BATCH, 1), 0, 1024, dtype=jnp.int32)
    positions = offset + jnp.arange(SEQ, dtype=jnp.int32)[None, :]
    return {
        "x": nrm(ks[0], (BATCH, SEQ, D_MODEL), 1.0),
        "c": nrm(ks[1], (BATCH, D_MODEL), 1.0),
        "positions": positions,
        "norm1_g": gain(ks[3], (L, D_MODEL)),
        "w_ada": nrm(ks[4], (L, D_MODEL, N_MOD * D_MODEL), 0.5 * D_MODEL ** -0.5),
        "b_ada": nrm(ks[5], (L, N_MOD * D_MODEL), 0.01),
        "w_in": nrm(ks[6], (L, D_MODEL, IN_WIDTH), D_MODEL ** -0.5),
        "q_latent_g": gain(ks[7], (L, Q_RANK)),
        "w_uq": nrm(ks[8], (L, Q_RANK, N_ATTN_HEADS * QK_HEAD_DIM), Q_RANK ** -0.5),
        "kv_latent_g": gain(ks[9], (L, KV_RANK)),
        "w_ukv": nrm(ks[10], (L, KV_RANK, N_ATTN_HEADS * (QK_NOPE_DIM + V_HEAD_DIM)), KV_RANK ** -0.5),
        "q_head_g": gain(ks[11], (L, QK_HEAD_DIM)),
        "k_head_g": gain(ks[12], (L, QK_HEAD_DIM)),
        "conv_w": nrm(ks[13], (L, CONV_WIDTH, CONV_CH), CONV_WIDTH ** -0.5),
        "conv_b": nrm(ks[14], (L, CONV_CH), 0.01),
        "conv_norm_g": gain(ks[15], (L, CONV_CH)),
        "conv_norm_b": nrm(ks[16], (L, CONV_CH), 0.01),
        "w_out": nrm(ks[17], (L, D_MIX, D_MODEL), D_MIX ** -0.5),
        "norm2_g": gain(ks[18], (L, D_MODEL)),
        "w_router": nrm(ks[19], (L, D_MODEL, N_EXPERTS), D_MODEL ** -0.5),
        "w_gate": nrm(ks[20], (L, N_EXPERTS, D_MODEL, EXPERT_FF), D_MODEL ** -0.5),
        "w_up": nrm(ks[21], (L, N_EXPERTS, D_MODEL, EXPERT_FF), D_MODEL ** -0.5),
        "w_down": nrm(ks[22], (L, N_EXPERTS, EXPERT_FF, D_MODEL), EXPERT_FF ** -0.5),
    }

def first_block(x, c, positions, norm1_g, w_ada, b_ada, w_in, q_latent_g, w_uq, kv_latent_g, w_ukv,
              q_head_g, k_head_g, conv_w, conv_b, conv_norm_g, conv_norm_b, w_out, norm2_g,
              w_router, w_gate, w_up, w_down):
    cos, sin = rope_tables(positions)
    c_act = jax.nn.silu(c)
    o1 = Q_RANK
    o2 = o1 + KV_RANK
    o3 = o2 + QK_ROPE_DIM
    for l in range(DEPTH):
        mod = jnp.einsum('bd,dk->bk', c_act, w_ada[l]) + b_ada[l]
        shift1, scale1, gate1, shift2, scale2, gate2 = [m[:, None, :] for m in jnp.split(mod, N_MOD, axis=-1)]
        h = rms_norm(x, norm1_g[l]) * (1.0 + scale1) + shift1
        proj = jnp.einsum('bsd,dk->bsk', h, w_in[l])
        c_q, c_kv = proj[..., :o1], proj[..., o1:o2]
        k_rope = proj[..., o2:o3]
        conv_u = proj[..., o3:]
        attn_out = mla_group(c_q, c_kv, k_rope, cos, sin, q_latent_g[l], w_uq[l], kv_latent_g[l], w_ukv[l],
                             q_head_g[l], k_head_g[l])
        conv_out = conv_group(conv_u, conv_w[l], conv_b[l], conv_norm_g[l], conv_norm_b[l])
        mix = jnp.einsum('bsk,kd->bsd', jnp.concatenate([attn_out, conv_out], axis=-1), w_out[l])
        x = x + gate1 * mix
        h2 = rms_norm(x, norm2_g[l]) * (1.0 + scale2) + shift2
        x = x + gate2 * expert_choice_ffn(h2, w_router[l], w_gate[l], w_up[l], w_down[l])
    return x


DEPTH_2 = 1

HG_HEADS = 4
HG_KDIM = 128
HG_VDIM = 128
HG_WIDTH = HG_HEADS * HG_KDIM
CHUNK = 32
LRU_WIDTH = 512
LRU_BLOCKS = 8
LRU_BLOCK_DIM = LRU_WIDTH // LRU_BLOCKS
CONV_WIDTH_2 = 4
LRU_C = 8.0
D_MIX_2 = HG_WIDTH + LRU_WIDTH
D_IN = 4 * HG_WIDTH + 2 * LRU_WIDTH
D_FF = -(-8 * D_MODEL // (3 * 256)) * 256


def rms_norm_2(x, w):
    xf = x.astype(jnp.float32)
    y = xf * lax.rsqrt(jnp.mean(xf * xf, axis=-1, keepdims=True) + EPS)
    return (y * w.astype(jnp.float32)).astype(x.dtype)

def hgrn2_mix(q, f_logit, i, g, lb, norm_w):
    B, S, _ = q.shape
    out_dtype = q.dtype
    qf = jax.nn.silu(q.astype(jnp.float32))
    f = lb + (1.0 - lb) * jax.nn.sigmoid(f_logit.astype(jnp.float32))
    log_f = jnp.log(f)
    k = 1.0 - f
    v = i.astype(jnp.float32)
    n_chunks = S // CHUNK

    def to_chunks(t, d):
        return t.reshape(B, n_chunks, CHUNK, HG_HEADS, d).transpose(1, 0, 3, 2, 4)

    qc, kc, gc, vc = to_chunks(qf, HG_KDIM), to_chunks(k, HG_KDIM), to_chunks(log_f, HG_KDIM), to_chunks(v, HG_VDIM)
    causal = jnp.tril(jnp.ones((CHUNK, CHUNK), dtype=bool))

    def step(state, xs):
        q_, k_, lg, v_ = xs
        b = jnp.cumsum(lg, axis=-2)
        b_last = b[..., -1:, :]
        q_dec = q_ * jnp.exp(b)
        k_dec = k_ * jnp.exp(-b)
        scores = jnp.where(causal, jnp.einsum('bhtk,bhsk->bhts', q_dec, k_dec), 0.0)
        o = jnp.einsum('bhts,bhsv->bhtv', scores, v_) + jnp.einsum('bhtk,bhkv->bhtv', q_dec, state)
        k_state = k_ * jnp.exp(b_last - b)
        new_state = jnp.exp(b_last)[..., 0, :, None] * state + jnp.einsum('bhsk,bhsv->bhkv', k_state, v_)
        return new_state, o

    state0 = jnp.zeros((B, HG_HEADS, HG_KDIM, HG_VDIM), jnp.float32)
    _, o = lax.scan(step, state0, (qc, kc, gc, vc))
    o = o.transpose(1, 0, 3, 2, 4).reshape(B, S, HG_HEADS, HG_VDIM)
    o = o * lax.rsqrt(jnp.mean(o * o, axis=-1, keepdims=True) + EPS) * norm_w.astype(jnp.float32)
    o = o * jax.nn.silu(g.astype(jnp.float32).reshape(B, S, HG_HEADS, HG_VDIM))
    return o.reshape(B, S, HG_WIDTH).astype(out_dtype)

def rglru_mix(xb, gate_b, conv_w, conv_b, wa, ba, wx, bx, a_param):
    B, S, W = xb.shape
    out_dtype = xb.dtype
    x_pad = jnp.pad(xb, ((0, 0), (CONV_WIDTH_2 - 1, 0), (0, 0)))
    xc = conv_b + sum(x_pad[:, tap:tap + S] * conv_w[tap] for tap in range(CONV_WIDTH_2))
    xc = xc.astype(jnp.float32)
    xblk = xc.reshape(B, S, LRU_BLOCKS, LRU_BLOCK_DIM)
    r = jax.nn.sigmoid(jnp.einsum('bsnd,nde->bsne', xblk, wa.astype(jnp.float32)).reshape(B, S, W) + ba)
    ig = jax.nn.sigmoid(jnp.einsum('bsnd,nde->bsne', xblk, wx.astype(jnp.float32)).reshape(B, S, W) + bx)
    log_a = -LRU_C * r * jax.nn.softplus(-a_param.astype(jnp.float32))
    a = jnp.exp(log_a)
    b_in = jnp.sqrt(-jnp.expm1(2.0 * log_a)) * (ig * xc)

    def combine(lhs, rhs):
        a1, b1 = lhs
        a2, b2 = rhs
        return a1 * a2, a2 * b1 + b2

    _, h = lax.associative_scan(combine, (a, b_in), axis=1)
    y = h * jax.nn.gelu(gate_b.astype(jnp.float32), approximate=True)
    return y.astype(out_dtype)

def second_inputs(seed: int = 0) -> dict:
    key = jax.random.key(seed)
    ks = jax.random.split(key, 20)
    f32 = jnp.float32
    nrm = lambda k, shape, scale: (jax.random.normal(k, shape, f32) * scale)
    s_lru = jax.random.uniform(ks[12], (DEPTH_2, LRU_WIDTH), f32, 0.9, 0.999) ** (1.0 / LRU_C)
    return {
        'x': nrm(ks[0], (BATCH, SEQ, D_MODEL), 1.0),
        'mix_norm_w': 1.0 + nrm(ks[1], (DEPTH_2, D_MODEL), 0.02),
        'w_in': nrm(ks[2], (DEPTH_2, D_MODEL, D_IN), D_MODEL ** -0.5),
        'hg_lb': nrm(ks[3], (DEPTH_2 + 1, HG_WIDTH), 0.5),
        'hg_norm_w': 1.0 + nrm(ks[4], (DEPTH_2, HG_VDIM), 0.02),
        'conv_w': nrm(ks[5], (DEPTH_2, CONV_WIDTH_2, LRU_WIDTH), CONV_WIDTH_2 ** -0.5),
        'conv_b': nrm(ks[6], (DEPTH_2, LRU_WIDTH), 0.02),
        'lru_wa': nrm(ks[7], (DEPTH_2, LRU_BLOCKS, LRU_BLOCK_DIM, LRU_BLOCK_DIM), LRU_BLOCK_DIM ** -0.5),
        'lru_ba': nrm(ks[8], (DEPTH_2, LRU_WIDTH), 0.02),
        'lru_wx': nrm(ks[9], (DEPTH_2, LRU_BLOCKS, LRU_BLOCK_DIM, LRU_BLOCK_DIM), LRU_BLOCK_DIM ** -0.5),
        'lru_bx': nrm(ks[10], (DEPTH_2, LRU_WIDTH), 0.02),
        'lru_a': jnp.log(s_lru) - jnp.log1p(-s_lru),
        'w_out': nrm(ks[11], (DEPTH_2, D_MIX_2, D_MODEL), D_MIX_2 ** -0.5),
        'ffn_norm_w': 1.0 + nrm(ks[13], (DEPTH_2, D_MODEL), 0.02),
        'w_gate_up': nrm(ks[14], (DEPTH_2, D_MODEL, 2 * D_FF), D_MODEL ** -0.5),
        'w_down': nrm(ks[15], (DEPTH_2, D_FF, D_MODEL), D_FF ** -0.5),
        'final_norm_w': 1.0 + nrm(ks[16], (D_MODEL,), 0.02),
    }

def second_block(x, mix_norm_w, w_in, hg_lb, hg_norm_w, conv_w, conv_b, lru_wa, lru_ba,
              lru_wx, lru_bx, lru_a, w_out, ffn_norm_w, w_gate_up, w_down, final_norm_w):
    lb_all = jnp.cumsum(jax.nn.softmax(hg_lb.astype(jnp.float32), axis=0), axis=0)
    h = x
    for l in range(DEPTH_2):
        xn = rms_norm_2(h, mix_norm_w[l])
        proj = jnp.einsum('bsd,de->bse', xn, w_in[l])
        q, f_logit, i_v, g, lru_x, lru_gate = jnp.split(
            proj, [HG_WIDTH, 2 * HG_WIDTH, 3 * HG_WIDTH, 4 * HG_WIDTH, 4 * HG_WIDTH + LRU_WIDTH], axis=-1)
        o_hg = hgrn2_mix(q, f_logit, i_v, g, lb_all[l], hg_norm_w[l])
        o_lru = rglru_mix(lru_x, lru_gate, conv_w[l], conv_b[l], lru_wa[l], lru_ba[l],
                          lru_wx[l], lru_bx[l], lru_a[l])
        mixed = jnp.concatenate([o_hg, o_lru], axis=-1)
        h = h + jnp.einsum('bse,ed->bsd', mixed, w_out[l])
        hn = rms_norm_2(h, ffn_norm_w[l])
        gate, up = jnp.split(jnp.einsum('bsd,df->bsf', hn, w_gate_up[l]), 2, axis=-1)
        h = h + jnp.einsum('bsf,fd->bsd', jax.nn.silu(gate) * up, w_down[l])
    return rms_norm_2(h, final_norm_w)


def setup_inputs(seed=0):
    out = dict(first_inputs(seed))
    for name, value in second_inputs(seed + 1).items():
        if name != "x":
            out[name + "_2"] = value
    return out


def reference(
    x, c, positions, norm1_g, w_ada, b_ada, w_in, q_latent_g, w_uq, kv_latent_g, w_ukv,
    q_head_g, k_head_g, conv_w, conv_b, conv_norm_g, conv_norm_b, w_out, norm2_g, w_router,
    w_gate, w_up, w_down, mix_norm_w_2, w_in_2, hg_lb_2, hg_norm_w_2, conv_w_2, conv_b_2,
    lru_wa_2, lru_ba_2, lru_wx_2, lru_bx_2, lru_a_2, w_out_2, ffn_norm_w_2, w_gate_up_2,
    w_down_2, final_norm_w_2,
):
    x = first_block(
        x, c, positions, norm1_g, w_ada, b_ada, w_in, q_latent_g, w_uq, kv_latent_g, w_ukv,
        q_head_g, k_head_g, conv_w, conv_b, conv_norm_g, conv_norm_b, w_out, norm2_g, w_router,
        w_gate, w_up, w_down,
    )
    return second_block(
        x, mix_norm_w_2, w_in_2, hg_lb_2, hg_norm_w_2, conv_w_2, conv_b_2, lru_wa_2, lru_ba_2,
        lru_wx_2, lru_bx_2, lru_a_2, w_out_2, ffn_norm_w_2, w_gate_up_2, w_down_2,
        final_norm_w_2,
    )


_drawn_inputs = setup_inputs


def setup_inputs(seed=0):
    import zlib

    import numpy as np

    out = dict(_drawn_inputs(seed))
    spreads = {}
    factors = {'norm1_g': 4.03,
     'b_ada': 3.274,
     'q_latent_g': 8.0,
     'kv_latent_g': 4.405,
     'q_head_g': 8.0,
     'k_head_g': 8.0,
     'conv_b': 6.992,
     'conv_norm_g': 3.014,
     'conv_norm_b': 8.0,
     'norm2_g': 2.926,
     'mix_norm_w_2': 3.621,
     'hg_norm_w_2': 24.519,
     'lru_ba_2': 47.559,
     'lru_bx_2': 29.464,
     'ffn_norm_w_2': 13.245,
     'final_norm_w_2': 7.475,
     'conv_b_2': 4.688}
    for name, (base, spread) in spreads.items():
        noise = np.random.default_rng([zlib.crc32(name.encode()), seed]).standard_normal(out[name].shape)
        drawn = base * np.exp(spread * noise) if base else spread * noise
        out[name] = __import__('jax').numpy.asarray(drawn.astype(out[name].dtype))
    for name, factor in factors.items():
        out[name] = (out[name] * factor).astype(out[name].dtype)
    return out
```

```python
from contextlib import ExitStack

import numpy as np
import concourse.bass as bass
from concourse import mybir

F32 = mybir.dt.float32
I32 = mybir.dt.int32
U32 = mybir.dt.uint32
ALU = mybir.AluOpType
ACT = mybir.ActivationFunctionType
AX = mybir.AxisListType

P = 128
S = 1024
D = 1024
DT = D // P
TB = S // P
HALF = 512
EPS = 1e-6
DEPTH = 2

HEADS = 4
NOPE = 128
ROPE = 64
QK = NOPE + ROPE
VD = 128
Q_RANK = 256
KV_RANK = 128
CONV_CH = 512
CT = CONV_CH // P
TAPS = 31
TAPS_PAD = 32
PAD = TAPS // 2
YW = S + TAPS_PAD
IN_TILES = 12
SCALE = 1.0 / float(np.sqrt(QK))
EXPERTS = 16
CAP = 2 * S // EXPERTS
FF = 1024
FT = FF // P
N_MOD = 6

CHUNK = 32
NCH = S // CHUNK
CPB = P // CHUNK
HG = 4
LT = 4
LTAPS = 4
LRU_C = 8.0
DFF = 2816
FFT = DFF // P
TWO_PI = 2.0 * float(np.pi)

LC = {}
_at = 0
for _name, _n in (("norm1", DT), ("norm2", DT), ("qlat", 2), ("kvlat", 1), ("qg_nope", 1), ("qg_rope", 1),
                  ("kg_nope", 1), ("kg_rope", 1), ("conv_w", CT * TAPS_PAD), ("conv_b", CT),
                  ("conv_g", CT), ("conv_nb", CT)):
    LC[_name] = (_at, _at + _n)
    _at += _n
N_LC = _at
SC = {}
_at = 0
for _name, _n in (("mix_norm", DT), ("lb0", HG), ("lb1", HG), ("hg_norm", 1), ("conv_w", LT * LTAPS),
                  ("conv_b", LT), ("ba", LT), ("bx", LT), ("lru_a", LT), ("ffn_norm", DT), ("final", DT)):
    SC[_name] = (_at, _at + _n)
    _at += _n
N_SC = _at
CC = {}
_at = 0
for _name, _n in (("ident", P), ("ones", P), ("turn", P), ("causal", P), ("half0", 1), ("half1", 1),
                  ("inv_freq", 1), ("cos_shift", 1)):
    CC[_name] = (_at, _at + _n)
    _at += _n
N_CONST = _at


class Chain:

    def __init__(self, eng, sem, base=0):
        self.eng, self.sem, self.base, self.n = eng, sem, base, 0

    def inc(self, ins):
        ins.then_inc(self.sem, 1)
        self.n += 1
        return self.n

    def wait(self, n=None):
        self.eng.wait_ge(self.sem, self.base + (self.n if n is None else n))

    def step(self, ins):
        self.inc(ins)
        self.wait()


def build(nc, A, stop=99, depth=DEPTH):
    sem_names = {}

    with ExitStack() as top:
        def sb(name, shape, dt=F32, ctx=top):
            return ctx.enter_context(nc.sbuf_tensor(name, shape, dt))

        sem_home = [top]

        def sem(name):
            assert name not in sem_names
            sem_names[name] = sem_home[0].enter_context(nc.semaphore(name))
            return sem_names[name]

        psum = top.enter_context(nc.psum_tensor("psum", [P, 8, HALF], F32))

        def bank(i):
            return psum[:, i, :]

        def banks(i):
            return psum[:, i:i + 2, :].rearrange("p a b -> p (a b)")

        h2_rows = nc.dram_tensor("h2_rows", [S, D], F32, kind="Internal").ap()
        moe_rows = nc.dram_tensor("moe_rows", [S, D], F32, kind="Internal").ap()

        const = sb("const", [P, N_CONST])
        x = sb("x", [P, DT, S])
        mod = sb("mod", [P, DEPTH, N_MOD * DT])
        scols = sb("scols", [P, N_SC])
        first_only = top.enter_context(ExitStack())
        cos = sb("cos", [P, S], F32, first_only)
        sin = sb("sin", [P, S], F32, first_only)
        zero_row = sb("zero_row", [P, D], F32, first_only)

        def cc(name):
            return const[:, CC[name][0]:CC[name][1]]

        ident, ones, turn = cc("ident"), cc("ones"), cc("turn")
        ones_col = const[:, CC["ones"][0]:CC["ones"][0] + 1]

        def block_of(i, t):
            return bass.ds(t * P, P) if not isinstance(t, int) else slice(t * P, (t + 1) * P)

        def setup():
            with ExitStack() as ctx:
                pos_i = sb("pos_i", [P, S], I32, ctx)
                ang = sb("ang", [P, S], F32, ctx)
                turns = sb("turns", [P, S], F32, ctx)
                red = sb("red", [P, 2, S], F32, ctx)
                c_col = sb("c_col", [P, DT], F32, ctx)
                c_act = sb("c_act", [P, DT], F32, ctx)
                b_ada = sb("b_ada", [P, DEPTH * N_MOD * DT], F32, ctx)
                ada_w = [sb(f"ada_w{i}", [P, DT, HALF], F32, ctx) for i in range(2)]
                small_in, x_in = sem("su_small_in"), sem("su_x_in")
                ada_in = [sem(f"su_ada_in{i}") for i in range(2)]
                c_ready = sem("su_c_ready")
                ada_done = [sem(f"su_ada_done{i}") for i in range(2)]
                ada_added = [sem(f"su_ada_added{i}") for i in range(2)]
                dve_step, tables_red, tables = sem("su_dve_step"), sem("su_tables_red"), sem("su_tables")
                zeroed = sem("su_zeroed")
                chunks = DEPTH * N_MOD * D // HALF
                with nc.Block() as block:
                    @block.sync
                    def _(sp):
                        sp.dma_start(c_col[:], A["c_cols"]).then_inc(small_in, 16)
                        sp.dma_start(const[:], A["consts"]).then_inc(small_in, 16)
                        sp.dma_start(b_ada[:], A["b_ada_cols"]).then_inc(small_in, 16)
                        sp.dma_start(pos_i[:], A["positions"].to_broadcast((P, S))).then_inc(small_in, 16)
                        sp.dma_start(scols[:], A["second_cols"]).then_inc(small_in, 16)
                        with sp.Fori(0, chunks // 2) as i:
                            for b in range(2):
                                sp.wait_ge(ada_done[b], i)
                                sp.dma_start(ada_w[b][:], A["w_ada"][bass.ds(2 * i + b, 1)].rearrange(
                                    "c (k p) n -> p (c k) n", p=P)).then_inc(ada_in[b], 16)
                        sp.dma_start(x[:], A["x_t"].rearrange("(k p) s -> p k s", p=P)).then_inc(x_in, 16)
                        sp.wait_ge(x_in, 16)

                    @block.gpsimd
                    def _(pool):
                        pool.memset(zero_row[:], 0.0).then_inc(zeroed, 1)

                    @block.tensor
                    def _(pe):
                        pe.wait_ge(c_ready, 1)
                        with pe.Fori(0, chunks // 2) as i:
                            for b in range(2):
                                pe.wait_ge(ada_in[b], 16 * i + 16)
                                pe.wait_ge(ada_added[b], i)
                                for j in range(HALF // P):
                                    for k in range(DT):
                                        mm = pe.matmul(psum[:, b, j:j + 1], ada_w[b][:, k, j * P:(j + 1) * P],
                                                       c_act[:, k:k + 1], start=k == 0, stop=k == DT - 1)
                                mm.then_inc(ada_done[b], 1)

                    @block.scalar
                    def _(act):
                        act.wait_ge(small_in, 80)
                        act.activation(c_act[:], c_col[:], ACT.Silu).then_inc(c_ready, 1)
                        act.wait_ge(tables_red, 2)
                        act.activation(sin[:], red[:, 0, :], ACT.Sin).then_inc(tables, 1)
                        act.activation(cos[:], red[:, 1, :], ACT.Sin).then_inc(tables, 1)

                    @block.vector
                    def _(dve):
                        ch = Chain(dve, dve_step)
                        dve.wait_ge(small_in, 80)
                        ch.step(dve.tensor_copy(turns[:], pos_i[:]))
                        ch.step(dve.tensor_scalar(ang[:], turns[:], cc("inv_freq"), None, ALU.mult))
                        c1 = float(np.float32(6.28125))
                        c2 = float(np.float32(np.floor((TWO_PI - c1) * 2 ** 20) / 2 ** 20))
                        c3 = float(np.float32(TWO_PI - c1 - c2))
                        magic = 12582912.0
                        for f, shift in ((0, 0.0), (1, 0.25)):
                            ch.step(dve.tensor_scalar(turns[:], ang[:], 1.0 / TWO_PI, shift, ALU.mult, ALU.add))
                            ch.step(dve.tensor_scalar(turns[:], turns[:], magic, magic, ALU.add, ALU.subtract))
                            ch.step(dve.scalar_tensor_tensor(out=red[:, f, :], in0=turns[:], scalar=-c1, in1=ang[:],
                                                             op0=ALU.mult, op1=ALU.add))
                            for part in (c2, c3):
                                ch.step(dve.scalar_tensor_tensor(out=red[:, f, :], in0=turns[:], scalar=-part,
                                                                 in1=red[:, f, :], op0=ALU.mult, op1=ALU.add))
                            if f:
                                ch.step(dve.tensor_scalar(red[:, f, :], red[:, f, :], float(np.pi / 2), None, ALU.add))
                            dve.tensor_scalar(red[:, f, :], red[:, f, :], 3.1415925, -3.1415925, ALU.min,
                                              ALU.max).then_inc(tables_red, 1)
                        flat = mod[:].rearrange("p l n -> p (l n)")
                        with dve.Fori(0, chunks // 2) as i:
                            for b in range(2):
                                dve.wait_ge(ada_done[b], i + 1)
                                at = bass.ds((2 * i + b) * (HALF // P), HALF // P)
                                dve.tensor_tensor(flat[:, at], psum[:, b, 0:HALF // P], b_ada[:, at],
                                                  ALU.add).then_inc(ada_added[b], 1)

        def square_tiles(eng_act, eng, src, sq, tiles, done, freed, first):
            for k in tiles:
                if k - tiles[0] >= 2:
                    eng_act.wait_ge(freed, k - tiles[0] - 1)
                eng_act.activation(sq[:, k % 2, :], src[:, k, :], ACT.Square).then_inc(done, 1)

        def sum_tiles(pe, col, sq, n, done, freed):
            for k in range(n):
                pe.wait_ge(done, k + 1)
                for t in range(TB):
                    mm = pe.matmul(col[:, t:t + 1], sq[:, k % 2, t * P:(t + 1) * P], ones_col,
                                   start=k == 0 and t == 0, stop=k == n - 1, skip_group_check=True)
                mm.then_inc(freed, 1)

        def spread(pe, out, diag, ready):
            for t in range(TB):
                pe.wait_ge(ready, t + 1)
                mm = pe.matmul(out[:, t * P:(t + 1) * P], ones, diag[:, t, :], start=True, stop=True)
            return mm

        def norm_tensors(tag, ctx):
            t = {n: sb(f"{tag}_{n}", s, F32, ctx) for n, s in
                 (("sq", [P, 2, S]), ("root", [P, TB]), ("rstd", [P, TB]), ("diag", [P, TB, P]))}
            t.update({n: sem(f"{tag}_{n}") for n in ("sq_done", "sq_free", "root_done", "rstd_done",
                                                     "diag_done", "spread_done")})
            return t

        def norm_act(act, t, src):
            square_tiles(act, act, src, t["sq"], range(DT), t["sq_done"], t["sq_free"], 0)
            act.wait_ge(t["sq_free"], DT)
            act.activation(t["root"][:], psum[:, 0, 0:TB], ACT.Sqrt, bias=EPS, scale=1.0 / D).then_inc(t["root_done"], 1)

        def norm_pe(pe, t):
            sum_tiles(pe, psum[:, 0, 0:TB], t["sq"], DT, t["sq_done"], t["sq_free"])
            spread(pe, banks(2), t["diag"], t["diag_done"]).then_inc(t["spread_done"], 1)

        def norm_dve(dve, t):
            dve.wait_ge(t["root_done"], 1)
            dve.reciprocal(t["rstd"][:], t["root"][:]).then_inc(t["rstd_done"], 1)
            dve.wait_ge(t["rstd_done"], 1)
            for b in range(TB):
                dve.tensor_scalar(t["diag"][:, b, :], ident, t["rstd"][:, b:b + 1], None,
                                  ALU.mult).then_inc(t["diag_done"], 1)
            dve.wait_ge(t["spread_done"], 1)

        def stream_tiles(sp, tiles, bufs, loaded, used, pairs, K):
            with sp.Fori(0, pairs) as i:
                for b in range(2):
                    sp.wait_ge(used[b], i)
                    sp.dma_start(bufs[b][:], tiles(2 * i + b)).then_inc(loaded[b], 16)

        def linear(pe, src, K, bufs, loaded, done, read, pairs, inputs=None):
            with pe.Fori(0, pairs) as i:
                for b in range(2):
                    pe.wait_ge(loaded[b], 16 * i + 16)
                    pe.wait_ge(read[b], i)
                    for k in range(K):
                        if inputs is not None and b == 0:
                            pe.wait_ge(inputs, k + 1)
                        for half in range(2):
                            mm = pe.matmul(bank(4 * b + half), bufs[b][:, k, :],
                                           src(k)[:, half * HALF:(half + 1) * HALF], start=k == 0, stop=k == K - 1)
                    mm.then_inc(done[b], 1)

        def linear_tensors(tag, K, ctx):
            w = [sb(f"{tag}_w{b}", [P, K, P], F32, ctx) for b in range(2)]
            return w, [sem(f"{tag}_loaded{b}") for b in range(2)], [sem(f"{tag}_done{b}") for b in range(2)], \
                [sem(f"{tag}_read{b}") for b in range(2)]

        def tile_of(t):
            return lambda n: t[bass.ds(n, 1)].rearrange("a p (k m) -> p (a k) m", m=P)

        def layer(l):
            with ExitStack() as ctx:
                lcols = sb("lcols", [P, N_LC], F32, ctx)
                modl = sb("modl", [P, N_MOD, DT], F32, ctx)
                gain = sb("gain", [P, 2, DT], F32, ctx)

                def lc(name):
                    return lcols[:, LC[name][0]:LC[name][1]]

                shift = (modl[:, 0, :], modl[:, 3, :])
                gate = (modl[:, 2, :], modl[:, 5, :])
                with ExitStack() as mixing:
                    mix = sb("mix", [P, DT, S], F32, mixing)
                    with ExitStack() as before:
                        y = sb("y", [P, CT, YW], F32, before)
                        lat = sb("lat", [P, 4, S], F32, before)
                        project(l, lcols, modl, gain, lc, shift, lat, y, mix)
                        if stop > 1:
                            q = {n: sb(n, s, F32, before) for n, s in (
                                ("q_nope", [P, HEADS, S]), ("q_rope", [P, HEADS // 2, S]), ("k_nope", [P, HEADS, S]),
                                ("k_rope", [P, HEADS // 2, S]), ("v", [P, TB, HEADS * VD]),
                                ("q_scale", [P, HEADS, TB]), ("q_neg", [P, HEADS, TB]))}
                            heads(l, lc, lat, q)
                        if stop > 2:
                            attend(lc, y, mix, q)
                    if stop > 3:
                        conv_norm(lc, mix)
                        mix_out("lo", tile_of(A["w_out"]), lambda n: n + l * DT, mix, gate[0])
                if stop > 4:
                    experts_part(l, gain, shift[1], gate[1])

        def project(l, lcols, modl, gain, lc, shift, lat, y, mix):
            with ExitStack() as ctx:
                h = sb("h", [P, DT, S], F32, ctx)
                t = norm_tensors("n1", ctx)
                w, loaded, done, read = linear_tensors("in", DT, ctx)
                sig = sb("sig", [P, S], F32, ctx)
                cols_in, gains, scaled, h_ready = sem("pr_cols_in"), sem("pr_gains"), sem("pr_scaled"), sem("pr_h_ready")
                padded = sem("pr_padded")
                with nc.Block() as block:
                    @block.sync
                    def _(sp):
                        sp.dma_start(lcols[:], A["layer_cols"][bass.ds(l, 1)].rearrange("a p n -> p (a n)")).then_inc(cols_in, 16)
                        tiles = tile_of(A["w_in"])
                        stream_tiles(sp, lambda n: tiles(n + l * IN_TILES), w, loaded, done, IN_TILES // 2, DT)

                    @block.gpsimd
                    def _(pool):
                        pool.memset(y[:, :, 0:PAD], 0.0).then_inc(padded, 1)
                        pool.memset(y[:, :, PAD + S:YW], 0.0).then_inc(padded, 1)
                        pool.wait_ge(cols_in, 16)
                        for j in range(CT):
                            pool.tensor_scalar(mix[:, HEADS + j, :], zero_row[:], 1.0, lc("conv_b")[:, j:j + 1],
                                               ALU.mult, ALU.add).then_inc(padded, 1)

                    @block.scalar
                    def _(act):
                        norm_act(act, t, x)
                        act.wait_ge(gains, 5)
                        for k in range(DT):
                            act.wait_ge(scaled, k + 1)
                            act.activation(h[:, k, :], h[:, k, :], ACT.Identity, scale=gain[:, 0, k:k + 1],
                                           bias=shift[0][:, k:k + 1]).then_inc(h_ready, 1)
                        with act.Fori(0, 2) as i:
                            for b in range(2):
                                act.wait_ge(done[b], i + 1)
                                act.copy(lat[:, bass.ds(2 * i + b, 1), :].rearrange("p a s -> p (a s)"),
                                         banks(4 * b)).then_inc(read[b], 1)
                        with act.Fori(0, CT) as j:
                            act.wait_ge(done[0], j + 3)
                            act.wait_ge(read[1], j + 2)
                            act.activation(sig[:], banks(0), ACT.Sigmoid).then_inc(read[0], 1)

                    @block.vector
                    def _(dve):
                        dve.wait_ge(cols_in, 16)
                        dve.tensor_copy(modl[:].rearrange("p a b -> p (a b)"), mod[:, bass.ds(l, 1), :].rearrange(
                            "p l n -> p (l n)")).then_inc(gains, 1)
                        dve.wait_ge(gains, 1)
                        for n, g in ((0, "norm1"), (1, "norm2")):
                            dve.tensor_scalar(gain[:, n, :], modl[:, 3 * n + 1, :], 1.0, None, ALU.add).then_inc(gains, 1)
                            dve.wait_ge(gains, 2 + 2 * n)
                            dve.tensor_tensor(gain[:, n, :], gain[:, n, :], lc(g), ALU.mult).then_inc(gains, 1)
                        norm_dve(dve, t)
                        for k in range(DT):
                            dve.tensor_tensor(h[:, k, :], x[:, k, :], banks(2), ALU.mult).then_inc(scaled, 1)
                        with dve.Fori(0, CT) as j:
                            dve.wait_ge(done[1], j + 3)
                            dve.wait_ge(read[0], j + 3)
                            dve.tensor_tensor(y[:, bass.ds(j, 1), PAD:PAD + S].rearrange("p a s -> p (a s)"),
                                              banks(4), sig[:], ALU.mult).then_inc(read[1], 1)

                    @block.tensor
                    def _(pe):
                        norm_pe(pe, t)
                        linear(pe, lambda k: h[:, k, :], DT, w, loaded, done, read, IN_TILES // 2, h_ready)

        def heads(l, lc, lat, q):
            q_nope, q_rope, k_nope, k_rope, v = q["q_nope"], q["q_rope"], q["k_nope"], q["k_rope"], q["v"]
            with ExitStack() as ctx:
                w_uq = sb("w_uq", [P, 6, 2, P], F32, ctx)
                w_k = sb("w_k", [P, HEADS, P], F32, ctx)
                w_v = sb("w_v", [P, HEADS * VD], F32, ctx)
                sq = sb("hd_sq", [P, 2, S], F32, ctx)
                root = sb("hd_root", [P, 2 + 2 * HEADS, TB], F32, ctx)
                rstd = sb("hd_rstd", [P, 2 + 2 * HEADS, TB], F32, ctx)
                kr_sum = sb("hd_kr_sum", [P, TB], F32, ctx)
                diag = sb("hd_diag", [P, TB, P], F32, ctx)
                rot = sb("hd_rot", [P, S], F32, ctx)
                names = ("w_in", "sq_done", "summed", "lat_root", "lat_rstd", "diag_done", "spread_done", "lat_done",
                         "prod", "raw_done", "v_prod", "v_copied", "kr_copied", "k_sums", "roots", "rstds",
                         "q_scaled", "turned", "sin_part", "cos_part", "roped", "k_done")
                (w_in, sq_done, summed, lat_root, lat_rstd, diag_done, spread_done, lat_done, prod, raw_done, v_prod,
                 v_copied, kr_copied, k_sums, roots, rstds, q_scaled, turned, sin_part, cos_part, roped,
                 k_done) = [sem("hd_" + n) for n in names]
                tiles = [("q", h) for h in range(HEADS)] + [("r", 0), ("r", 1)] + [("k", h) for h in range(HEADS)]
                dest = {"q": q_nope, "r": q_rope, "k": k_nope}
                gains = {"q": "qg_nope", "r": "qg_rope", "k": "kg_nope"}
                lat_sums = psum[:, 6, 0:2 * TB]
                sums = psum[:, 7, 0:9 * TB].rearrange("p (a t) -> p a t", t=TB)
                n_sq = 4 + len(tiles)

                with nc.Block() as block:
                    @block.sync
                    def _(sp):
                        sp.dma_start(w_uq[:].rearrange("p n k m -> p (n k m)"), A["w_uq"][bass.ds(l, 1)].rearrange(
                            "a p n -> p (a n)")).then_inc(w_in, 16)
                        sp.dma_start(w_k[:].rearrange("p n m -> p (n m)"), A["w_uk"][bass.ds(l, 1)].rearrange(
                            "a p n -> p (a n)")).then_inc(w_in, 16)
                        sp.dma_start(w_v[:], A["w_uv"][bass.ds(l, 1)].rearrange("a p n -> p (a n)")).then_inc(w_in, 16)

                    @block.scalar
                    def _(act):
                        for k in range(4):
                            if k >= 2:
                                act.wait_ge(summed, k - 1)
                            act.activation(sq[:, k % 2, :], lat[:, k, :], ACT.Square).then_inc(sq_done, 1)
                            if k == 2:
                                act.wait_ge(summed, 3)
                                act.activation(root[:, 0, :], lat_sums[:, 0:TB], ACT.Sqrt, bias=EPS,
                                               scale=1.0 / Q_RANK).then_inc(lat_root, 1)
                                act.activation(root[:, 1, :], lat_sums[:, TB:2 * TB], ACT.Sqrt, bias=EPS,
                                               scale=1.0 / KV_RANK).then_inc(lat_root, 1)
                        for n in range(len(tiles)):
                            act.wait_ge(prod, n + 1)
                            act.wait_ge(summed, n + 3)
                            act.activation(sq[:, n % 2, :], banks(2 * (n % 2)), ACT.Square).then_inc(sq_done, 1)
                        for t in range(TB):
                            act.wait_ge(v_prod, t + 1)
                            act.copy(v[:, t, :], bank(4 + t % 2)).then_inc(v_copied, 1)
                        act.wait_ge(k_sums, 2)
                        act.activation(root[:, 2:2 + HEADS, :], sums[:, 0:HEADS, :], ACT.Sqrt, bias=EPS,
                                       scale=1.0 / QK).then_inc(roots, 1)
                        act.activation(root[:, 2 + HEADS:, :], rstd[:, 2 + HEADS:, :], ACT.Sqrt, bias=EPS,
                                       scale=1.0 / QK).then_inc(roots, 1)

                    @block.gpsimd
                    def _(pool):
                        for n in range(3):
                            rows = q_rope[:, n, :] if n < 2 else lat[:, 3, :]
                            pool.wait_ge(turned, n + 1)
                            pool.tensor_tensor(rows, rows, cos[:], ALU.mult).then_inc(cos_part, 1)

                    @block.vector
                    def _(dve):
                        dve.wait_ge(lat_root, 2)
                        dve.reciprocal(rstd[:, 0:2, :], root[:, 0:2, :]).then_inc(lat_rstd, 1)
                        dve.wait_ge(lat_rstd, 1)
                        for g in range(2):
                            if g:
                                dve.wait_ge(spread_done, 1)
                            for t in range(TB):
                                dve.tensor_scalar(diag[:, t, :], ident, rstd[:, g, t:t + 1], None,
                                                  ALU.mult).then_inc(diag_done, 1)
                        for k, name in ((0, "qlat"), (1, "qlat"), (2, "kvlat")):
                            dve.wait_ge(spread_done, 1 + k // 2)
                            col = lc(name)[:, k % 2:k % 2 + 1]
                            dve.scalar_tensor_tensor(out=lat[:, k, :], in0=lat[:, k, :], scalar=col, in1=banks(2 * (k // 2)),
                                                     op0=ALU.mult, op1=ALU.mult).then_inc(lat_done, 1)
                        dve.wait_ge(sq_done, 4)
                        dve.tensor_scalar(lat[:, 3, :], lat[:, 3, :], lc("kg_rope"), None, ALU.mult).then_inc(lat_done, 1)
                        for n, (kind, j) in enumerate(tiles):
                            dve.wait_ge(sq_done, 5 + n)
                            dve.tensor_scalar(dest[kind][:, j, :], banks(2 * (n % 2)), lc(gains[kind]), None,
                                              ALU.mult).then_inc(raw_done, 1)
                        for n in range(3):
                            rows = q_rope[:, n, :] if n < 2 else lat[:, 3, :]
                            dve.wait_ge(turned, n + 1)
                            if n:
                                dve.wait_ge(roped, n)
                            dve.tensor_tensor(rot[:], banks(2 * (n % 2)), sin[:], ALU.mult).then_inc(sin_part, 1)
                            dve.wait_ge(sin_part, n + 1)
                            dve.wait_ge(cos_part, n + 1)
                            dve.tensor_tensor(rows, rows, rot[:], ALU.add).then_inc(roped, 1)
                        dve.wait_ge(summed, n_sq)
                        dve.tensor_copy(kr_sum[:], sums[:, 8, :]).then_inc(k_sums, 1)
                        dve.wait_ge(k_sums, 1)
                        dve.tensor_tensor(rstd[:, 2 + HEADS:, :], sums[:, HEADS:2 * HEADS, :],
                                          kr_sum[:].unsqueeze(1).to_broadcast([P, HEADS, TB]), ALU.add).then_inc(k_sums, 1)
                        dve.wait_ge(roots, 2)
                        dve.reciprocal(rstd[:, 2:, :], root[:, 2:, :]).then_inc(rstds, 1)
                        dve.wait_ge(rstds, 1)
                        dve.tensor_scalar(q["q_scale"][:], rstd[:, 2:2 + HEADS, :], SCALE, None, ALU.mult).then_inc(q_scaled, 1)
                        dve.tensor_scalar(q["q_neg"][:], rstd[:, 2:2 + HEADS, :], -SCALE, None, ALU.mult).then_inc(q_scaled, 1)
                        dve.wait_ge(roped, 3)
                        for h in range(HEADS):
                            dve.wait_ge(spread_done, 2 + h)
                            for t in range(TB):
                                dve.tensor_scalar(diag[:, t, :], ident, rstd[:, 2 + HEADS + h, t:t + 1], None,
                                                  ALU.mult).then_inc(diag_done, 1)
                            dve.wait_ge(spread_done, 3 + h)
                            over = banks(2 * (h % 2))
                            half = slice(ROPE * (h % 2), ROPE * (h % 2) + ROPE)
                            dve.tensor_tensor(k_nope[:, h, :], k_nope[:, h, :], over, ALU.mult).then_inc(k_done, 1)
                            dve.tensor_tensor(k_rope[half, h // 2, :], lat[half, 3, :], over[half, :],
                                              ALU.mult).then_inc(k_done, 1)

                    @block.tensor
                    def _(pe):
                        def add_squares(n, out, col, first):
                            for t in range(TB):
                                mm = pe.matmul(out[:, t:t + 1], sq[:, n % 2, t * P:(t + 1) * P], col,
                                               start=first and t == 0, stop=True, skip_group_check=True)
                            return mm

                        for k in range(3):
                            pe.wait_ge(sq_done, k + 1)
                            add_squares(k, lat_sums[:, (k // 2) * TB:(k // 2 + 1) * TB], ones_col, k == 0).then_inc(summed, 1)
                        pe.wait_ge(sq_done, 4)
                        add_squares(3, sums[:, 8, :], cc("half0"), True).then_inc(summed, 1)
                        for g in range(2):
                            for t in range(TB):
                                pe.wait_ge(diag_done, g * TB + t + 1)
                                mm = pe.matmul(banks(2 * g)[:, t * P:(t + 1) * P], ones, diag[:, t, :], start=True, stop=True)
                            mm.then_inc(spread_done, 1)
                        pe.wait_ge(w_in, 48)
                        pe.wait_ge(lat_done, 3)

                        def sums_of(n):
                            kind, j = tiles[n]
                            pe.wait_ge(sq_done, 5 + n)
                            if kind == "r":
                                add_squares(n, sums[:, 2 * j, :], cc("half0"), False)
                                mm = add_squares(n, sums[:, 2 * j + 1, :], cc("half1"), False)
                            else:
                                mm = add_squares(n, sums[:, j + (HEADS if kind == "k" else 0), :], ones_col, False)
                            mm.then_inc(summed, 1)

                        for n, (kind, j) in enumerate(tiles):
                            if n >= 2:
                                pe.wait_ge(sq_done, 3 + n)
                                pe.wait_ge(raw_done, n - 1)
                            for k in range(1 if kind == "k" else 2):
                                wt = w_k[:, j, :] if kind == "k" else w_uq[:, j + (HEADS if kind == "r" else 0), k, :]
                                src = lat[:, 2 if kind == "k" else k, :]
                                for half in range(2):
                                    mm = pe.matmul(bank(2 * (n % 2) + half), wt, src[:, half * HALF:(half + 1) * HALF],
                                                   start=k == 0, stop=kind == "k" or k == 1)
                            mm.then_inc(prod, 1)
                            if n:
                                sums_of(n - 1)
                        sums_of(len(tiles) - 1)
                        for t in range(TB):
                            if t >= 2:
                                pe.wait_ge(v_copied, t - 1)
                            pe.matmul(bank(4 + t % 2), lat[:, 2, t * P:(t + 1) * P], w_v[:], start=True,
                                      stop=True).then_inc(v_prod, 1)
                        pe.wait_ge(raw_done, len(tiles))
                        pe.wait_ge(lat_done, 4)
                        for n in range(3):
                            if n >= 2:
                                pe.wait_ge(sin_part, n - 1)
                            src = q_rope[:, n, :] if n < 2 else lat[:, 3, :]
                            for half in range(2):
                                mm = pe.matmul(bank(2 * (n % 2) + half), turn, src[:, half * HALF:(half + 1) * HALF],
                                               start=True, stop=True)
                            mm.then_inc(turned, 1)
                        pe.wait_ge(sin_part, 3)
                        for h in range(HEADS):
                            if h >= 2:
                                pe.wait_ge(k_done, 2 * (h - 1))
                            for t in range(TB):
                                pe.wait_ge(diag_done, (2 + h) * TB + t + 1)
                                mm = pe.matmul(banks(2 * (h % 2))[:, t * P:(t + 1) * P], ones, diag[:, t, :], start=True, stop=True)
                            mm.then_inc(spread_done, 1)

        def attend(lc, y, mix, q):
            q_nope, q_rope, k_nope, k_rope, v = q["q_nope"], q["q_rope"], q["k_nope"], q["k_rope"], q["v"]
            with ExitStack() as ctx:
                qs_nope = sb("qs_nope", [P, HEADS, P], F32, ctx)
                qs_rope = sb("qs_rope", [P, HEADS // 2, P], F32, ctx)
                probs = sb("probs", [P, 2, S], F32, ctx)
                probs_t = sb("probs_t", [P, 2, TB, P], F32, ctx)
                neg_max = sb("neg_max", [P, 2], F32, ctx)
                row_max = sb("row_max", [P, 2], F32, ctx)
                row_sum = sb("row_sum", [P, 2], F32, ctx)
                inv_sum = sb("inv_sum", [P, 2], F32, ctx)
                taps = sb("taps", [P, TAPS_PAD // 2], F32, ctx)
                names = ("scores_done", "maxes", "neg_done", "exp_done", "inv_done", "probs_done", "conv_step", "taps_in")
                scores_done, maxes, neg_done, exp_done, inv_done, probs_done, conv_step, taps_in = [sem("at_" + n) for n in names]
                staged = [sem(f"at_staged{p}") for p in range(HEADS // 2)]
                turned = [sem(f"at_turned{b}") for b in range(2)]
                copied = [sem(f"at_copied{b}") for b in range(2)]
                pv_done = [sem(f"at_pv_done{b}") for b in range(2)]
                out_copied = [sem(f"at_out_copied{b}") for b in range(2)]
                n_conv = TAPS_PAD // 2

                def score_slot(s):
                    return banks(2 * s)

                with nc.Block() as block:
                    @block.gpsimd
                    def _(pool):
                        def stage(pair, blk, at):
                            pool.tensor_copy(qs_nope[:, 2 * pair:2 * pair + 2, :], q_nope[:, 2 * pair:2 * pair + 2, at]).then_inc(staged[pair], 1)
                            pool.tensor_copy(qs_rope[:, pair, :], q_rope[:, pair, at]).then_inc(staged[pair], 1)

                        for pair in range(HEADS // 2):
                            stage(pair, 0, slice(0, P))
                        with pool.Fori(0, CT) as j:
                            with pool.Fori(0, 2) as part:
                                blk = 2 * j + part
                                nxt = (blk + 1) % TB
                                pool.wait_ge(conv_step, 2 * n_conv * blk)
                                pool.tensor_copy(taps[:], lc("conv_w")[:, bass.ds((2 * j + part) * n_conv, n_conv)]).then_inc(taps_in, 1)
                                for pair in range(HEADS // 2):
                                    pool.wait_ge(scores_done, HEADS * blk + 2 * pair + 2)
                                    stage(pair, blk + 1, bass.ds(nxt * P, P))

                    @block.tensor
                    def _(pe):
                        def scores(h, slot, blk):
                            pe.wait_ge(staged[h // 2], 2 * blk + 2)
                            rows = slice(ROPE * (h % 2), ROPE * (h % 2) + ROPE)
                            for half in range(2):
                                at = slice(half * HALF, (half + 1) * HALF)
                                pe.matmul(bank(2 * slot + half), qs_nope[:, h, :], k_nope[:, h, at], start=True, stop=False)
                                mm = pe.matmul(bank(2 * slot + half), qs_rope[rows, h // 2, :], k_rope[rows, h // 2, at],
                                               start=False, stop=True)
                            mm.then_inc(scores_done, 1)

                        scores(0, 0, 0)
                        scores(1, 1, 0)
                        with pe.Fori(0, CT) as j:
                            with pe.Fori(0, 2) as part:
                                blk = 2 * j + part
                                for h in range(HEADS):
                                    g = HEADS * blk + h
                                    slot = h % 2
                                    pe.wait_ge(probs_done, g + 1)
                                    for b in range(2):
                                        pe.wait_ge(copied[b], g)
                                        for t in range(TB // 2):
                                            k = b * (TB // 2) + t
                                            mm = pe.transpose(psum[:, 4 + b, t * P:(t + 1) * P], probs[:, slot, k * P:(k + 1) * P], ident)
                                        mm.then_inc(turned[b], 1)
                                    scores((h + 2) % HEADS, slot, blk + (h + 2) // HEADS)
                                    pe.wait_ge(out_copied[slot], 2 * blk + h // 2)
                                    for k in range(TB):
                                        if k % (TB // 2) == 0:
                                            pe.wait_ge(copied[k // (TB // 2)], g + 1)
                                        mm = pe.matmul(psum[:, 6 + slot, 0:P], v[:, k, h * VD:(h + 1) * VD], probs_t[:, slot, k, :],
                                                       start=k == 0, stop=k == TB - 1)
                                    mm.then_inc(pv_done[slot], 1)

                    @block.scalar
                    def _(act):
                        def exps(h, slot, g, blk):
                            act.wait_ge(neg_done, g + 1)
                            act.activation(probs[:, slot, :], score_slot(slot), ACT.Exp, bias=neg_max[:, slot:slot + 1],
                                           scale=q["q_scale"][:, h, blk], accum_out=row_sum[:, slot:slot + 1]).then_inc(exp_done, 1)

                        exps(0, 0, 0, slice(0, 1))
                        exps(1, 1, 1, slice(0, 1))
                        with act.Fori(0, CT) as j:
                            with act.Fori(0, 2) as part:
                                blk = 2 * j + part
                                nxt = (blk + 1) % TB
                                for h in range(HEADS):
                                    g = HEADS * blk + h
                                    slot = h % 2
                                    act.wait_ge(pv_done[slot], 2 * blk + h // 2)
                                    for b in range(2):
                                        act.wait_ge(turned[b], g + 1)
                                        act.copy(probs_t[:, slot, b * (TB // 2):(b + 1) * (TB // 2), :],
                                                 psum[:, 4 + b, :].rearrange("p (t m) -> p t m", m=P)).then_inc(copied[b], 1)
                                    exps((h + 2) % HEADS, slot, g + 2, bass.ds(blk if h < 2 else nxt, 1))
                                    act.wait_ge(pv_done[slot], 2 * blk + h // 2 + 1)
                                    act.copy(mix[:, h, bass.ds(blk * P, P)], psum[:, 6 + slot, 0:P]).then_inc(out_copied[slot], 1)

                    @block.vector
                    def _(dve):
                        def maxima(h, slot, g, blk):
                            dve.wait_ge(scores_done, g + 1)
                            dve.reduce_max(row_max[:, slot:slot + 1], score_slot(slot), AX.X).then_inc(maxes, 1)
                            dve.wait_ge(maxes, g + 1)
                            dve.tensor_scalar(neg_max[:, slot:slot + 1], row_max[:, slot:slot + 1], q["q_neg"][:, h, blk], None,
                                              ALU.mult).then_inc(neg_done, 1)

                        def normalise(slot, g):
                            dve.wait_ge(exp_done, g + 1)
                            dve.reciprocal(inv_sum[:, slot:slot + 1], row_sum[:, slot:slot + 1]).then_inc(inv_done, 1)
                            dve.wait_ge(inv_done, g + 1)
                            dve.tensor_scalar(probs[:, slot, :], probs[:, slot, :], inv_sum[:, slot:slot + 1], None,
                                              ALU.mult).then_inc(probs_done, 1)

                        def conv_taps(j, part, blk, first, n):
                            for t in range(first, first + n):
                                for half in range(2):
                                    if t or half:
                                        dve.wait_ge(conv_step, 2 * n_conv * blk + 2 * t + half - 1)
                                    at = mix[:, bass.ds(j + HEADS, 1), half * HALF:(half + 1) * HALF].rearrange("p a s -> p (a s)")
                                    src = y[:, bass.ds(j, 1), bass.ds(part * n_conv + t + half * HALF, HALF)].rearrange("p a s -> p (a s)")
                                    dve.scalar_tensor_tensor(out=at, in0=src, scalar=taps[:, t:t + 1], in1=at,
                                                             op0=ALU.mult, op1=ALU.add).then_inc(conv_step, 1)

                        maxima(0, 0, 0, slice(0, 1))
                        maxima(1, 1, 1, slice(0, 1))
                        with dve.Fori(0, CT) as j:
                            with dve.Fori(0, 2) as part:
                                blk = 2 * j + part
                                nxt = (blk + 1) % TB
                                dve.wait_ge(taps_in, blk + 1)
                                dve.wait_ge(conv_step, 2 * n_conv * blk)
                                for h in range(HEADS):
                                    g = HEADS * blk + h
                                    slot = h % 2
                                    normalise(slot, g)
                                    conv_taps(j, part, blk, h * n_conv // HEADS, n_conv // HEADS)
                                    maxima((h + 2) % HEADS, slot, g + 2, bass.ds(blk if h < 2 else nxt, 1))

        def conv_norm(lc, mix):
            with ExitStack() as ctx:
                sq = sb("cn_sq", [P, CT, S], F32, ctx)
                stat = sb("cn_stat", [P, 3, TB], F32, ctx)
                diag = sb("cn_diag", [P, 2, TB, P], F32, ctx)
                names = ("mean_sum", "mean", "diag", "spread", "centred", "sq", "var_sum", "root", "rstd", "scaled", "silu")
                mean_sum, mean, diag_done, spread_done, centred, sq_done, var_sum, root, rstd, scaled, silu = [sem("cn_" + n) for n in names]
                rows = [mix[:, HEADS + j, :] for j in range(CT)]
                with nc.Block() as block:
                    @block.tensor
                    def _(pe):
                        def sums(src, out, ready):
                            for j in range(CT):
                                if ready is not None:
                                    pe.wait_ge(ready, j + 1)
                                for t in range(TB):
                                    mm = pe.matmul(out[:, t:t + 1], src(j)[:, t * P:(t + 1) * P], ones_col,
                                                   start=j == 0 and t == 0, stop=j == CT - 1, skip_group_check=True)
                            return mm

                        sums(lambda j: rows[j], psum[:, 0, 0:TB], None).then_inc(mean_sum, 1)
                        for g in range(2):
                            for t in range(TB):
                                pe.wait_ge(diag_done, g * TB + t + 1)
                                mm = pe.matmul(banks(2 + 2 * g)[:, t * P:(t + 1) * P], ones, diag[:, g, t, :], start=True, stop=True)
                            mm.then_inc(spread_done, 1)
                            if g == 0:
                                sums(lambda j: sq[:, j, :], psum[:, 1, 0:TB], sq_done).then_inc(var_sum, 1)

                    @block.vector
                    def _(dve):
                        dve.wait_ge(mean_sum, 1)
                        dve.tensor_scalar(stat[:, 0, :], psum[:, 0, 0:TB], 1.0 / CONV_CH, None, ALU.mult).then_inc(mean, 1)
                        dve.wait_ge(mean, 1)
                        for t in range(TB):
                            dve.tensor_scalar(diag[:, 0, t, :], ident, stat[:, 0, t:t + 1], None, ALU.mult).then_inc(diag_done, 1)
                        dve.wait_ge(spread_done, 1)
                        for j in range(CT):
                            dve.tensor_tensor(rows[j], rows[j], banks(2), ALU.subtract).then_inc(centred, 1)
                        dve.wait_ge(root, 1)
                        dve.reciprocal(stat[:, 2, :], stat[:, 1, :]).then_inc(rstd, 1)
                        dve.wait_ge(rstd, 1)
                        for t in range(TB):
                            dve.tensor_scalar(diag[:, 1, t, :], ident, stat[:, 2, t:t + 1], None, ALU.mult).then_inc(diag_done, 1)
                        dve.wait_ge(spread_done, 2)
                        dve.wait_ge(centred, CT)
                        for j in range(CT):
                            dve.tensor_tensor(rows[j], rows[j], banks(4), ALU.mult).then_inc(scaled, 1)

                    @block.scalar
                    def _(act):
                        for j in range(CT):
                            act.wait_ge(centred, j + 1)
                            act.activation(sq[:, j, :], rows[j], ACT.Square).then_inc(sq_done, 1)
                        act.wait_ge(var_sum, 1)
                        act.activation(stat[:, 1, :], psum[:, 1, 0:TB], ACT.Sqrt, bias=EPS, scale=1.0 / CONV_CH).then_inc(root, 1)
                        for j in range(CT):
                            act.wait_ge(scaled, j + 1)
                            act.activation(rows[j], rows[j], ACT.Silu, scale=lc("conv_g")[:, j:j + 1],
                                           bias=lc("conv_nb")[:, j:j + 1]).then_inc(silu, 1)

        def mix_out(tag, tiles, index, mix, gate):
            with ExitStack() as ctx:
                w, loaded, done, read = linear_tensors(tag, DT, ctx)
                with nc.Block() as block:
                    @block.sync
                    def _(sp):
                        stream_tiles(sp, lambda n: tiles(index(n)), w, loaded, done, DT // 2, DT)

                    @block.tensor
                    def _(pe):
                        linear(pe, lambda k: mix[:, k, :], DT, w, loaded, done, read, DT // 2)

                    @block.vector
                    def _(dve):
                        add_to_x(dve, done, read, gate)

        def add_to_x(dve, done, read, gate):
            with dve.Fori(0, DT // 2) as i:
                for b in range(2):
                    dve.wait_ge(done[b], i + 1)
                    xn = x[:, bass.ds(2 * i + b, 1), :].rearrange("p a s -> p (a s)")
                    if gate is None:
                        ins = dve.tensor_tensor(xn, banks(4 * b), xn, ALU.add)
                    else:
                        ins = dve.scalar_tensor_tensor(out=xn, in0=banks(4 * b), scalar=gate[:, bass.ds(2 * i + b, 1)],
                                                       in1=xn, op0=ALU.mult, op1=ALU.add)
                    ins.then_inc(read[b], 1)

        def experts_part(l, gain, shift, gate):
            with ExitStack() as ctx:
                slots = sb("slots", [P, EXPERTS], U32, ctx)
                slot_gate = sb("slot_gate", [P, EXPERTS], F32, ctx)
                route(l, gain, shift, slots, slot_gate)
                if stop > 5:
                    run_experts(l, slots, slot_gate)
                    combine(gate)

        def route(l, gain, shift, slots, slot_gate):
            with ExitStack() as ctx:
                h = sb("rt_h", [P, DT, S], F32, ctx)
                t = norm_tensors("n2", ctx)
                w_r = sb("w_r", [P, DT, EXPERTS], F32, ctx)
                logit = sb("logit", [EXPERTS, S], F32, ctx)
                aff = sb("aff", [P, TB, EXPERTS], F32, ctx)
                stat = sb("rt_stat", [P, 3, TB], F32, ctx)
                aff_t = sb("aff_t", [EXPERTS, S], F32, ctx)
                best = sb("best", [EXPERTS, CAP], F32, ctx)
                place = sb("place", [EXPERTS, CAP], U32, ctx)
                place_f = sb("place_f", [EXPERTS, CAP], F32, ctx)
                part = sb("rt_part", [P, 2, DT, P], F32, ctx)
                rows = sb("rt_rows", [P, 2, D], F32, ctx)
                names = ("w_in", "scaled", "h_ready", "logits", "logit_copied", "turned", "soft", "exp_done", "aff_done",
                         "aff_turned", "aff_copied", "pick", "place_done", "back", "slots_done", "zeroed", "rows_out")
                (w_in, scaled, h_ready, logits, logit_copied, turned, soft, exp_done, aff_done, aff_turned, aff_copied, pick,
                 place_done, back, slots_done, zeroed, rows_out) = [sem("rt_" + n) for n in names]
                part_in = [sem(f"rt_part_in{b}") for b in range(2)]
                row_turned = [sem(f"rt_row_turned{b}") for b in range(2)]
                row_copied = [sem(f"rt_row_copied{b}") for b in range(2)]
                soft_psum = psum[:, 4, 0:TB * EXPERTS].rearrange("p (t e) -> p t e", e=EXPERTS)
                with nc.Block() as block:
                    @block.sync
                    def _(sp):
                        sp.dma_start(w_r[:], A["w_router"][bass.ds(l, 1)].rearrange("a (k p) e -> p (a k) e", p=P)).then_inc(w_in, 16)
                        with sp.Fori(0, TB) as i:
                            sp.dma_start(moe_rows[bass.ds(i * P, P), :], zero_row[:]).then_inc(zeroed, 16)
                        with sp.Fori(0, TB // 2) as i:
                            for b in range(2):
                                sp.wait_ge(row_copied[b], i + 1)
                                sp.dma_start(h2_rows[bass.ds((2 * i + b) * P, P), :], rows[:, b, :]).then_inc(rows_out, 16)
                        sp.wait_ge(zeroed, 16 * TB)
                        sp.wait_ge(rows_out, 16 * TB)

                    @block.gpsimd
                    def _(pool):
                        pool.wait_ge(h_ready, DT)
                        with pool.Fori(0, TB // 2) as i:
                            for b in range(2):
                                pool.wait_ge(row_turned[b], i)
                                pool.tensor_copy(part[:, b, :, :], h[:, :, bass.ds((2 * i + b) * P, P)]).then_inc(part_in[b], 1)

                    @block.scalar
                    def _(act):
                        norm_act(act, t, x)
                        for k in range(DT):
                            act.wait_ge(scaled, k + 1)
                            act.activation(h[:, k, :], h[:, k, :], ACT.Identity, scale=gain[:, 1, k:k + 1],
                                           bias=shift[:, k:k + 1]).then_inc(h_ready, 1)
                        act.wait_ge(logits, 1)
                        act.copy(logit[:], banks(0)[0:EXPERTS, :]).then_inc(logit_copied, 1)
                        act.wait_ge(soft, 2)
                        act.activation(aff[:], aff[:], ACT.Exp).then_inc(exp_done, 1)
                        act.wait_ge(aff_turned, 1)
                        act.copy(aff_t[:], banks(0)[0:EXPERTS, :]).then_inc(aff_copied, 1)
                        with act.Fori(0, TB // 2) as i:
                            for b in range(2):
                                act.wait_ge(row_turned[b], i + 1)
                                if b == 0:
                                    act.wait_ge(rows_out, 32 * i)
                                else:
                                    act.wait_ge(rows_out, 32 * i)
                                act.copy(rows[:, b, :], banks(2 + 4 * b)).then_inc(row_copied[b], 1)

                    @block.vector
                    def _(dve):
                        norm_dve(dve, t)
                        for k in range(DT):
                            dve.tensor_tensor(h[:, k, :], x[:, k, :], banks(2), ALU.mult).then_inc(scaled, 1)
                        dve.wait_ge(turned, 1)
                        dve.tensor_reduce(stat[:, 0, :], soft_psum, AX.X, ALU.max).then_inc(soft, 1)
                        dve.wait_ge(soft, 1)
                        dve.tensor_tensor(aff[:], soft_psum, stat[:, 0, :].unsqueeze(2).to_broadcast([P, TB, EXPERTS]),
                                          ALU.subtract).then_inc(soft, 1)
                        dve.wait_ge(exp_done, 1)
                        dve.tensor_reduce(stat[:, 1, :], aff[:], AX.X, ALU.add).then_inc(soft, 1)
                        dve.wait_ge(soft, 3)
                        dve.reciprocal(stat[:, 2, :], stat[:, 1, :]).then_inc(soft, 1)
                        dve.wait_ge(soft, 4)
                        dve.tensor_tensor(aff[:], aff[:], stat[:, 2, :].unsqueeze(2).to_broadcast([P, TB, EXPERTS]),
                                          ALU.mult).then_inc(aff_done, 1)
                        dve.wait_ge(aff_copied, 1)
                        ch = Chain(dve, pick)
                        for r in range(CAP // 8):
                            at = slice(8 * r, 8 * r + 8)
                            ch.step(dve.max(best[:, at], aff_t[:]))
                            ch.step(dve.max_index(place[:, at], best[:, at], aff_t[:]))
                            ch.step(dve.match_replace(aff_t[:], best[:, at], aff_t[:], -1.0))
                        dve.tensor_copy(place_f[:], place[:]).then_inc(place_done, 1)
                        dve.wait_ge(back, 1)
                        dve.tensor_copy(slots[:], psum[:, 5, 0:EXPERTS]).then_inc(slots_done, 1)
                        dve.tensor_copy(slot_gate[:], psum[:, 5, EXPERTS:2 * EXPERTS]).then_inc(slots_done, 1)

                    @block.tensor
                    def _(pe):
                        norm_pe(pe, t)
                        pe.wait_ge(w_in, 16)
                        for k in range(DT):
                            pe.wait_ge(h_ready, k + 1)
                            for half in range(2):
                                mm = pe.matmul(bank(half)[0:EXPERTS, :], w_r[:, k, :], h[:, k, half * HALF:(half + 1) * HALF],
                                               start=k == 0, stop=k == DT - 1)
                        mm.then_inc(logits, 1)
                        pe.wait_ge(logit_copied, 1)
                        for b in range(TB):
                            mm = pe.transpose(soft_psum[:, b, :], logit[:, b * P:(b + 1) * P], ident[0:EXPERTS, 0:EXPERTS])
                        mm.then_inc(turned, 1)
                        pe.wait_ge(aff_done, 1)
                        for b in range(TB):
                            mm = pe.transpose(banks(0)[0:EXPERTS, b * P:(b + 1) * P], aff[:, b, :], ident)
                        mm.then_inc(aff_turned, 1)
                        with pe.Fori(0, TB // 2) as i:
                            for b in range(2):
                                pe.wait_ge(part_in[b], i + 1)
                                pe.wait_ge(row_copied[b], i)
                                for k in range(DT):
                                    mm = pe.transpose(banks(2 + 4 * b)[:, k * P:(k + 1) * P], part[:, b, k, :], ident)
                                mm.then_inc(row_turned[b], 1)
                        pe.wait_ge(place_done, 1)
                        pe.transpose(psum[:, 5, 0:EXPERTS], place_f[:], ident[0:EXPERTS, 0:EXPERTS])
                        pe.transpose(psum[:, 5, EXPERTS:2 * EXPERTS], best[:], ident[0:EXPERTS, 0:EXPERTS]).then_inc(back, 1)

        def run_experts(l, slots, slot_gate):
            with ExitStack() as ctx:
                wg = [sb(f"wg{f}", [P, DT, HALF], F32, ctx) for f in range(2)]
                wu = [sb(f"wu{f}", [P, DT, HALF], F32, ctx) for f in range(2)]
                wd = [sb(f"wd{f}", [P, FT // 2, D], F32, ctx) for f in range(2)]
                idx_in = sb("idx_in", [P, 1], U32, ctx)
                idx_out = sb("idx_out", [P, 1], U32, ctx)
                xe = sb("xe", [P, D], F32, ctx)
                xe_t = sb("xe_t", [P, DT, P], F32, ctx)
                act_g = sb("act_g", [P, 2, HALF], F32, ctx)
                hid = sb("hid", [P, 2, HALF], F32, ctx)
                hid_t = sb("hid_t", [P, FT, P], F32, ctx)
                ye = sb("ye", [P, D], F32, ctx)
                names = ("idx_in", "gathered", "idx_out", "scattered", "silu", "hid", "xe_t", "hid_t", "ye")
                idx_in_done, gathered, idx_out_done, scattered, silu_done, hid_done, xe_t_done, hid_t_done, ye_done = [sem("ex_" + n) for n in names]
                parts = ("g0", "u0", "g1", "u1", "d0", "d1")
                loaded = {n: sem("ex_loaded_" + n) for n in parts}
                done = {n: sem("ex_done_" + n) for n in parts}
                turned = [sem(f"ex_turned{b}") for b in range(2)]
                buf = {"g0": wg[0], "g1": wg[1], "u0": wu[0], "u1": wu[1], "d0": wd[0], "d1": wd[1]}

                def source(n, e):
                    f = int(n[1])
                    if n[0] == "d":
                        return A["w_down"][bass.ds(l * EXPERTS + e, 1), f * HALF:(f + 1) * HALF, :].rearrange("a (k p) n -> p (a k) n", p=P)
                    w = A["w_gate"] if n[0] == "g" else A["w_up"]
                    return w[bass.ds(l * EXPERTS + e, 1), :, f * HALF:(f + 1) * HALF].rearrange("a (k p) n -> p (a k) n", p=P)

                with nc.Block() as block:
                    @block.sync
                    def _(sp):
                        with sp.Fori(0, EXPERTS) as e:
                            for n in parts:
                                sp.wait_ge(done[n], e)
                                sp.dma_start(buf[n][:], source(n, e)).then_inc(loaded[n], 16)

                    @block.gpsimd
                    def _(pool):
                        def gather(e, count):
                            pool.tensor_copy(idx_in[:], slots[:, bass.ds(e, 1)]).then_inc(idx_in_done, 1)
                            pool.wait_ge(idx_in_done, 1)
                            pool.wait_ge(idx_in_done, count)
                            pool.indirect_dma_start(xe[:], None, h2_rows, bass.IndirectOffsetOnAxis(ap=idx_in[:, 0:1], axis=0)).then_inc(gathered, 16)

                        gather(0, 1)
                        with pool.Fori(0, EXPERTS) as e:
                            picked, written = pool.snap(pool.to_reg(e + 2)), pool.snap(pool.to_reg(2 * e + 2))
                            placed = pool.snap(pool.to_reg(e + 1))
                            pool.wait_ge(turned[1], 2 * e + 1)
                            pool.wait_ge(gathered, 16 * e + 16)
                            gather((e + 1) % EXPERTS, picked)
                            pool.wait_ge(scattered, 16 * e)
                            pool.tensor_copy(idx_out[:], slots[:, bass.ds(e, 1)]).then_inc(idx_out_done, 1)
                            pool.wait_ge(idx_out_done, 1)
                            pool.wait_ge(idx_out_done, placed)
                            pool.wait_ge(ye_done, written)
                            pool.indirect_dma_start(moe_rows, bass.IndirectOffsetOnAxis(ap=idx_out[:, 0:1], axis=0), ye[:], None,
                                                    compute_op=ALU.add).then_inc(scattered, 16)
                        pool.wait_ge(scattered, 16 * EXPERTS)
                        pool.wait_ge(gathered, 16 * EXPERTS + 16)

                    @block.tensor
                    def _(pe):
                        def turn_rows(e, use):
                            pe.wait_ge(gathered, 16 * e + 16)
                            for b in range(2):
                                for k in range(DT // 2):
                                    mm = pe.transpose(psum[:, 4 + b, k * P:(k + 1) * P], xe[:, (4 * b + k) * P:(4 * b + k + 1) * P], ident)
                                mm.then_inc(turned[b], 1)

                        turn_rows(0, 0)
                        with pe.Fori(0, EXPERTS) as e:
                            for f in range(2):
                                for n, at in (("g", 2 * f), ("u", 2 * f + 1)):
                                    part = n + str(f)
                                    pe.wait_ge(loaded[part], 16 * e + 16)
                                    if f == 0 and n == "g":
                                        pe.wait_ge(xe_t_done, 2 * e + 2)
                                    pe.wait_ge(hid_done if n == "u" else silu_done, 2 * e + f if f == 0 else 2 * e)
                                    for k in range(DT):
                                        mm = pe.matmul(bank(at), xe_t[:, k, :], buf[part][:, k, :], start=k == 0, stop=k == DT - 1)
                                    mm.then_inc(done[part], 1)
                            pe.wait_ge(hid_t_done, 2 * e)
                            turn_rows(e + 1, 0)
                            for b in range(2):
                                pe.wait_ge(hid_done, 2 * e + b + 1)
                                pe.wait_ge(xe_t_done, 2 * e + 2 + b + 1)
                                for k in range(FT // 2):
                                    mm = pe.transpose(psum[:, 4 + b, k * P:(k + 1) * P], hid[:, b, k * P:(k + 1) * P], ident)
                                mm.then_inc(turned[b], 1)
                            for f in range(2):
                                pe.wait_ge(loaded[f"d{f}"], 16 * e + 16)
                                pe.wait_ge(hid_t_done, 2 * e + f + 1)
                                if f == 0:
                                    pe.wait_ge(ye_done, 2 * e)
                                for k in range(FT // 2):
                                    for o in range(2):
                                        mm = pe.matmul(bank(6 + o), hid_t[:, f * (FT // 2) + k, :], wd[f][:, k, o * HALF:(o + 1) * HALF],
                                                       start=f == 0 and k == 0, stop=f == 1 and k == FT // 2 - 1)
                                mm.then_inc(done[f"d{f}"], 1)

                    @block.scalar
                    def _(act):
                        def rows_out_of_psum(use):
                            for b in range(2):
                                act.wait_ge(turned[b], use)
                                act.copy(xe_t[:, 4 * b:4 * b + 4, :], psum[:, 4 + b, :].rearrange("p (k m) -> p k m", m=P)).then_inc(xe_t_done, 1)

                        rows_out_of_psum(1)
                        with act.Fori(0, EXPERTS) as e:
                            for f in range(2):
                                act.wait_ge(done[f"g{f}"], e + 1)
                                act.wait_ge(hid_done, 2 * e + f if f == 0 else 2 * e)
                                act.activation(act_g[:, f, :], bank(2 * f), ACT.Silu).then_inc(silu_done, 1)
                            rows_out_of_psum(2 * e + 2)
                            for b in range(2):
                                act.wait_ge(turned[b], 2 * e + 3)
                                act.copy(hid_t[:, 4 * b:4 * b + 4, :], psum[:, 4 + b, :].rearrange("p (k m) -> p k m", m=P)).then_inc(hid_t_done, 1)

                    @block.vector
                    def _(dve):
                        with dve.Fori(0, EXPERTS) as e:
                            for f in range(2):
                                dve.wait_ge(done[f"u{f}"], e + 1)
                                dve.wait_ge(silu_done, 2 * e + f + 1)
                                dve.wait_ge(turned[f], 2 * e + 1)
                                dve.tensor_tensor(hid[:, f, :], act_g[:, f, :], bank(2 * f + 1), ALU.mult).then_inc(hid_done, 1)
                            dve.wait_ge(done["d1"], e + 1)
                            dve.wait_ge(scattered, 16 * e)
                            for o in range(2):
                                dve.tensor_scalar(ye[:, o * HALF:(o + 1) * HALF], bank(6 + o), slot_gate[:, bass.ds(e, 1)], None,
                                                  ALU.mult).then_inc(ye_done, 1)

        def combine(gate):
            with ExitStack() as ctx:
                rows = [sb(f"cb_rows{b}", [P, TB, P], F32, ctx) for b in range(2)]
                loaded = [sem(f"cb_loaded{b}") for b in range(2)]
                turned = [sem(f"cb_turned{b}") for b in range(2)]
                read = [sem(f"cb_read{b}") for b in range(2)]
                with nc.Block() as block:
                    @block.sync
                    def _(sp):
                        with sp.Fori(0, DT // 2) as i:
                            for b in range(2):
                                sp.wait_ge(turned[b], i)
                                sp.dma_start(rows[b][:], moe_rows[:, bass.ds((2 * i + b) * P, P)].rearrange("(t p) m -> p t m", p=P)).then_inc(loaded[b], 16)

                    @block.tensor
                    def _(pe):
                        with pe.Fori(0, DT // 2) as i:
                            for b in range(2):
                                pe.wait_ge(loaded[b], 16 * i + 16)
                                pe.wait_ge(read[b], i)
                                for t in range(TB):
                                    mm = pe.transpose(banks(4 * b)[:, t * P:(t + 1) * P], rows[b][:, t, :], ident)
                                mm.then_inc(turned[b], 1)

                    @block.vector
                    def _(dve):
                        add_to_x(dve, turned, read, gate)

        def second(out):
            def s2(name):
                return scols[:, SC[name][0]:SC[name][1]]

            with ExitStack() as ctx:
                mix = sb("mix2", [P, DT, S], F32, ctx)
                v = sb("v2", [P, TB, HG * P], F32, ctx)
                qfg = sb("qfg", [P, 3, HG, S], F32, ctx)
                with ExitStack() as lru_ctx:
                    lru_x = sb("lru_x", [P, LT, LTAPS - 1 + S], F32, lru_ctx)
                    lru_g = sb("lru_g", [P, LT, S], F32, lru_ctx)
                    norm_and_values(mix, v, s2("mix_norm"))
                    if stop > 7:
                        project2(mix, qfg, lru_x, lru_g)
                    if stop > 8:
                        recurrent_unit(mix, lru_x, lru_g, s2)
                if stop > 9:
                    hgrn(mix, v, qfg, s2)
                if stop > 10:
                    tiles = tile_of(A["w_out_2"])
                    mix_out("so", tiles, lambda n: n, mix, None)
            if stop > 11:
                with ExitStack() as ctx:
                    hid = sb("hid2", [P, FFT, S], F32, ctx)
                    feed_forward_up(hid, s2("ffn_norm"))
                    feed_forward_down(hid)
            if stop > 12:
                final_norm(out, s2("final"))

        def scale_rows(dve, dst, gain, done):
            for k in range(DT):
                dve.scalar_tensor_tensor(out=dst[:, k, :], in0=x[:, k, :], scalar=gain[:, k:k + 1], in1=banks(2),
                                         op0=ALU.mult, op1=ALU.mult).then_inc(done, 1)

        def norm_and_values(xn, v, gain):
            with ExitStack() as ctx:
                t = norm_tensors("n3", ctx)
                w_i = sb("w_i", [P, DT, HG * P], F32, ctx)
                part = sb("nv_part", [P, 2, DT, P], F32, ctx)
                w_in, scaled = sem("nv_w_in"), sem("nv_scaled")
                part_in = [sem(f"nv_part_in{b}") for b in range(2)]
                prod = [sem(f"nv_prod{b}") for b in range(2)]
                copied = [sem(f"nv_copied{b}") for b in range(2)]
                with nc.Block() as block:
                    @block.sync
                    def _(sp):
                        sp.dma_start(w_i[:], A["w_i_2"].rearrange("(k p) n -> p k n", p=P)).then_inc(w_in, 16)

                    @block.gpsimd
                    def _(pool):
                        pool.wait_ge(scaled, DT)
                        with pool.Fori(0, TB // 2) as i:
                            for b in range(2):
                                pool.wait_ge(prod[b], i)
                                pool.tensor_copy(part[:, b, :, :], xn[:, :, bass.ds((2 * i + b) * P, P)]).then_inc(part_in[b], 1)

                    @block.tensor
                    def _(pe):
                        norm_pe(pe, t)
                        pe.wait_ge(w_in, 16)
                        with pe.Fori(0, TB // 2) as i:
                            for b in range(2):
                                pe.wait_ge(part_in[b], i + 1)
                                pe.wait_ge(copied[b], i)
                                for k in range(DT):
                                    mm = pe.matmul(bank(4 + b), part[:, b, k, :], w_i[:, k, :], start=k == 0, stop=k == DT - 1)
                                mm.then_inc(prod[b], 1)

                    @block.scalar
                    def _(act):
                        norm_act(act, t, x)
                        with act.Fori(0, TB // 2) as i:
                            for b in range(2):
                                act.wait_ge(prod[b], i + 1)
                                act.copy(v[:, bass.ds(2 * i + b, 1), :].rearrange("p a n -> p (a n)"), bank(4 + b)).then_inc(copied[b], 1)

                    @block.vector
                    def _(dve):
                        norm_dve(dve, t)
                        scale_rows(dve, xn, gain, scaled)

        def project2(xn, qfg, lru_x, lru_g):
            with ExitStack() as ctx:
                w, loaded, done, read = linear_tensors("p2", DT, ctx)
                padded = sem("p2_padded")
                groups = [(ACT.Silu, lambda n: qfg[:, 0, n, :]), (ACT.Sigmoid, lambda n: qfg[:, 1, n, :]),
                          (ACT.Silu, lambda n: qfg[:, 2, n, :]), (ACT.Copy, lambda n: lru_x[:, n, LTAPS - 1:]),
                          (ACT.Gelu_apprx_tanh, lambda n: lru_g[:, n, :])]
                n_pairs = len(groups) * HG // 2
                with nc.Block() as block:
                    @block.sync
                    def _(sp):
                        stream_tiles(sp, tile_of(A["w_in_2"]), w, loaded, done, n_pairs, DT)

                    @block.gpsimd
                    def _(pool):
                        pool.memset(lru_x[:, :, 0:LTAPS - 1], 0.0).then_inc(padded, 1)

                    @block.tensor
                    def _(pe):
                        linear(pe, lambda k: xn[:, k, :], DT, w, loaded, done, read, n_pairs)

                    @block.scalar
                    def _(act):
                        for g, (func, dst) in enumerate(groups):
                            for n in range(HG):
                                act.wait_ge(done[n % 2], 2 * g + n // 2 + 1)
                                act.activation(dst(n), banks(4 * (n % 2)), func).then_inc(read[n % 2], 1)

        def recurrent_unit(mix, lru_x, lru_g, s2):
            with ExitStack() as ctx:
                w_a = sb("w_a", [P, LT, P], F32, ctx)
                w_x = sb("w_x", [P, LT, P], F32, ctx)
                xc = sb("xc", [P, LT, S], F32, ctx)
                r = sb("lru_r", [P, S], F32, ctx)
                ig = sb("lru_ig", [P, S], F32, ctx)
                a = sb("lru_a", [P, S], F32, ctx)
                th = sb("lru_th", [P, S], F32, ctx)
                wide = sb("lru_wide", [P, S], F32, ctx)
                state = sb("lru_state", [P, S], F32, ctx)
                sp_col = sb("lru_sp", [P, 8, LT], F32, ctx)
                names = ("zeroed", "w_in", "col", "col_act", "conv", "prod", "gates", "decay", "dve", "rooted")
                zeroed, w_in, col, col_act, conv, prod, gates, decay, dve_step, rooted = [sem("ru_" + n) for n in names]
                per_tile = 9
                absneg, u, w1, lnw, d, rd, zero, rate = (sp_col[:, i, :] for i in range(8))
                with nc.Block() as block:
                    @block.sync
                    def _(sp):
                        sp.wait_ge(zeroed, 2)
                        for w, name in ((w_a, "lru_wa"), (w_x, "lru_wx")):
                            for half in range(2):
                                at = slice(half * 64, half * 64 + 64)
                                sp.dma_start(w[at, :, at], A[name].rearrange("(n two) d e -> two d n e", two=2)[half]).then_inc(w_in, 16)

                    @block.gpsimd
                    def _(pool):
                        pool.memset(w_a[:], 0.0).then_inc(zeroed, 1)
                        pool.memset(w_x[:], 0.0).then_inc(zeroed, 1)

                    @block.vector
                    def _(dve):
                        cs = Chain(dve, col)
                        la = s2("lru_a")
                        cs.step(dve.tensor_scalar(u, la, -1.0, None, ALU.mult))
                        cs.step(dve.tensor_tensor(absneg, la, u, ALU.min))
                        dve.wait_ge(col_act, 1)
                        cs.step(dve.tensor_scalar(w1, rate, 1.0, None, ALU.add))
                        cs.step(dve.tensor_scalar(d, w1, -1.0, None, ALU.add))
                        cs.step(dve.tensor_scalar(zero, d, 0.0, None, ALU.is_equal))
                        cs.step(dve.tensor_scalar(d, d, 1e-30, None, ALU.max))
                        cs.step(dve.reciprocal(rd, d))
                        dve.wait_ge(col_act, 2)
                        cs.step(dve.tensor_tensor(rd, rd, lnw, ALU.mult))
                        cs.step(dve.tensor_tensor(rd, rd, zero, ALU.add))
                        cs.step(dve.tensor_tensor(rd, rd, rate, ALU.mult))
                        cs.step(dve.scalar_tensor_tensor(out=u, in0=u, scalar=0.0, in1=rd, op0=ALU.max, op1=ALU.add))
                        cs.step(dve.tensor_scalar(d, u, LRU_C, None, ALU.mult))
                        cs.step(dve.tensor_scalar(zero, u, -LRU_C, None, ALU.mult))
                        cw, cb = s2("conv_w"), s2("conv_b")
                        for t in range(LTAPS):
                            for j in range(LT):
                                src = lru_x[:, j, t:t + S]
                                tap = cw[:, j * LTAPS + t:j * LTAPS + t + 1]
                                if t == 0:
                                    ins = dve.tensor_scalar(xc[:, j, :], src, tap, cb[:, j:j + 1], ALU.mult, ALU.add)
                                else:
                                    dve.wait_ge(conv, LT * (t - 1) + j + 1)
                                    ins = dve.scalar_tensor_tensor(out=xc[:, j, :], in0=src, scalar=tap, in1=xc[:, j, :],
                                                                   op0=ALU.mult, op1=ALU.add)
                                ins.then_inc(conv, 1)
                        ch = Chain(dve, dve_step)
                        for j in range(LT):
                            dve.wait_ge(gates, 2 * j + 2)
                            ch.step(dve.tensor_tensor(ig[:], ig[:], xc[:, j, :], ALU.mult))
                            dve.wait_ge(decay, 2 * j + 2)
                            ch.step(dve.tensor_tensor(wide[:], a[:], a[:], ALU.mult))
                            ch.step(dve.scalar_tensor_tensor(out=wide[:], in0=wide[:], scalar=1.0, in1=th[:], op0=ALU.add, op1=ALU.mult))
                            dve.wait_ge(rooted, j + 1)
                            ch.step(dve.tensor_tensor(wide[:], wide[:], ig[:], ALU.mult))
                            ch.step(dve.tensor_tensor_scan(state[:], a[:], wide[:], 0.0, ALU.mult, ALU.add))
                            ch.step(dve.tensor_tensor(mix[:, HG + j, :], state[:], lru_g[:, j, :], ALU.mult))
                        assert ch.n == 6 * LT

                    @block.scalar
                    def _(act):
                        act.wait_ge(col, 2)
                        act.activation(rate, absneg, ACT.Exp).then_inc(col_act, 1)
                        act.wait_ge(col, 3)
                        act.activation(lnw, w1, ACT.Ln).then_inc(col_act, 1)
                        act.wait_ge(col, 13)
                        for j in range(LT):
                            act.wait_ge(prod, 2 * j + 1)
                            act.wait_ge(decay, 2 * j)
                            if j:
                                act.wait_ge(dve_step, 6 * j)
                            act.activation(r[:], banks(0), ACT.Sigmoid, bias=s2("ba")[:, j:j + 1]).then_inc(gates, 1)
                            act.wait_ge(prod, 2 * j + 2)
                            act.activation(ig[:], banks(4), ACT.Sigmoid, bias=s2("bx")[:, j:j + 1]).then_inc(gates, 1)
                            act.wait_ge(gates, 2 * j + 1)
                            act.activation(a[:], r[:], ACT.Exp, scale=zero[:, j:j + 1]).then_inc(decay, 1)
                            act.activation(th[:], r[:], ACT.Tanh, scale=d[:, j:j + 1]).then_inc(decay, 1)
                            act.wait_ge(dve_step, 6 * j + 3)
                            act.activation(wide[:], wide[:], ACT.Sqrt).then_inc(rooted, 1)

                    @block.tensor
                    def _(pe):
                        pe.wait_ge(w_in, 64)
                        for j in range(LT):
                            pe.wait_ge(conv, LT * (LTAPS - 1) + j + 1)
                            for n, w in ((0, w_a), (1, w_x)):
                                if j:
                                    pe.wait_ge(gates, 2 * (j - 1) + n + 1)
                                for half in range(2):
                                    mm = pe.matmul(bank(4 * n + half), w[:, j, :], xc[:, j, half * HALF:(half + 1) * HALF], start=True, stop=True)
                                mm.then_inc(prod, 1)

        def hgrn(mix, v, qfg, s2):
            with ExitStack() as ctx:
                kd = sb("kd", [P, HG, S], F32, ctx)
                cum = sb("hg_cum", [P, 2, S], F32, ctx)
                diff = sb("hg_diff", [P, 2, S], F32, ctx)
                last = sb("hg_last", [P, HG, NCH], F32, ctx)
                lb = sb("hg_lb", [P, 3, HG], F32, ctx)
                reset = sb("hg_reset", [P, S], F32, ctx)
                names = ("lb", "lb_act", "reset", "keys", "logs", "cums", "grow", "shrink", "diffs", "tail", "q_dec", "k_dec", "k_state")
                lbs, lb_act, reset_done, keys, logs, cums, grow, shrink, diffs, tail, q_dec, k_dec, k_state = [sem("hp_" + n) for n in names]
                q, f, g = (qfg[:, i, :, :] for i in range(3))
                with nc.Block() as block:
                    @block.gpsimd
                    def _(pool):
                        pool.memset(reset[:], 1.0).then_inc(reset_done, 1)
                        pool.wait_ge(reset_done, 1)
                        pool.memset(reset[:].rearrange("p (c t) -> p c t", t=CHUNK)[:, :, 0:1], 0.0).then_inc(reset_done, 1)

                    @block.scalar
                    def _(act):
                        act.wait_ge(lbs, 1)
                        act.activation(lb[:, 1, :], lb[:, 0, :], ACT.Sigmoid).then_inc(lb_act, 1)
                        for h in range(HG):
                            b = h % 2
                            act.wait_ge(keys, 2 * h + 2)
                            act.activation(f[:, h, :], f[:, h, :], ACT.Ln).then_inc(logs, 1)
                        for h in range(HG):
                            b = h % 2
                            act.wait_ge(cums, h + 1)
                            act.activation(f[:, h, :], cum[:, b, :], ACT.Exp).then_inc(grow, 1)
                            act.wait_ge(diffs, h + 1)
                            act.activation(cum[:, b, :], cum[:, b, :], ACT.Exp, scale=-1.0).then_inc(shrink, 1)
                            act.activation(diff[:, b, :], diff[:, b, :], ACT.Exp).then_inc(tail, 1)

                    @block.vector
                    def _(dve):
                        dve.tensor_tensor(lb[:, 0, :], s2("lb0"), s2("lb1"), ALU.subtract).then_inc(lbs, 1)
                        dve.wait_ge(lb_act, 1)
                        dve.tensor_scalar(lb[:, 2, :], lb[:, 1, :], -1.0, 1.0, ALU.mult, ALU.add).then_inc(lbs, 1)
                        dve.wait_ge(lbs, 2)
                        for h in range(HG):
                            dve.tensor_scalar(f[:, h, :], f[:, h, :], lb[:, 2, h:h + 1], lb[:, 1, h:h + 1], ALU.mult, ALU.add).then_inc(keys, 1)
                            dve.wait_ge(keys, 2 * h + 1)
                            dve.tensor_scalar(kd[:, h, :], f[:, h, :], -1.0, 1.0, ALU.mult, ALU.add).then_inc(keys, 1)
                        dve.wait_ge(reset_done, 2)
                        for h in range(HG):
                            b = h % 2
                            dve.wait_ge(logs, h + 1)
                            if h >= 2:
                                dve.wait_ge(k_state, h - 1)
                            dve.tensor_tensor_scan(cum[:, b, :], reset[:], f[:, h, :], 0.0, ALU.mult, ALU.add).then_inc(cums, 1)
                            dve.wait_ge(cums, h + 1)
                            by_chunk = cum[:, b, :].rearrange("p (c t) -> p c t", t=CHUNK)
                            dve.tensor_tensor(diff[:, b, :].rearrange("p (c t) -> p c t", t=CHUNK),
                                              by_chunk[:, :, CHUNK - 1:CHUNK].to_broadcast([P, NCH, CHUNK]), by_chunk, ALU.subtract).then_inc(diffs, 1)
                            dve.wait_ge(grow, h + 1)
                            dve.tensor_tensor(q[:, h, :], q[:, h, :], f[:, h, :], ALU.mult).then_inc(q_dec, 1)
                            dve.tensor_copy(last[:, h, :].unsqueeze(2), f[:, h, :].rearrange("p (c t) -> p c t", t=CHUNK)[:, :, CHUNK - 1:CHUNK]).then_inc(q_dec, 1)
                            dve.wait_ge(tail, h + 1)
                            dve.wait_ge(q_dec, 2 * h + 2)
                            dve.tensor_tensor(f[:, h, :], kd[:, h, :], diff[:, b, :], ALU.mult).then_inc(k_state, 1)
                            dve.wait_ge(k_state, h + 1)
                            dve.tensor_tensor(kd[:, h, :], kd[:, h, :], cum[:, b, :], ALU.mult).then_inc(k_dec, 1)

                if stop > 9.5:
                    hgrn_chunks(mix, v, q, kd, f, last)
                    hgrn_norm(mix, g, s2("hg_norm"))

        def hgrn_chunks(mix, v, q, kd, ks, last):
            with ExitStack() as ctx:
                kd_s = sb("kd_s", [P, HG, P], F32, ctx)
                ks_s = sb("ks_s", [P, HG, P], F32, ctx)
                v_s = sb("v_s", [P, HG * P], F32, ctx)
                ks_t = sb("ks_t", [P, HG, P], F32, ctx)
                sc_t = sb("sc_t", [P, HG, P], F32, ctx)
                state = sb("hc_state", [P, CPB, HG, P], F32, ctx)
                last_s = sb("last_s", [P, HG, CPB], F32, ctx)
                causal = sb("causal", [P, HG, P], U32, ctx)
                names = ("init", "staged", "scores", "turned", "masked", "copied", "update", "state", "inter", "out_copied")
                init, staged, scores, turned, masked, copied, update, state_done, inter, out_copied = [sem("hc_" + n) for n in names]
                n_stage = 4
                with nc.Block() as block:
                    @block.gpsimd
                    def _(pool):
                        pool.memset(state[:, 0, :, :], 0.0).then_inc(init, 1)
                        pool.memset(sc_t[:], 0.0).then_inc(init, 1)
                        for h in range(HG):
                            pool.tensor_copy(causal[:, h, :], cc("causal")).then_inc(init, 1)
                        with pool.Fori(0, TB) as t:
                            pool.wait_ge(scores, t)
                            pool.tensor_copy(kd_s[:], kd[:, :, bass.ds(t * P, P)]).then_inc(staged, 1)
                            pool.wait_ge(turned, t)
                            pool.tensor_copy(ks_s[:], ks[:, :, bass.ds(t * P, P)]).then_inc(staged, 1)
                            pool.wait_ge(inter, CPB * t)
                            pool.tensor_copy(v_s[:], v[:, bass.ds(t, 1), :].rearrange("p a n -> p (a n)")).then_inc(staged, 1)
                            pool.wait_ge(state_done, CPB * HG * t)
                            pool.tensor_copy(last_s[:], last[:, :, bass.ds(t * CPB, CPB)]).then_inc(staged, 1)

                    @block.tensor
                    def _(pe):
                        pe.wait_ge(init, 2 + HG)
                        with pe.Fori(0, TB) as t:
                            pe.wait_ge(staged, n_stage * t + 1)
                            pe.wait_ge(masked, t)
                            for h in range(HG):
                                mm = pe.matmul(psum[:, 0, h * P:(h + 1) * P], kd_s[:, h, :], q[:, h, bass.ds(t * P, P)], start=True, stop=True)
                            mm.then_inc(scores, 1)
                            pe.wait_ge(staged, n_stage * t + 2)
                            pe.wait_ge(copied, t)
                            for h in range(HG):
                                mm = pe.transpose(psum[:, 1, h * P:(h + 1) * P], ks_s[:, h, :], ident)
                            mm.then_inc(turned, 1)
                            pe.wait_ge(staged, n_stage * t + 3)
                            pe.wait_ge(copied, t + 1)
                            pe.wait_ge(state_done, CPB * HG * t)
                            for c in range(CPB):
                                at = slice(c * CHUNK, (c + 1) * CHUNK)
                                for h in range(HG):
                                    mm = pe.matmul(psum[:, 2 + c, h * P:(h + 1) * P], ks_t[at, h, :], v_s[at, h * P:(h + 1) * P],
                                                   start=True, stop=True, tile_position=(c * CHUNK, 0))
                                mm.then_inc(update, 1)
                            pe.wait_ge(masked, t + 1)
                            pe.wait_ge(out_copied, t)
                            for h in range(HG):
                                pe.matmul(psum[:, 6, h * P:(h + 1) * P], v_s[:, h * P:(h + 1) * P], sc_t[:, h, :],
                                          start=h == 0, stop=False, skip_group_check=True)
                            for c in range(CPB):
                                if c:
                                    pe.wait_ge(state_done, CPB * HG * t + HG * c)
                                for h in range(HG):
                                    mm = pe.matmul(psum[:, 6, h * P + c * CHUNK:h * P + (c + 1) * CHUNK], state[:, c, h, :],
                                                   q[:, h, bass.ds(t * P + c * CHUNK, CHUNK)], start=False, stop=True, skip_group_check=True)
                                mm.then_inc(inter, 1)

                    @block.scalar
                    def _(act):
                        with act.Fori(0, TB) as t:
                            act.wait_ge(turned, t + 1)
                            act.wait_ge(update, CPB * t)
                            act.copy(ks_t[:], psum[:, 1, :].rearrange("p (h m) -> p h m", m=P)).then_inc(copied, 1)
                            act.wait_ge(inter, CPB * t + CPB)
                            act.copy(mix[:, 0:HG, bass.ds(t * P, P)], psum[:, 6, :].rearrange("p (h m) -> p h m", m=P)).then_inc(out_copied, 1)

                    @block.vector
                    def _(dve):
                        with dve.Fori(0, TB) as t:
                            used, scored = dve.snap(dve.to_reg(CPB * t)), dve.snap(dve.to_reg(t + 1))
                            dve.wait_ge(init, 2 + HG)
                            dve.wait_ge(inter, used)
                            dve.wait_ge(scores, scored)
                            dve.copy_predicated(sc_t[:].rearrange("p h m -> p (h m)"), causal[:].rearrange("p h m -> p (h m)"), psum[:, 0, :]).then_inc(masked, 1)
                            dve.wait_ge(staged, n_stage * t + 4)
                            for c in range(CPB):
                                dve.wait_ge(update, CPB * t + c + 1)
                                dve.wait_ge(state_done, CPB * HG * t + HG * c)
                                if c == CPB - 1:
                                    dve.wait_ge(inter, CPB * t + 1)
                                else:
                                    dve.wait_ge(inter, CPB * t)
                                for h in range(HG):
                                    dve.scalar_tensor_tensor(out=state[:, (c + 1) % CPB, h, :], in0=state[:, c, h, :],
                                                             scalar=last_s[:, h, c:c + 1], in1=psum[:, 2 + c, h * P:(h + 1) * P],
                                                             op0=ALU.mult, op1=ALU.add).then_inc(state_done, 1)

        def hgrn_norm(mix, g, norm_w):
            with ExitStack() as ctx:
                sq = sb("hn_sq", [P, 2, S], F32, ctx)
                root = sb("hn_root", [P, HG, TB], F32, ctx)
                rstd = sb("hn_rstd", [P, HG, TB], F32, ctx)
                diag = sb("hn_diag", [P, 2, TB, P], F32, ctx)
                names = ("sq", "summed", "root", "rstd", "diag", "spread", "scaled", "gated")
                sq_done, summed, rooted, inverted, diag_done, spread_done, scaled, gated = [sem("hn_" + n) for n in names]
                sums = psum[:, 0, 0:HG * TB].rearrange("p (h t) -> p h t", t=TB)
                with nc.Block() as block:
                    @block.scalar
                    def _(act):
                        for h in range(HG):
                            if h >= 2:
                                act.wait_ge(summed, h - 1)
                            act.activation(sq[:, h % 2, :], mix[:, h, :], ACT.Square).then_inc(sq_done, 1)
                        act.wait_ge(summed, HG)
                        act.activation(root[:], sums, ACT.Sqrt, bias=EPS, scale=1.0 / P).then_inc(rooted, 1)

                    @block.tensor
                    def _(pe):
                        for h in range(HG):
                            pe.wait_ge(sq_done, h + 1)
                            for t in range(TB):
                                mm = pe.matmul(sums[:, h, t:t + 1], sq[:, h % 2, t * P:(t + 1) * P], ones_col, start=True, stop=True)
                            mm.then_inc(summed, 1)
                        for h in range(HG):
                            if h >= 2:
                                pe.wait_ge(scaled, h - 1)
                            for t in range(TB):
                                pe.wait_ge(diag_done, h * TB + t + 1)
                                mm = pe.matmul(banks(2 + 2 * (h % 2))[:, t * P:(t + 1) * P], ones, diag[:, h % 2, t, :], start=True, stop=True)
                            mm.then_inc(spread_done, 1)

                    @block.vector
                    def _(dve):
                        dve.wait_ge(rooted, 1)
                        dve.reciprocal(rstd[:], root[:]).then_inc(inverted, 1)
                        dve.wait_ge(inverted, 1)

                        def diagonals(h):
                            if h >= 2:
                                dve.wait_ge(spread_done, h - 1)
                            for t in range(TB):
                                dve.tensor_scalar(diag[:, h % 2, t, :], ident, rstd[:, h, t:t + 1], None, ALU.mult).then_inc(diag_done, 1)

                        diagonals(0)
                        for h in range(HG):
                            if h + 1 < HG:
                                diagonals(h + 1)
                            dve.wait_ge(spread_done, h + 1)
                            dve.scalar_tensor_tensor(out=mix[:, h, :], in0=mix[:, h, :], scalar=norm_w, in1=banks(2 + 2 * (h % 2)),
                                                     op0=ALU.mult, op1=ALU.mult).then_inc(scaled, 1)
                            dve.wait_ge(scaled, h + 1)
                            dve.tensor_tensor(mix[:, h, :], mix[:, h, :], g[:, h, :], ALU.mult).then_inc(gated, 1)

        def feed_forward_up(hid, gain):
            with ExitStack() as ctx:
                hn = sb("hn", [P, DT, S], F32, ctx)
                sil = sb("ff_silu", [P, S], F32, ctx)
                t = norm_tensors("n4", ctx)
                w, loaded, done, read = linear_tensors("up", DT, ctx)
                scaled = sem("up_scaled")
                with nc.Block() as block:
                    @block.sync
                    def _(sp):
                        stream_tiles(sp, tile_of(A["w_gate_up"]), w, loaded, done, FFT, DT)

                    @block.tensor
                    def _(pe):
                        norm_pe(pe, t)
                        linear(pe, lambda k: hn[:, k, :], DT, w, loaded, done, read, FFT, scaled)

                    @block.scalar
                    def _(act):
                        norm_act(act, t, x)
                        with act.Fori(0, FFT) as i:
                            act.wait_ge(done[0], i + 1)
                            act.wait_ge(read[1], i)
                            act.activation(sil[:], banks(0), ACT.Silu).then_inc(read[0], 1)

                    @block.vector
                    def _(dve):
                        norm_dve(dve, t)
                        scale_rows(dve, hn, gain, scaled)
                        with dve.Fori(0, FFT) as i:
                            dve.wait_ge(done[1], i + 1)
                            dve.wait_ge(read[0], i + 1)
                            dve.tensor_tensor(hid[:, bass.ds(i, 1), :].rearrange("p a s -> p (a s)"), banks(4), sil[:],
                                              ALU.mult).then_inc(read[1], 1)

        def feed_forward_down(hid):
            with ExitStack() as ctx:
                w, loaded, done, read = linear_tensors("dn", FFT, ctx)
                with nc.Block() as block:
                    @block.sync
                    def _(sp):
                        stream_tiles(sp, tile_of(A["w_down_2"]), w, loaded, done, DT // 2, FFT)

                    @block.tensor
                    def _(pe):
                        linear(pe, lambda k: hid[:, k, :], FFT, w, loaded, done, read, DT // 2)

                    @block.vector
                    def _(dve):
                        add_to_x(dve, done, read, None)

        def final_norm(out, gain):
            with ExitStack() as ctx:
                res = sb("res", [P, DT, S], F32, ctx)
                t = norm_tensors("n5", ctx)
                scaled, stored = sem("fn_scaled"), sem("fn_stored")
                with nc.Block() as block:
                    @block.tensor
                    def _(pe):
                        norm_pe(pe, t)

                    @block.scalar
                    def _(act):
                        norm_act(act, t, x)

                    @block.vector
                    def _(dve):
                        norm_dve(dve, t)
                        scale_rows(dve, res, gain, scaled)

                    @block.sync
                    def _(sp):
                        for k in range(DT):
                            sp.wait_ge(scaled, k + 1)
                            sp.dma_start(out[k * P:(k + 1) * P, :], res[:, k, :]).then_inc(stored, 16)
                        sp.wait_ge(stored, 16 * DT)

        setup()
        if stop > 0:
            before = set(sem_names)
            sem_home[0] = first_only
            with nc.Fori(0, depth) as l:
                layer(l)
                with nc.Block() as block:
                    @block.gpsimd
                    def _(pool):
                        for name in sem_names:
                            if name in ("ex_gathered", "ex_scattered"):
                                pool.dma_reset(range(sem_names[name].num, sem_names[name].num + 1))
                            if name not in before:
                                pool.sem_clear(sem_names[name])
        first_only.close()
        sem_home[0] = top
        if stop > 6:
            second(A["out"])
    return sem_names


def host_arrays(inputs):
    f = {n: np.asarray(a) for n, a in inputs.items()}

    def cols(v, rows=P):
        v = np.asarray(v)
        return np.ascontiguousarray(v.reshape(-1, rows).T)

    def tiles(w):
        k, n = w.shape
        return np.ascontiguousarray(w.reshape(k // P, P, n // P, P).transpose(2, 1, 0, 3).reshape(n // P, P, k))

    o1, o2, o3 = Q_RANK, Q_RANK + KV_RANK, Q_RANK + KV_RANK + ROPE
    w_in, layer_cols, w_uq, w_uk, w_uv = [], [], [], [], []
    for l in range(DEPTH):
        w = f["w_in"][l]
        rope = w[:, o2:o3]
        val, gat = w[:, o3:o3 + CONV_CH], w[:, o3 + CONV_CH:]
        pairs = [p for j in range(CT) for p in (gat[:, j * P:(j + 1) * P], val[:, j * P:(j + 1) * P])]
        w_in.append(tiles(np.concatenate([w[:, :o2], rope, rope] + pairs, axis=1)))
        uq = f["w_uq"][l].reshape(Q_RANK, HEADS, QK)
        uq = np.concatenate([uq[:, :, :NOPE].reshape(Q_RANK, -1), uq[:, :, NOPE:].reshape(Q_RANK, -1)], axis=1)
        w_uq.append(tiles(uq).transpose(1, 0, 2).reshape(P, -1))
        ukv = f["w_ukv"][l].reshape(KV_RANK, HEADS, NOPE + VD)
        w_uk.append(ukv[:, :, :NOPE].reshape(KV_RANK, -1))
        w_uv.append(ukv[:, :, NOPE:].reshape(KV_RANK, -1))
        conv_w = np.zeros((TAPS_PAD, CONV_CH), f["conv_w"].dtype)
        conv_w[:TAPS] = f["conv_w"][l]
        qg, kg = f["q_head_g"][l], f["k_head_g"][l]
        layer_cols.append(np.concatenate([
            cols(f["norm1_g"][l]), cols(f["norm2_g"][l]), cols(f["q_latent_g"][l]), cols(f["kv_latent_g"][l]),
            cols(qg[:NOPE]), cols(np.concatenate([qg[NOPE:], qg[NOPE:]])),
            cols(kg[:NOPE]), cols(np.concatenate([kg[NOPE:], kg[NOPE:]])),
            conv_w.reshape(TAPS_PAD, CT, P).transpose(2, 1, 0).reshape(P, -1),
            cols(f["conv_b"][l]), cols(f["conv_norm_g"][l]), cols(f["conv_norm_b"][l])], axis=1))
    w2 = f["w_in_2"][0]
    hw = HG * P
    w2_tiled = np.concatenate([w2[:, :2 * hw], w2[:, 3 * hw:]], axis=1)
    gu = f["w_gate_up_2"][0]
    gu = np.stack([gu[:, :DFF].reshape(D, FFT, P), gu[:, DFF:].reshape(D, FFT, P)], axis=2).reshape(D, 2 * DFF)
    second_cols = np.concatenate([
        cols(f["mix_norm_w_2"][0]), cols(f["hg_lb_2"][0]), cols(f["hg_lb_2"][1]), cols(f["hg_norm_w_2"][0]),
        f["conv_w_2"][0].reshape(LTAPS, LT, P).transpose(2, 1, 0).reshape(P, -1), cols(f["conv_b_2"][0]),
        cols(f["lru_ba_2"][0]), cols(f["lru_bx_2"][0]), cols(f["lru_a_2"][0]), cols(f["ffn_norm_w_2"][0]),
        cols(f["final_norm_w_2"])], axis=1)

    consts = np.zeros((P, N_CONST), np.float32)
    n = np.arange(P)
    consts[:, CC["ident"][0]:CC["ident"][1]] = np.eye(P)
    consts[:, CC["ones"][0]:CC["ones"][1]] = 1
    m = n % ROPE
    for r in range(P):
        if m[r] < ROPE // 2:
            consts[r + ROPE // 2, CC["turn"][0] + r] = -1
        else:
            consts[r - ROPE // 2, CC["turn"][0] + r] = 1
    consts[:, CC["causal"][0]:CC["causal"][1]] = (n[:, None] // CHUNK == n[None, :] // CHUNK) & (n[:, None] <= n[None, :])
    consts[:, CC["half0"][0]] = n < ROPE
    consts[:, CC["half1"][0]] = n >= ROPE
    consts[:, CC["inv_freq"][0]] = (np.float32(1) / (10000.0 ** (np.arange(0, ROPE, 2) / ROPE)).astype(np.float32))[n % (ROPE // 2)]
    return {
        "x_t": np.ascontiguousarray(f["x"][0].T), "c_cols": cols(f["c"][0]), "consts": consts,
        "positions": np.ascontiguousarray(f["positions"]),
        "b_ada_cols": cols(f["b_ada"]),
        "w_ada": np.ascontiguousarray(f["w_ada"].reshape(DEPTH, D, N_MOD * D // HALF, HALF).transpose(0, 2, 1, 3).reshape(-1, D, HALF)),
        "layer_cols": np.ascontiguousarray(np.stack(layer_cols)),
        "w_in": np.concatenate(w_in), "w_uq": np.ascontiguousarray(np.stack(w_uq)), "w_uk": np.ascontiguousarray(np.stack(w_uk)),
        "w_uv": np.ascontiguousarray(np.stack(w_uv)),
        "w_out": np.concatenate([tiles(f["w_out"][l]) for l in range(DEPTH)]),
        "w_router": np.ascontiguousarray(f["w_router"]),
        "w_gate": f["w_gate"].reshape(-1, D, FF), "w_up": f["w_up"].reshape(-1, D, FF), "w_down": f["w_down"].reshape(-1, FF, D),
        "second_cols": np.ascontiguousarray(second_cols),
        "w_i_2": np.ascontiguousarray(w2[:, 2 * hw:3 * hw]), "w_in_2": tiles(w2_tiled),
        "lru_wa": np.ascontiguousarray(f["lru_wa_2"][0]), "lru_wx": np.ascontiguousarray(f["lru_wx_2"][0]),
        "w_out_2": tiles(f["w_out_2"][0]), "w_gate_up": tiles(gu), "w_down_2": tiles(f["w_down_2"][0]),
    }


def kernel(**inputs):
    import concourse.bacc as bacc
    from concourse.bass_utils import run_bass_kernel_spmd

    nc = bacc.Bacc("TRN2", target_bir_lowering=False, num_devices=1)
    arrays = host_arrays(inputs)
    aps = {n: nc.dram_tensor(n + "_dram", a.shape, mybir.dt.from_np(a.dtype), kind="ExternalInput").ap() for n, a in arrays.items()}
    aps["out"] = nc.dram_tensor("out_t", (D, S), F32, kind="ExternalOutput").ap()
    build(nc, aps)
    r = run_bass_kernel_spmd(nc, [{n + "_dram": a for n, a in arrays.items()}], core_ids=[0])
    return np.ascontiguousarray(r.results[0]["out_t"].T).reshape(1, S, D)
```

```python
from contextlib import ExitStack, contextmanager

import numpy as np
import concourse.bass as bass
from concourse import mybir

F32 = mybir.dt.float32
F32R = mybir.dt.float32r
I32 = mybir.dt.int32
U32 = mybir.dt.uint32
ALU = mybir.AluOpType
ACT = mybir.ActivationFunctionType
AX = mybir.AxisListType

P = 128
S = 1024
D = 1024
DT = D // P
TB = S // P
HALF = 512
EPS = 1e-6
DEPTH = 2

HEADS = 4
NOPE = 128
ROPE = 64
QK = NOPE + ROPE
VD = 128
Q_RANK = 256
KV_RANK = 128
CONV_CH = 512
CT = CONV_CH // P
TAPS = 31
TAPS_PAD = 32
PAD = TAPS // 2
PROJECT_TAPS = 16
HEADS_TAPS = 16
ATTEND_TAPS = TAPS_PAD + TB
YW = S + TAPS_PAD
IN_TILES = 12
SCALE = 1.0 / float(np.sqrt(QK))
EXPERTS = 16
CAP = 2 * S // EXPERTS
FF = 1024
FT = FF // P
PIECES = 12
RAW = 6
PARTS = 4
SPLIT_EARLY = 3
N_MOD = 6
ADA_BUFS = 4
ADA_GROUPS = DEPTH * N_MOD * D // (HALF * ADA_BUFS)

CHUNK = 32
NCH = S // CHUNK
CPB = P // CHUNK
HG = 4
LT = 4
LTAPS = 4
LRU_C = 8.0
DFF = 2816
FFT = DFF // P
TWO_PI = 2.0 * float(np.pi)

LC = {}
_at = 0
for _name, _n in (("norm1", DT), ("norm2", DT), ("qlat", 2), ("kvlat", 1), ("qg_nope", 1), ("qg_rope", 1),
                  ("kg_nope", 1), ("kg_rope", 1), ("conv_w", CT * TAPS_PAD), ("conv_b", CT),
                  ("conv_g", CT), ("conv_nb", CT)):
    LC[_name] = (_at, _at + _n)
    _at += _n
N_LC = _at
SC = {}
_at = 0
for _name, _n in (("mix_norm", DT), ("lb0", HG), ("lb1", HG), ("hg_norm", 1), ("conv_w", LT * LTAPS),
                  ("conv_b", LT), ("ba", LT), ("bx", LT), ("lru_a", LT), ("ffn_norm", DT), ("final", DT)):
    SC[_name] = (_at, _at + _n)
    _at += _n
N_SC = _at
CC = {}
_at = 0
for _name, _n in (("ident", P), ("ones", P), ("turn", P), ("causal", P),
                  ("inv_freq", 1), ("sel", 11 * 2 * HEADS), ("fold", ADA_BUFS), ("flip", P)):
    CC[_name] = (_at, _at + _n)
    _at += _n
N_CONST = _at


class Chain:

    def __init__(self, eng, sem, base=0):
        self.eng, self.sem, self.base, self.n = eng, sem, base, 0

    def inc(self, ins):
        ins.then_inc(self.sem, 1)
        self.n += 1
        return self.n

    def wait(self, n=None):
        self.eng.wait_ge(self.sem, self.base + (self.n if n is None else n))

    def step(self, ins):
        self.inc(ins)
        self.wait()


def build(nc, A):
    sem_names = {}

    with ExitStack() as top:
        def sb(name, shape, dt=F32, ctx=top):
            return ctx.enter_context(nc.sbuf_tensor(name, shape, dt))

        sem_home = [top]

        def sem(name):
            assert name not in sem_names
            sem_names[name] = sem_home[0].enter_context(nc.semaphore(name))
            return sem_names[name]

        @contextmanager
        def own_semaphores():
            before, home = set(sem_names), sem_home[0]
            with ExitStack() as mine:
                sem_home[0] = mine
                yield
                with nc.Block() as block:
                    @block.gpsimd
                    def _(pool):
                        for name in sem_names:
                            if name in ("ex_gathered", "ex_scattered") and name not in before:
                                pool.dma_reset(range(sem_names[name].num, sem_names[name].num + 1))
                            if name not in before:
                                pool.sem_clear(sem_names[name])
            sem_home[0] = home

        psum = top.enter_context(nc.psum_tensor("psum", [P, 8, HALF], F32))

        def bank(i):
            return psum[:, i, :]

        def banks(i):
            return psum[:, i:i + 2, :].rearrange("p a b -> p (a b)")

        h2_rows = nc.dram_tensor("h2_rows", [S, D], F32, kind="Internal").ap()
        x_rows = nc.dram_tensor("x_rows", [D, S], F32, kind="Internal").ap()
        moe_rows = nc.dram_tensor("moe_rows", [S, D], F32, kind="Internal").ap()

        const = sb("const", [P, CC["flip"][0]])
        x = sb("x", [P, DT, S])
        mod = sb("mod", [P, DEPTH, N_MOD * DT])
        scols = sb("scols", [P, N_SC])
        sq_sum = sb("sq_sum", [P, S])
        first_only = top.enter_context(ExitStack())
        cos = sb("cos", [P, S], F32, first_only)
        sin = sb("sin", [P, S], F32, first_only)
        zero_row = sb("zero_row", [P, D], F32, first_only)
        flip = sb("flip", [P, P], F32, first_only)

        def cc(name):
            return const[:, CC[name][0]:CC[name][1]]

        ident, ones, turn = cc("ident"), cc("ones"), cc("turn")
        ones_col = const[:, CC["ones"][0]:CC["ones"][0] + 1]

        def block_of(t):
            return slice(t * P, (t + 1) * P) if isinstance(t, int) else bass.ds(t * P, P)

        def setup():
            with ExitStack() as ctx:
                pos_i = sb("pos_i", [P, S], I32, ctx)
                table = sb("table", [P, 4, S], F32, ctx)
                ang, turns, red = table[:, 0, :], table[:, 1, :], table[:, 2:4, :]
                mod_rows = sb("mod_rows", [2 * ADA_BUFS, HALF], F32, ctx)
                c_col = sb("c_col", [P, DT], F32, ctx)
                c_act = sb("c_act", [P, DT], F32, ctx)
                c_rows = sb("c_rows", [P, ADA_BUFS, DT, 2 * ADA_BUFS], F32R, ctx)
                b_ada = sb("b_ada", [P, DEPTH * N_MOD * DT], F32, ctx)
                ada_w = [sb(f"ada_w{i}", [P, DT, HALF], F32, ctx) for i in range(ADA_BUFS)]
                ada_hi, ada_lo = ([sb(f"ada_{n}{i}", [P, DT // 2, HALF], F32R, ctx) for i in range(4)] for n in ("hi", "lo"))

                def half(j):
                    return slice(j * DT // 2, (j + 1) * DT // 2)

                small_in, x_in = sem("su_small_in"), sem("su_x_in")
                ada_in = [sem(f"su_ada_in{i}") for i in range(ADA_BUFS)]
                c_ready = sem("su_c_ready")
                w_hi, w_lo, w_used = sem("su_w_hi"), sem("su_w_lo"), sem("su_w_used")
                rows_copied, rows_turned, added = sem("su_rows_copied"), sem("su_rows_turned"), sem("su_added")
                dve_step, tables_red, tables = sem("su_dve_step"), sem("su_tables_red"), sem("su_tables")
                zeroed, sq_done, sq_added = sem("su_zeroed"), sem("su_sq_done"), sem("su_sq_added")
                mod_cols = psum[:, 7, 0:DEPTH * N_MOD * DT].rearrange("p (i b j) -> p i b j", b=ADA_BUFS, j=HALF // P)
                with nc.Block() as block:
                    @block.sync
                    def _(sp):
                        sp.dma_start(c_col[:], A["c_cols"]).then_inc(small_in, 16)
                        sp.dma_start(const[:], A["consts"][:, 0:CC["flip"][0]]).then_inc(small_in, 16)
                        sp.dma_start(flip[:], A["consts"][:, CC["flip"][0]:N_CONST]).then_inc(small_in, 16)
                        sp.dma_start(b_ada[:], A["b_ada_cols"]).then_inc(small_in, 16)
                        sp.dma_start(pos_i[:], A["positions"].to_broadcast((P, S))).then_inc(small_in, 16)
                        sp.dma_start(scols[:], A["second_cols"]).then_inc(small_in, 16)
                        sp.dma_start(x[:], A["x_t"].rearrange("(k p) s -> p k s", p=P)).then_inc(x_in, 16)
                        with sp.Fori(0, ADA_GROUPS) as i:
                            for b in range(ADA_BUFS):
                                sp.wait_ge(w_lo, 2 * (ADA_BUFS * i + b) + 2)
                                sp.dma_start(ada_w[b][:], A["w_ada"][bass.ds(ADA_BUFS * i + b, 1)].rearrange(
                                    "c (k p) n -> p (c k) n", p=P)).then_inc(ada_in[b], 16)

                    @block.gpsimd
                    def _(pool):
                        pool.memset(zero_row[:], 0.0).then_inc(zeroed, 1)
                        pool.wait_ge(zeroed, 1)
                        flat = c_rows[:].rearrange("p b k r -> p (b k r)")
                        pool.tensor_scalar(flat, zero_row[:, 0:flat.shape[1]], 1.0, None, ALU.mult).then_inc(zeroed, 1)

                    @block.tensor
                    def _(pe):
                        pe.sem_inc(rows_turned, 1)
                        pe.sem_inc(w_used, 4)
                        pe.wait_ge(c_ready, 1 + 2 * ADA_BUFS)
                        with pe.Fori(0, ADA_GROUPS) as i:
                            for b in range(ADA_BUFS):
                                for k in range(DT):
                                    j, at = divmod(k, DT // 2)
                                    if at == 0:
                                        split = pe.snap(pe.to_reg(2 * (ADA_BUFS * (i + 1) + b) + j + 1))
                                        pe.wait_ge(w_lo, 2 * ADA_BUFS + 1)
                                        pe.wait_ge(w_lo, split)
                                    for n, part in enumerate((ada_hi, ada_lo)):
                                        mm = pe.matmul(psum[0:2 * ADA_BUFS, bass.ds(i, 1), :].rearrange("p a n -> p (a n)"),
                                                       c_rows[:, b, k, :], part[(2 * b + j) % 4][:, at, :],
                                                       start=b == 0 and k == 0 and n == 0,
                                                       stop=b == ADA_BUFS - 1 and k == DT - 1 and n == 1)
                                    if at == DT // 2 - 1:
                                        mm.then_inc(w_used, 1)
                            pe.wait_ge(rows_copied, 1)
                            pe.wait_ge(rows_copied, i + 1)
                            for j in range(HALF // P):
                                mm = pe.matmul(mod_cols[:, bass.ds(i, 1), :, j].rearrange("p a b -> p (a b)"), mod_rows[:, j * P:(j + 1) * P],
                                               cc("fold")[0:2 * ADA_BUFS, :], start=True, stop=True)
                            mm.then_inc(rows_turned, 1)

                    @block.scalar
                    def _(act):
                        act.wait_ge(small_in, 96)
                        act.activation(c_act[:], c_col[:], ACT.Silu).then_inc(c_ready, 1)
                        act.wait_ge(c_ready, 1)
                        act.wait_ge(zeroed, 2)
                        for b in range(ADA_BUFS):
                            act.copy(c_rows[:, b, :, b], c_act[:]).then_inc(c_ready, 1)
                        act.wait_ge(tables_red, 2)
                        act.activation(sin[:], red[:, 0, :], ACT.Sin).then_inc(tables, 1)
                        act.activation(cos[:], red[:, 1, :], ACT.Sin).then_inc(tables, 1)
                        act.wait_ge(x_in, 16)
                        act.wait_ge(tables, 2)
                        for k in range(DT):
                            if k >= 2:
                                act.wait_ge(sq_added, max(1, k - 2))
                            act.activation(red[:, k % 2, :], x[:, k, :], ACT.Square).then_inc(sq_done, 1)
                        with act.Fori(0, ADA_GROUPS) as i:
                            for b in range(ADA_BUFS):
                                act.wait_ge(ada_in[b], 16 * i + 16)
                                for j in range(2):
                                    act.wait_ge(w_used, 2 * (ADA_BUFS * i + b) + j + 1)
                                    act.copy(ada_hi[(2 * b + j) % 4][:], ada_w[b][:, half(j), :]).then_inc(w_hi, 1)
                            act.wait_ge(w_used, 2 * ADA_BUFS * (i + 1) + 4)
                            act.wait_ge(rows_turned, i + 1)
                            act.copy(mod_rows[:], psum[0:2 * ADA_BUFS, bass.ds(i, 1), :].rearrange("p a n -> p (a n)")).then_inc(rows_copied, 1)

                    @block.vector
                    def _(dve):
                        ch = Chain(dve, dve_step)
                        dve.sem_inc(w_lo, 2 * ADA_BUFS)
                        dve.wait_ge(small_in, 96)
                        ch.step(dve.tensor_copy(turns, pos_i[:]))
                        ch.step(dve.tensor_scalar(ang, turns, cc("inv_freq"), None, ALU.mult))
                        c1 = float(np.float32(6.28125))
                        c2 = float(np.float32(np.floor((TWO_PI - c1) * 2 ** 20) / 2 ** 20))
                        c3 = float(np.float32(TWO_PI - c1 - c2))
                        magic = 12582912.0
                        for f, shift in ((0, 0.0), (1, 0.25)):
                            ch.step(dve.tensor_scalar(turns, ang, 1.0 / TWO_PI, shift, ALU.mult, ALU.add))
                            ch.step(dve.tensor_scalar(turns, turns, magic, magic, ALU.add, ALU.subtract))
                            ch.step(dve.scalar_tensor_tensor(out=red[:, f, :], in0=turns, scalar=-c1, in1=ang,
                                                             op0=ALU.mult, op1=ALU.add))
                            for part in (c2, c3):
                                ch.step(dve.scalar_tensor_tensor(out=red[:, f, :], in0=turns, scalar=-part,
                                                                 in1=red[:, f, :], op0=ALU.mult, op1=ALU.add))
                            if f:
                                ch.step(dve.tensor_scalar(red[:, f, :], red[:, f, :], float(np.pi / 2), None, ALU.add))
                            dve.tensor_scalar(red[:, f, :], red[:, f, :], 3.1415925, -3.1415925, ALU.min,
                                              ALU.max).then_inc(tables_red, 1)
                        dve.wait_ge(c_ready, 1 + ADA_BUFS)
                        for b in range(ADA_BUFS):
                            dve.tensor_tensor(c_rows[:, b, :, ADA_BUFS + b], c_act[:], c_rows[:, b, :, b].bitcast(F32),
                                              ALU.subtract).then_inc(c_ready, 1)
                        for k in range(1, DT):
                            dve.wait_ge(sq_done, k + 1)
                            if k > 1:
                                dve.wait_ge(sq_added, k - 1)
                            dve.tensor_tensor(sq_sum[:], red[:, 0, :] if k == 1 else sq_sum[:], red[:, k % 2, :],
                                              ALU.add).then_inc(sq_added, 1)
                        with dve.Fori(0, ADA_GROUPS) as i:
                            for b in range(ADA_BUFS):
                                for j in range(2):
                                    dve.wait_ge(w_hi, 2 * (ADA_BUFS * i + b) + j + 1)
                                    dve.tensor_tensor(ada_lo[(2 * b + j) % 4][:], ada_w[b][:, half(j), :],
                                                      ada_hi[(2 * b + j) % 4][:].bitcast(F32), ALU.subtract).then_inc(w_lo, 1)
                        dve.wait_ge(rows_turned, 1 + ADA_GROUPS)
                        dve.tensor_tensor(mod[:].rearrange("p l n -> p (l n)"), psum[:, 7, 0:DEPTH * N_MOD * DT], b_ada[:],
                                          ALU.add).then_inc(added, 1)

        def spread(pe, out, diag, ready):
            for t in range(TB):
                pe.wait_ge(ready, t + 1)
                mm = pe.matmul(out[:, t * P:(t + 1) * P], ones, diag[:, t, :], start=True, stop=True)
            return mm


        def norm_tensors(tag, ctx, room=None):
            t = {n: sb(f"{tag}_{n}", [P, TB], F32, ctx) for n in ("root", "rstd")}
            room = sb(f"{tag}_diag", [P, S], F32, ctx)[:] if room is None else room
            t["diag"] = room.rearrange("p (t m) -> p t m", m=P)
            t.update({n: sem(f"{tag}_{n}") for n in ("summed", "root_done", "rstd_done", "diag_done", "spread_done")})
            return t

        def token_sums(pe, col, row):
            for b in range(TB):
                mm = pe.matmul(col[:, b:b + 1], row[:, b * P:(b + 1) * P], ones_col, start=b == 0, stop=True,
                               skip_group_check=True)
            return mm

        def norm_act(act, t):
            act.wait_ge(t["summed"], 1)
            act.activation(t["root"][:], psum[:, 0, 0:TB], ACT.Sqrt, bias=EPS, scale=1.0 / D).then_inc(t["root_done"], 1)

        def norm_pe(pe, t):
            token_sums(pe, psum[:, 0, 0:TB], sq_sum).then_inc(t["summed"], 1)
            spread(pe, banks(2), t["diag"], t["diag_done"]).then_inc(t["spread_done"], 1)

        def norm_dve(dve, t):
            dve.wait_ge(t["root_done"], 1)
            dve.reciprocal(t["rstd"][:], t["root"][:]).then_inc(t["rstd_done"], 1)
            dve.wait_ge(t["rstd_done"], 1)
            for b in range(TB):
                dve.tensor_scalar(t["diag"][:, b, :], ident, t["rstd"][:, b:b + 1], None,
                                  ALU.mult).then_inc(t["diag_done"], 1)
            dve.wait_ge(t["spread_done"], 1)


        def split_tensors(tag, K, ctx):
            w = {"raw": [sb(f"{tag}_raw{b}", [P, K, P], F32, ctx) for b in range(2)]}
            for part in ("hi", "lo"):
                w[part] = [sb(f"{tag}_{part}{b}", [P, K, P], F32R, ctx) for b in range(2)]
            for n in ("loaded", "split", "done", "read"):
                w[n] = [sem(f"{tag}_{n}{b}") for b in range(2)]
            return w

        def stream_tiles(sp, tiles, w, pairs, between=None):
            for b in range(2):
                sp.dma_start(w["raw"][b][:], tiles(b)).then_inc(w["loaded"][b], 16)
            if between is not None:
                between()
            with sp.Fori(1, pairs) as i:
                for b in range(2):
                    sp.wait_ge(w["split"][b], 2 * i + 1)
                    sp.dma_start(w["raw"][b][:], tiles(2 * i + b)).then_inc(w["loaded"][b], 16)

        def split_tile(eng, w, b, n):
            loaded, used = eng.snap(eng.to_reg(16 * n + 16)), eng.snap(eng.to_reg(n + 1))
            eng.wait_ge(w["loaded"][b], 16)
            eng.wait_ge(w["loaded"][b], loaded)
            eng.wait_ge(w["done"][b], used)
            eng.tensor_scalar(w["hi"][b][:], w["raw"][b][:], 1.0, None, ALU.mult).then_inc(w["split"][b], 1)
            eng.wait_ge(w["split"][b], 2 * n + 2)
            eng.tensor_tensor(w["lo"][b][:], w["raw"][b][:], w["hi"][b][:].bitcast(F32), ALU.subtract).then_inc(w["split"][b], 1)

        def split_tiles(pool, w, pairs):
            for b in range(2):
                pool.sem_inc(w["split"][b], 1)
            with pool.Fori(0, pairs) as i:
                for b in range(2):
                    split_tile(pool, w, b, i)

        def products(pe, out, w_hi, w_lo, x_hi, x_lo, first, last):
            for n, (wt, xt) in enumerate(((w_hi, x_hi), (w_hi, x_lo), (w_lo, x_hi))):
                for half in range(2):
                    mm = pe.matmul(bank(out + half), wt, xt[:, half * HALF:(half + 1) * HALF],
                                   start=first and n == 0, stop=last and n == 2)
            return mm

        def linear(pe, x_hi, x_lo, K, w, pairs, inputs, between=None):
            for b in range(2):
                pe.sem_inc(w["done"][b], 1)
            for part in range(2):
                if part and between is not None:
                    between()
                for b in range(2):
                    if part == 0:
                        pe.wait_ge(w["split"][b], 3)
                        pe.wait_ge(w["read"][b], 1)
                    for k in range(part * K // 2, (part + 1) * K // 2):
                        pe.wait_ge(inputs, k + 1)
                        mm = products(pe, 4 * b, w["hi"][b][:, k, :], w["lo"][b][:, k, :], x_hi[:, k, :], x_lo[:, k, :],
                                      k == 0, k == K - 1)
                    if part:
                        mm.then_inc(w["done"][b], 1)
            with pe.Fori(1, pairs) as i:
                for b in range(2):
                    pe.wait_ge(w["split"][b], 2 * i + 3)
                    pe.wait_ge(w["read"][b], i + 1)
                    for k in range(K):
                        mm = products(pe, 4 * b, w["hi"][b][:, k, :], w["lo"][b][:, k, :], x_hi[:, k, :], x_lo[:, k, :],
                                      k == 0, k == K - 1)
                    mm.then_inc(w["done"][b], 1)

        def tile_of(t):
            return lambda n: t[bass.ds(n, 1)].rearrange("a p (k m) -> p (a k) m", m=P)

        def layer(l):
            with ExitStack() as ctx:
                lcols = sb("lcols", [P, N_LC], F32, ctx)
                modl = sb("modl", [P, N_MOD, DT], F32, ctx)
                gain = sb("gain", [P, 2, DT], F32, ctx)

                def lc(name):
                    return lcols[:, LC[name][0]:LC[name][1]]

                shift = (modl[:, 0, :], modl[:, 3, :])
                gate = (modl[:, 2, :], modl[:, 5, :])
                with ExitStack() as mixing:
                    mixing.enter_context(own_semaphores())
                    mix = sb("mix", [P, DT, S], F32, mixing)
                    with ExitStack() as before:
                        y = sb("y", [P, CT, YW], F32, before)
                        latents = before.enter_context(ExitStack())
                        lat = sb("lat", [P, 4, S], F32, latents)
                        project(l, lcols, modl, gain, lc, shift, lat, y, mix)
                        latents.close()
                        q = {"k_hi": sb("k_hi", [P, HEADS, S], F32R, before)}
                        q.update({n: sb(n, s, F32, before) for n, s in (
                            ("q_nope", [P, HEADS, S]), ("q_rope", [P, HEADS // 2, S]), ("v", [P, TB, HEADS * VD]),
                            ("q_scale", [P, HEADS, TB]), ("q_neg", [P, HEADS, TB]))})
                        with ExitStack() as whole:
                            q.update({n: sb(n, [P, HEADS, S], F32, whole) for n in ("k_nope", "k_rope")})
                        q.update({n: sb(n, [P, HEADS, S], F32R, before) for n in ("k_lo", "k_parts")})
                        heads(l, lc, lat, q, y, mix)
                        attend(lc, y, mix, q)
                    conv_norm_and_mix(l, lc, mix, gate[0])
                with own_semaphores():
                    experts_part(l, gain, shift[1], gate[1])

        def conv_taps(dve, lc, y, mix, step, done):
            at = [done]

            def more(n):
                for _ in range(n):
                    j, t = divmod(at[0], TAPS_PAD)
                    if t and at[0] > done:
                        dve.wait_ge(step, at[0] - done)
                    acc = mix[:, HEADS + j, :]
                    dve.scalar_tensor_tensor(out=acc, in0=y[:, j, t:t + S], scalar=lc("conv_w")[:, at[0]:at[0] + 1], in1=acc,
                                             op0=ALU.mult, op1=ALU.add).then_inc(step, 1)
                    at[0] += 1

            return more

        def project(l, lcols, modl, gain, lc, shift, lat, y, mix):
            with ExitStack() as ctx:
                h_hi, h_lo = (sb("h_" + n, [P, DT, S], F32R, ctx) for n in ("hi", "lo"))
                t = norm_tensors("n1", ctx, mix[:, 2, :])
                sig = mix[:, 3, :]
                h = mix[:, 0:2, :]
                w = split_tensors("in", DT, ctx)
                done, read = w["done"], w["read"]
                cols_in, gains, scaled, hi_done, full_done, h_ready, padded = [sem("pr_" + n) for n in (
                    "cols_in", "gains", "scaled", "hi_done", "full_done", "h_ready", "padded")]
                conv_step = sem("pr_conv_step")
                with nc.Block() as block:
                    @block.sync
                    def _(sp):
                        sp.dma_start(lcols[:], A["layer_cols"][bass.ds(l, 1)].rearrange("a p n -> p (a n)")).then_inc(cols_in, 16)
                        tiles = tile_of(A["w_in"])
                        stream_tiles(sp, lambda n: tiles(n + l * IN_TILES), w, IN_TILES // 2)

                    @block.gpsimd
                    def _(pool):
                        pool.memset(y[:, :, 0:PAD], 0.0).then_inc(padded, 1)
                        pool.memset(y[:, :, PAD + S:YW], 0.0).then_inc(padded, 1)
                        split_tiles(pool, w, IN_TILES // 2)

                    @block.scalar
                    def _(act):
                        act.sem_inc(read[0], 1)
                        norm_act(act, t)
                        act.wait_ge(gains, 5)
                        for k in range(DT):
                            act.wait_ge(scaled, k + 1)
                            act.activation(h_hi[:, k, :], h[:, k % 2, :], ACT.Identity, scale=gain[:, 0, k:k + 1],
                                           bias=shift[0][:, k:k + 1]).then_inc(hi_done, 1)
                            act.wait_ge(hi_done, k + 1)
                            act.activation(h[:, k % 2, :], h[:, k % 2, :], ACT.Identity, scale=gain[:, 0, k:k + 1],
                                           bias=shift[0][:, k:k + 1]).then_inc(full_done, 1)
                        act.wait_ge(cols_in, 16)
                        for j in range(CT):
                            act.activation(mix[:, HEADS + j, :], zero_row[:], ACT.Identity, scale=1.0,
                                           bias=lc("conv_b")[:, j:j + 1]).then_inc(padded, 1)
                        with act.Fori(0, CT) as j:
                            act.wait_ge(done[0], j + 2)
                            act.wait_ge(read[1], j + 1)
                            act.activation(sig, banks(0), ACT.Sigmoid).then_inc(read[0], 1)
                        with act.Fori(0, 2) as i:
                            for b in range(2):
                                act.wait_ge(done[b], i + CT + 2)
                                act.copy(lat[:, bass.ds(2 * i + b, 1), :].rearrange("p a s -> p (a s)"),
                                         banks(4 * b)).then_inc(read[b], 1)

                    @block.vector
                    def _(dve):
                        dve.sem_inc(read[1], 1)
                        dve.wait_ge(cols_in, 16)
                        dve.tensor_copy(modl[:].rearrange("p a b -> p (a b)"), mod[:, bass.ds(l, 1), :].rearrange(
                            "p l n -> p (l n)")).then_inc(gains, 1)
                        dve.wait_ge(gains, 1)
                        for n, g in ((0, "norm1"), (1, "norm2")):
                            dve.tensor_scalar(gain[:, n, :], modl[:, 3 * n + 1, :], 1.0, None, ALU.add).then_inc(gains, 1)
                            dve.wait_ge(gains, 2 + 2 * n)
                            dve.tensor_tensor(gain[:, n, :], gain[:, n, :], lc(g), ALU.mult).then_inc(gains, 1)
                        norm_dve(dve, t)

                        def low_part(k):
                            dve.wait_ge(full_done, k + 1)
                            dve.tensor_tensor(h_lo[:, k, :], h[:, k % 2, :], h_hi[:, k, :].bitcast(F32), ALU.subtract).then_inc(h_ready, 1)

                        for k in range(DT):
                            if k >= 2:
                                low_part(k - 2)
                                dve.wait_ge(h_ready, k - 1)
                            dve.tensor_tensor(h[:, k % 2, :], x[:, k, :], banks(2), ALU.mult).then_inc(scaled, 1)
                        low_part(DT - 2)
                        low_part(DT - 1)
                        dve.wait_ge(padded, 2 + CT)
                        taps = conv_taps(dve, lc, y, mix, conv_step, 0)
                        for j in range(CT):
                            dve.wait_ge(done[1], j + 2)
                            dve.wait_ge(read[0], j + 2)
                            dve.tensor_tensor(y[:, j, PAD:PAD + S], banks(4), sig, ALU.mult).then_inc(read[1], 1)
                            dve.wait_ge(read[1], j + 2)
                            taps(PROJECT_TAPS)
                        taps(CT * TAPS_PAD - ATTEND_TAPS - HEADS_TAPS - CT * PROJECT_TAPS)

                    @block.tensor
                    def _(pe):
                        norm_pe(pe, t)
                        linear(pe, h_hi, h_lo, DT, w, IN_TILES // 2, h_ready)

        def heads(l, lc, lat, q, y, mix):
            q_nope, q_rope, k_nope, k_rope, v = q["q_nope"], q["q_rope"], q["k_nope"], q["k_rope"], q["v"]
            k_hi, k_lo, k_parts = q["k_hi"], q["k_lo"], q["k_parts"]
            with ExitStack() as ctx:
                w_uq = sb("w_uq", [P, 6, 2, P], F32, ctx)
                w_k = sb("w_k", [P, HEADS, P], F32, ctx)
                w_v = sb("w_v", [P, HEADS * VD], F32, ctx)
                lat_root = sb("hd_lat_root", [P, 2, TB], F32, ctx)
                lat_rstd = sb("hd_lat_rstd", [P, 2, TB], F32, ctx)
                row_root = sb("hd_row_root", [2 * HEADS, S], F32, ctx)
                rstd = sb("hd_rstd", [P, TB, 2 * HEADS], F32, ctx)
                sq, rot = mix[:, 0:2, :], mix[:, 2, :]
                rope_hi = mix[ROPE:P, 0:2, :].bitcast(F32R)
                rope_rows = [lat[:, 3, :], q_rope[:, 0, :], q_rope[:, 1, :]]
                cos_rows = [k_rope[:, 0, :], k_rope[:, 1, :], k_rope[:, 0, :]]
                diags = [mix[:, r, :].rearrange("p (t m) -> p t m", m=P) for r in (2, 3)]
                names = ("w_in", "sq_done", "q_added", "lat_summed", "lat_root", "lat_rstd", "diag_done", "spread_done", "lat_done",
                         "summed", "prod", "raw_done", "v_prod", "v_copied", "row_root", "root_turned", "rstd", "q_scaled",
                         "turned", "sin_part", "cos_part", "roped", "k_done", "k_rounded", "k_split", "rope_split", "conv_step")
                (w_in, sq_done, q_added, lat_summed, lat_rooted, lat_inverted, diag_done, spread_done, lat_done,
                 summed, prod, raw_done, v_prod, v_copied, row_rooted, root_turned, inverted, q_scaled,
                 turned, sin_part, cos_part, roped, k_done, k_rounded, k_split, rope_split, conv_step) = [sem("hd_" + n) for n in names]
                tiles = [("q", h) for h in range(HEADS)] + [("r", 0), ("r", 1)] + [("k", h) for h in range(HEADS)]
                dest = {"q": q_nope, "r": q_rope, "k": k_nope}
                gains = {"q": "qg_nope", "r": "qg_rope", "k": "kg_nope"}
                lat_sums = psum[:, 4, 0:2 * TB]
                turn_at = (2, 6, 8)
                taps_at = (3, 3, 3, 0, 2, 2, 2, 0, 1, 0)
                assert sum(taps_at) == HEADS_TAPS
                rotate_at = (3, 7, 9)
                head_sums = psum[0:2 * HEADS, 6:8, :].rearrange("p a b -> p (a b)")
                sel = cc("sel").rearrange("p (n h) -> p n h", h=2 * HEADS)

                with nc.Block() as block:
                    @block.sync
                    def _(sp):
                        sp.dma_start(w_uq[:].rearrange("p n k m -> p (n k m)"), A["w_uq"][bass.ds(l, 1)].rearrange(
                            "a p n -> p (a n)")).then_inc(w_in, 16)
                        sp.dma_start(w_k[:].rearrange("p n m -> p (n m)"), A["w_uk"][bass.ds(l, 1)].rearrange(
                            "a p n -> p (a n)")).then_inc(w_in, 16)
                        sp.dma_start(w_v[:], A["w_uv"][bass.ds(l, 1)].rearrange("a p n -> p (a n)")).then_inc(w_in, 16)

                    @block.scalar
                    def _(act):
                        for k in range(4):
                            if k == 2:
                                act.wait_ge(lat_summed, 1)
                            if k == 3:
                                act.wait_ge(q_added, 1)
                            act.activation(sq[:, k % 2, :], lat[:, k, :], ACT.Square).then_inc(sq_done, 1)
                        act.wait_ge(lat_summed, 2)
                        act.activation(lat_root[:, 0, :], lat_sums[:, 0:TB], ACT.Sqrt, bias=EPS, scale=1.0 / Q_RANK).then_inc(lat_rooted, 1)
                        act.activation(lat_root[:, 1, :], lat_sums[:, TB:2 * TB], ACT.Sqrt, bias=EPS, scale=1.0 / KV_RANK).then_inc(lat_rooted, 1)
                        for n in range(len(tiles)):
                            act.wait_ge(prod, n + 1)
                            if n:
                                act.wait_ge(summed, n)
                            act.activation(sq[:, n % 2, :], banks(2 * (n % 2)), ACT.Square).then_inc(sq_done, 1)
                        act.wait_ge(summed, 1 + len(tiles))
                        act.activation(row_root[:], head_sums, ACT.Sqrt, bias=EPS, scale=1.0 / QK).then_inc(row_rooted, 1)
                        for t in range(TB):
                            act.wait_ge(v_prod, t + 1)
                            act.copy(v[:, t, :], bank(4 + t % 2)).then_inc(v_copied, 1)
                        for h in range(HEADS):
                            act.wait_ge(k_done, 2 * h + 2)
                            if h >= 2:
                                act.wait_ge(rope_split, h - 1)
                            act.copy(k_hi[:, h, :], k_nope[:, h, :]).then_inc(k_rounded, 1)
                            act.copy(rope_hi[:, h % 2, :], k_rope[ROPE:P, h, :]).then_inc(k_rounded, 1)
                            act.copy(k_parts[0:ROPE, h, :], k_rope[0:ROPE, h, :]).then_inc(k_rounded, 1)

                    @block.gpsimd
                    def _(pool):
                        for n in range(3):
                            if n:
                                pool.wait_ge(raw_done, HEADS + n)
                            else:
                                pool.wait_ge(lat_done, 4)
                            if n == 2:
                                pool.wait_ge(roped, 1)
                            pool.tensor_tensor(cos_rows[n], rope_rows[n], cos[:], ALU.mult).then_inc(cos_part, 1)
                        for h in range(HEADS):
                            pool.wait_ge(k_rounded, 3 * h + 1)
                            pool.tensor_tensor(k_lo[:, h, :], k_nope[:, h, :], k_hi[:, h, :].bitcast(F32),
                                               ALU.subtract).then_inc(k_split, 1)

                    @block.vector
                    def _(dve):
                        def diagonals(n, col):
                            for t in range(TB):
                                dve.tensor_scalar(diags[n % 2][:, t, :], ident, col(t), None, ALU.mult).then_inc(diag_done, 1)

                        dve.wait_ge(sq_done, 2)
                        dve.tensor_tensor(sq[:, 0, :], sq[:, 0, :], sq[:, 1, :], ALU.add).then_inc(q_added, 1)
                        dve.wait_ge(lat_rooted, 2)
                        dve.reciprocal(lat_rstd[:], lat_root[:]).then_inc(lat_inverted, 1)
                        dve.wait_ge(lat_inverted, 1)
                        for g in range(2):
                            diagonals(g, lambda t: lat_rstd[:, g, t:t + 1])
                        for k, name in ((0, "qlat"), (1, "qlat"), (2, "kvlat")):
                            dve.wait_ge(spread_done, 1 + k // 2)
                            col = lc(name)[:, k % 2:k % 2 + 1]
                            dve.scalar_tensor_tensor(out=lat[:, k, :], in0=lat[:, k, :], scalar=col, in1=banks(2 * (k // 2)),
                                                     op0=ALU.mult, op1=ALU.mult).then_inc(lat_done, 1)
                        dve.wait_ge(sq_done, 4)
                        dve.tensor_scalar(lat[:, 3, :], lat[:, 3, :], lc("kg_rope"), None, ALU.mult).then_inc(lat_done, 1)

                        def rotate(n):
                            dve.wait_ge(turned, n + 1)
                            if n:
                                dve.wait_ge(roped, n)
                            dve.tensor_tensor(rot, banks(4), sin[:], ALU.mult).then_inc(sin_part, 1)
                            dve.wait_ge(sin_part, n + 1)
                            dve.wait_ge(cos_part, n + 1)
                            dve.tensor_tensor(rope_rows[n], cos_rows[n], rot, ALU.add).then_inc(roped, 1)

                        taps = conv_taps(dve, lc, y, mix, conv_step, CT * TAPS_PAD - ATTEND_TAPS - HEADS_TAPS)
                        for n, (kind, j) in enumerate(tiles):
                            dve.wait_ge(sq_done, 5 + n)
                            dve.tensor_scalar(dest[kind][:, j, :], banks(2 * (n % 2)), lc(gains[kind]), None,
                                              ALU.mult).then_inc(raw_done, 1)
                            if n in rotate_at:
                                rotate(rotate_at.index(n))
                            taps(taps_at[n])
                        dve.wait_ge(root_turned, 1)
                        dve.reciprocal(rstd[:].rearrange("p t h -> p (t h)"), psum[:, 6, 0:TB * 2 * HEADS]).then_inc(inverted, 1)
                        dve.wait_ge(inverted, 1)
                        q_rstd = rstd[:, :, 0:HEADS].rearrange("p t h -> p h t")
                        dve.tensor_scalar(q["q_scale"][:], q_rstd, SCALE, None, ALU.mult).then_inc(q_scaled, 1)
                        dve.tensor_scalar(q["q_neg"][:], q_rstd, -SCALE, None, ALU.mult).then_inc(q_scaled, 1)
                        diagonals(1, lambda t: rstd[:, t, HEADS:HEADS + 1])
                        dve.wait_ge(roped, 3)

                        def rope_low_part(h):
                            dve.wait_ge(k_rounded, 3 * h + 2)
                            dve.tensor_tensor(k_parts[ROPE:P, h, :], k_rope[ROPE:P, h, :], rope_hi[:, h % 2, :].bitcast(F32),
                                              ALU.subtract).then_inc(rope_split, 1)

                        for h in range(HEADS):
                            if h + 1 < HEADS:
                                if h:
                                    dve.wait_ge(spread_done, 2 + h)
                                diagonals(h, lambda t: rstd[:, t, HEADS + h + 1:HEADS + h + 2])
                            dve.wait_ge(spread_done, 3 + h)
                            over = banks(2 * (h % 2))
                            dve.tensor_tensor(k_nope[:, h, :], k_nope[:, h, :], over, ALU.mult).then_inc(k_done, 1)
                            dve.tensor_tensor(k_rope[:, h, :], lat[:, 3, :], over, ALU.mult).then_inc(k_done, 1)
                            if h:
                                rope_low_part(h - 1)
                        rope_low_part(HEADS - 1)

                    @block.tensor
                    def _(pe):
                        def head_squares(n, k, first, last):
                            for half in range(2):
                                mm = pe.matmul(psum[0:2 * HEADS, 6 + half, :], sel[:, n, :], sq[:, k, half * HALF:(half + 1) * HALF],
                                               start=first, stop=last)
                            mm.then_inc(summed, 1)

                        def turn_rows(n):
                            if n:
                                pe.wait_ge(raw_done, HEADS + n)
                                pe.wait_ge(sin_part, n)
                            else:
                                pe.wait_ge(lat_done, 4)
                            for half in range(2):
                                mm = pe.matmul(bank(4 + half), turn, rope_rows[n][:, half * HALF:(half + 1) * HALF], start=True, stop=True)
                            mm.then_inc(turned, 1)

                        pe.wait_ge(q_added, 1)
                        token_sums(pe, lat_sums[:, 0:TB], sq[:, 0, :]).then_inc(lat_summed, 1)
                        pe.wait_ge(sq_done, 3)
                        token_sums(pe, lat_sums[:, TB:2 * TB], sq[:, 0, :]).then_inc(lat_summed, 1)
                        pe.wait_ge(sq_done, 4)
                        head_squares(10, 1, True, False)
                        for g in range(2):
                            for t in range(TB):
                                pe.wait_ge(diag_done, g * TB + t + 1)
                                mm = pe.matmul(banks(2 * g)[:, t * P:(t + 1) * P], ones, diags[g][:, t, :], start=True, stop=True)
                            mm.then_inc(spread_done, 1)
                        pe.wait_ge(w_in, 48)
                        pe.wait_ge(lat_done, 3)
                        for n, (kind, j) in enumerate(tiles):
                            if n >= 2:
                                pe.wait_ge(sq_done, 3 + n)
                                pe.wait_ge(raw_done, n - 1)
                            for k in range(1 if kind == "k" else 2):
                                wt = w_k[:, j, :] if kind == "k" else w_uq[:, j + (HEADS if kind == "r" else 0), k, :]
                                src = lat[:, 2 if kind == "k" else k, :]
                                for half in range(2):
                                    mm = pe.matmul(bank(2 * (n % 2) + half), wt, src[:, half * HALF:(half + 1) * HALF],
                                                   start=k == 0, stop=kind == "k" or k == 1)
                            mm.then_inc(prod, 1)
                            if n in turn_at:
                                turn_rows(turn_at.index(n))
                            if n:
                                pe.wait_ge(sq_done, 4 + n)
                                head_squares(n - 1, (n - 1) % 2, False, False)
                        pe.wait_ge(sq_done, 4 + len(tiles))
                        head_squares(len(tiles) - 1, (len(tiles) - 1) % 2, False, True)
                        pe.wait_ge(sin_part, 3)
                        for t in range(TB):
                            if t == 3:
                                pe.wait_ge(row_rooted, 1)
                                for b in range(TB):
                                    mm = pe.transpose(psum[:, 6, b * 2 * HEADS:(b + 1) * 2 * HEADS], row_root[:, b * P:(b + 1) * P],
                                                      ident[0:2 * HEADS, 0:2 * HEADS])
                                mm.then_inc(root_turned, 1)
                            if t >= 2:
                                pe.wait_ge(v_copied, t - 1)
                            pe.matmul(bank(4 + t % 2), lat[:, 2, t * P:(t + 1) * P], w_v[:], start=True,
                                      stop=True).then_inc(v_prod, 1)
                        pe.wait_ge(raw_done, len(tiles))
                        for h in range(HEADS):
                            if h >= 2:
                                pe.wait_ge(k_done, 2 * (h - 1))
                            for t in range(TB):
                                pe.wait_ge(diag_done, (2 + h) * TB + t + 1)
                                mm = pe.matmul(banks(2 * (h % 2))[:, t * P:(t + 1) * P], ones, diags[(h + 1) % 2][:, t, :], start=True, stop=True)
                            mm.then_inc(spread_done, 1)

        def attend(lc, y, mix, q):
            q_nope, q_rope, v = q["q_nope"], q["q_rope"], q["v"]
            k_hi, k_lo, k_parts = q["k_hi"], q["k_lo"], q["k_parts"]
            with ExitStack() as ctx:
                qs_hi, qs_lo = (sb("qs_" + n, [P, HEADS, P], F32R, ctx) for n in ("hi", "lo"))
                rope_in = sb("qs_rope", [P, HEADS, P], F32, ctx)
                rope_hi = sb("qs_rope_hi", [P, HEADS, P], F32R, ctx)
                rope_lo = sb("qs_rope_lo", [ROPE, HEADS, P], F32R, ctx)
                probs = y[:, 0:2, 0:S]
                probs_t = sb("probs_t", [P, 2, TB, P], F32, ctx)
                neg_max = sb("neg_max", [P, 2], F32, ctx)
                row_max = sb("row_max", [P, 2], F32, ctx)
                row_sum = sb("row_sum", [P, 2], F32, ctx)
                inv_sum = sb("inv_sum", [P, 2], F32, ctx)
                taps = sb("taps", [P, HEADS + 1], F32, ctx)
                names = ("scores_done", "maxes", "neg_done", "exp_done", "inv_done", "probs_done", "conv_step", "taps_in")
                scores_done, maxes, neg_done, exp_done, inv_done, probs_done, conv_step, taps_in = [sem("at_" + n) for n in names]
                staged = [sem(f"at_staged{p}") for p in range(HEADS // 2)]
                rope_loaded = [sem(f"at_rope_loaded{p}") for p in range(HEADS // 2)]
                turned = [sem(f"at_turned{b}") for b in range(2)]
                copied = [sem(f"at_copied{b}") for b in range(2)]
                pv_done = [sem(f"at_pv_done{b}") for b in range(2)]
                out_copied = [sem(f"at_out_copied{b}") for b in range(2)]
                n_conv = HEADS + 1
                assert HEADS * TB == TAPS_PAD and n_conv * TB == ATTEND_TAPS
                first_taps = ((CT - 1) * TAPS_PAD, (CT - 1) * TAPS_PAD - TB)

                def score_slot(s):
                    return banks(2 * s)

                with nc.Block() as block:
                    @block.sync
                    def _(sp):
                        def load_rope(pair, at):
                            for j in range(2):
                                for copy in range(2):
                                    sp.dma_start(rope_in[copy * ROPE:(copy + 1) * ROPE, 2 * pair + j, :],
                                                 q_rope[j * ROPE:(j + 1) * ROPE, pair, at]).then_inc(rope_loaded[pair], 16)

                        for pair in range(HEADS // 2):
                            load_rope(pair, slice(0, P))
                        with sp.Fori(0, TB) as blk:
                            nxt = (blk + 1) % TB
                            for pair in range(HEADS // 2):
                                sp.wait_ge(staged[pair], 4 * blk + 4)
                                load_rope(pair, bass.ds(nxt * P, P))
                        for pair in range(HEADS // 2):
                            sp.wait_ge(rope_loaded[pair], 64 * (TB + 1))

                    @block.gpsimd
                    def _(pool):
                        def stage(pair, count, at):
                            two = slice(2 * pair, 2 * pair + 2)
                            loaded, rounded = (pool.snap(pool.to_reg(n)) for n in (64 * count, 4 * count - 2))
                            pool.tensor_copy(qs_hi[:, two, :], q_nope[:, two, at]).then_inc(staged[pair], 1)
                            pool.wait_ge(rope_loaded[pair], 64)
                            pool.wait_ge(rope_loaded[pair], loaded)
                            pool.tensor_copy(rope_hi[:, two, :], rope_in[:, two, :]).then_inc(staged[pair], 1)
                            pool.wait_ge(staged[pair], 2)
                            pool.wait_ge(staged[pair], rounded)
                            pool.tensor_tensor(qs_lo[:, two, :], q_nope[:, two, at], qs_hi[:, two, :].bitcast(F32),
                                               ALU.subtract).then_inc(staged[pair], 1)
                            pool.tensor_tensor(rope_lo[:, two, :], rope_in[0:ROPE, two, :], rope_hi[0:ROPE, two, :].bitcast(F32),
                                               ALU.subtract).then_inc(staged[pair], 1)

                        for pair in range(HEADS // 2):
                            stage(pair, 1, slice(0, P))
                        with pool.Fori(0, TB) as blk:
                            nxt = (blk + 1) % TB
                            pool.wait_ge(conv_step, n_conv * blk + 1)
                            pool.tensor_copy(taps[:, 0:HEADS], lc("conv_w")[:, bass.ds(HEADS * blk + first_taps[0], HEADS)]).then_inc(taps_in, 1)
                            pool.tensor_copy(taps[:, HEADS:n_conv], lc("conv_w")[:, bass.ds(blk + first_taps[1], 1)]).then_inc(taps_in, 1)
                            for pair in range(HEADS // 2):
                                pool.wait_ge(scores_done, HEADS * blk + 2 * pair + 2)
                                stage(pair, blk + 2, bass.ds(nxt * P, P))

                    @block.tensor
                    def _(pe):
                        def scores(h, slot, blk):
                            pe.wait_ge(staged[h // 2], 4 * blk + 4)
                            parts = ((qs_hi[:, h, :], k_hi[:, h, :]), (qs_hi[:, h, :], k_lo[:, h, :]), (qs_lo[:, h, :], k_hi[:, h, :]),
                                     (rope_hi[:, h, :], k_parts[:, h, :]), (rope_lo[:, h, :], k_parts[0:ROPE, h, :]))
                            for n, (queries, keys) in enumerate(parts):
                                for half in range(2):
                                    mm = pe.matmul(bank(2 * slot + half), queries, keys[:, half * HALF:(half + 1) * HALF],
                                                   start=n == 0, stop=n == len(parts) - 1)
                            mm.then_inc(scores_done, 1)

                        for b in range(2):
                            pe.sem_inc(pv_done[b], 1)
                        scores(0, 0, 0)
                        scores(1, 1, 0)
                        with pe.Fori(0, TB) as blk:
                            for h in range(HEADS):
                                g = HEADS * blk + h
                                slot = h % 2
                                pe.wait_ge(probs_done, g + 1)
                                for b in range(2):
                                    pe.wait_ge(copied[b], g + 1)
                                    for t in range(TB // 2):
                                        k = b * (TB // 2) + t
                                        mm = pe.transpose(psum[:, 4 + b, t * P:(t + 1) * P], probs[:, slot, k * P:(k + 1) * P], ident)
                                    mm.then_inc(turned[b], 1)
                                scores((h + 2) % HEADS, slot, blk + (h + 2) // HEADS)
                                pe.wait_ge(out_copied[slot], 2 * blk + h // 2 + 1)
                                for k in range(TB):
                                    if k % (TB // 2) == 0:
                                        pe.wait_ge(copied[k // (TB // 2)], g + 2)
                                    mm = pe.matmul(psum[:, 6 + slot, 0:P], v[:, k, h * VD:(h + 1) * VD], probs_t[:, slot, k, :],
                                                   start=k == 0, stop=k == TB - 1)
                                mm.then_inc(pv_done[slot], 1)

                    @block.scalar
                    def _(act):
                        def exps(h, slot, g, blk):
                            act.wait_ge(neg_done, g + 1)
                            act.activation(probs[:, slot, :], score_slot(slot), ACT.Exp, bias=neg_max[:, slot:slot + 1],
                                           scale=q["q_scale"][:, h, blk], accum_out=row_sum[:, slot:slot + 1]).then_inc(exp_done, 1)

                        for b in range(2):
                            act.sem_inc(copied[b], 1)
                            act.sem_inc(out_copied[b], 1)
                        exps(0, 0, 0, slice(0, 1))
                        exps(1, 1, 1, slice(0, 1))
                        with act.Fori(0, TB) as blk:
                            nxt = (blk + 1) % TB
                            for h in range(HEADS):
                                g = HEADS * blk + h
                                slot = h % 2
                                act.wait_ge(pv_done[slot], 2 * blk + h // 2 + 1)
                                for b in range(2):
                                    act.wait_ge(turned[b], g + 1)
                                    act.copy(probs_t[:, slot, b * (TB // 2):(b + 1) * (TB // 2), :],
                                             psum[:, 4 + b, :].rearrange("p (t m) -> p t m", m=P)).then_inc(copied[b], 1)
                                exps((h + 2) % HEADS, slot, g + 2, bass.ds(blk if h < 2 else nxt, 1))
                                act.wait_ge(pv_done[slot], 2 * blk + h // 2 + 2)
                                act.copy(mix[:, h, bass.ds(blk * P, P)], psum[:, 6 + slot, 0:P]).then_inc(out_copied[slot], 1)

                    @block.vector
                    def _(dve):
                        def maxima(h, slot, g, blk):
                            dve.wait_ge(scores_done, g + 1)
                            dve.reduce_max(row_max[:, slot:slot + 1], score_slot(slot), AX.X).then_inc(maxes, 1)
                            dve.wait_ge(maxes, g + 1)
                            dve.tensor_scalar(neg_max[:, slot:slot + 1], row_max[:, slot:slot + 1], q["q_neg"][:, h, blk], None,
                                              ALU.mult).then_inc(neg_done, 1)

                        def normalise(slot, g):
                            dve.wait_ge(exp_done, g + 1)
                            dve.reciprocal(inv_sum[:, slot:slot + 1], row_sum[:, slot:slot + 1]).then_inc(inv_done, 1)
                            dve.wait_ge(inv_done, g + 1)
                            dve.tensor_scalar(probs[:, slot, :], probs[:, slot, :], inv_sum[:, slot:slot + 1], None,
                                              ALU.mult).then_inc(probs_done, 1)

                        def conv_tap(blk, t):
                            if t:
                                dve.wait_ge(conv_step, n_conv * blk + t + 1)
                            tile, tap = (CT - 1, HEADS * blk + t) if t < HEADS else (CT - 2, blk + TAPS_PAD - TB)
                            acc = mix[:, HEADS + tile, :]
                            src = y[:, tile, bass.ds(tap, S)]
                            dve.scalar_tensor_tensor(out=acc, in0=src, scalar=taps[:, t:t + 1], in1=acc,
                                                     op0=ALU.mult, op1=ALU.add).then_inc(conv_step, 1)

                        dve.sem_inc(conv_step, 1)
                        maxima(0, 0, 0, slice(0, 1))
                        maxima(1, 1, 1, slice(0, 1))
                        normalise(0, 0)
                        with dve.Fori(0, TB) as blk:
                            nxt = (blk + 1) % TB
                            dve.wait_ge(taps_in, 2 * blk + 2)
                            dve.wait_ge(conv_step, n_conv * blk + 1)
                            for h in range(HEADS):
                                g = HEADS * blk + h
                                slot = h % 2
                                conv_tap(blk, h)
                                if h == HEADS - 1:
                                    conv_tap(blk, HEADS)
                                normalise(1 - slot, g + 1)
                                maxima((h + 2) % HEADS, slot, g + 2, bass.ds(blk if h < 2 else nxt, 1))

        def conv_norm_and_mix(l, lc, mix, gate):
            with ExitStack() as ctx:
                sq = sb("cn_sq", [P, 2, S], F32, ctx)
                x_sq = sb("cn_x_sq", [P, 2, S], F32, ctx)
                acc = sb("cn_acc", [P, S], F32, ctx)
                stat = sb("cn_stat", [P, 2, TB], F32, ctx)
                diag = sb("cn_diag", [P, TB, P], F32, ctx)
                w = split_tensors("lo", DT, ctx)
                mix_hi, mix_lo = (sb(f"lo_mix_{n}", [P, DT, S], F32R, ctx) for n in ("hi", "lo"))
                names = ("means", "centred", "sq", "added", "var_sum", "root", "rstd", "diag", "spread", "scaled", "silu", "hi", "lo", "sq_done",
                         "sq_added")
                (means, centred, sq_done, added, var_sum, root, rstd, diag_done, spread_done, scaled, silu, hi_done,
                 lo_done, x_sq_done, x_sq_added) = [sem("cn_" + n) for n in names]
                rows = [mix[:, HEADS + j, :] for j in range(CT)]
                mean_banks, spread_banks, var_cols = banks(2), banks(6), psum[:, 2, 0:TB]
                tiles = tile_of(A["w_out"])

                with nc.Block() as block:
                    @block.sync
                    def _(sp):
                        stream_tiles(sp, lambda n: tiles(n + l * DT), w, DT // 2)

                    @block.gpsimd
                    def _(pool):
                        clear_squares(pool, x_sq, x_sq_added)
                        split_tiles(pool, w, DT // 2)

                    @block.tensor
                    def _(pe):
                        def variance():
                            pe.wait_ge(added, CT - 1)
                            token_sums(pe, var_cols, acc).then_inc(var_sum, 1)
                            spread(pe, spread_banks, diag, diag_done).then_inc(spread_done, 1)

                        for half in range(2):
                            for j in range(CT):
                                mm = pe.matmul(bank(2 + half), ones, rows[j][:, half * HALF:(half + 1) * HALF],
                                               start=j == 0, stop=j == CT - 1)
                        mm.then_inc(means, 1)
                        linear(pe, mix_hi, mix_lo, DT, w, DT // 2, lo_done, variance)

                    @block.vector
                    def _(dve):
                        def low_part(k):
                            dve.wait_ge(hi_done, k + 1)
                            dve.tensor_tensor(mix_lo[:, k, :], mix[:, k, :], mix_hi[:, k, :].bitcast(F32),
                                              ALU.subtract).then_inc(lo_done, 1)

                        def add(j):
                            dve.wait_ge(sq_done, j + 1)
                            if j > 1:
                                dve.wait_ge(added, j - 1)
                            dve.tensor_tensor(acc[:], sq[:, 0, :] if j == 1 else acc[:], sq[:, j % 2, :], ALU.add).then_inc(added, 1)

                        for b in range(2):
                            dve.sem_inc(w["read"][b], 1)
                        for k in range(HEADS):
                            low_part(k)
                        dve.wait_ge(means, 1)
                        for j in range(CT):
                            dve.scalar_tensor_tensor(out=rows[j], in0=mean_banks, scalar=-1.0 / CONV_CH, in1=rows[j],
                                                     op0=ALU.mult, op1=ALU.add).then_inc(centred, 1)
                            if j >= 2:
                                add(j - 1)
                        add(CT - 1)
                        dve.wait_ge(root, 1)
                        dve.reciprocal(stat[:, 1, :], stat[:, 0, :]).then_inc(rstd, 1)
                        dve.wait_ge(rstd, 1)
                        for b in range(TB):
                            dve.tensor_scalar(diag[:, b, :], ident, stat[:, 1, b:b + 1], None, ALU.mult).then_inc(diag_done, 1)
                        dve.wait_ge(spread_done, 1)
                        for j in range(CT):
                            dve.tensor_tensor(rows[j], rows[j], spread_banks, ALU.mult).then_inc(scaled, 1)
                            if j >= 2:
                                low_part(HEADS + j - 2)
                        for j in (CT - 2, CT - 1):
                            low_part(HEADS + j)
                        add_to_x(dve, w["done"], w["read"], gate, (x_sq, x_sq_done, x_sq_added))

                    @block.scalar
                    def _(act):
                        for k in range(HEADS):
                            act.copy(mix_hi[:, k, :], mix[:, k, :]).then_inc(hi_done, 1)
                        for j in range(CT):
                            act.wait_ge(centred, j + 1)
                            if j >= 2:
                                act.wait_ge(added, max(1, j - 2))
                            act.activation(sq[:, j % 2, :], rows[j], ACT.Square).then_inc(sq_done, 1)
                        act.wait_ge(var_sum, 1)
                        act.activation(stat[:, 0, :], var_cols, ACT.Sqrt, bias=EPS, scale=1.0 / CONV_CH).then_inc(root, 1)
                        for j in range(CT):
                            act.wait_ge(scaled, j + 1)
                            act.activation(rows[j], rows[j], ACT.Silu, scale=lc("conv_g")[:, j:j + 1],
                                           bias=lc("conv_nb")[:, j:j + 1]).then_inc(silu, 1)
                            act.wait_ge(silu, j + 1)
                            act.copy(mix_hi[:, HEADS + j, :], rows[j]).then_inc(hi_done, 1)
                        square_added(act, w["read"], x_sq, x_sq_done, x_sq_added)

        def mix_out(tag, tiles, rows, back):
            with ExitStack() as ctx:
                w = split_tensors(tag, DT, ctx)
                mix_hi, mix_lo = (sb(f"{tag}_mix_{n}", [P, DT, S], F32R, ctx) for n in ("hi", "lo"))
                sq = sb(f"{tag}_sq", [P, 2, S], F32, ctx)
                hi_done, lo_done, x_back, sq_done, sq_added = [sem(f"{tag}_{n}") for n in (
                    "hi_done", "lo_done", "x_back", "sq_done", "sq_added")]
                with nc.Block() as block:
                    @block.sync
                    def _(sp):
                        def x_back_in():
                            sp.wait_ge(lo_done, DT)
                            back(sp).then_inc(x_back, 16)

                        stream_tiles(sp, tiles, w, DT // 2, x_back_in)

                    @block.gpsimd
                    def _(pool):
                        clear_squares(pool, sq, sq_added)
                        split_tiles(pool, w, DT // 2)

                    @block.scalar
                    def _(act):
                        for k in range(DT):
                            act.copy(mix_hi[:, k, :], rows(k)).then_inc(hi_done, 1)
                        square_added(act, w["read"], sq, sq_done, sq_added)

                    @block.tensor
                    def _(pe):
                        linear(pe, mix_hi, mix_lo, DT, w, DT // 2, lo_done)

                    @block.vector
                    def _(dve):
                        for b in range(2):
                            dve.sem_inc(w["read"][b], 1)
                        for k in range(DT):
                            dve.wait_ge(hi_done, k + 1)
                            dve.tensor_tensor(mix_lo[:, k, :], rows(k), mix_hi[:, k, :].bitcast(F32),
                                              ALU.subtract).then_inc(lo_done, 1)
                        dve.wait_ge(x_back, 16)
                        add_to_x(dve, w["done"], w["read"], None, (sq, sq_done, sq_added))

        def clear_squares(pool, sq, sq_added):
            pool.memset(sq[:, 1, :], 0.0).then_inc(sq_added, 1)
            pool.memset(sq_sum[:], 0.0).then_inc(sq_added, 1)

        def square_added(act, read, sq, sq_done, sq_added):
            act.sem_inc(sq_done, 1)
            with act.Fori(0, DT // 2) as i:
                for b in range(2):
                    act.wait_ge(read[b], i + 2)
                    act.wait_ge(sq_added, 2 * i + b + 2)
                    act.activation(sq[:, b, :], x[:, bass.ds(2 * i + b, 1), :].rearrange("p a s -> p (a s)"),
                                   ACT.Square).then_inc(sq_done, 1)

        def add_to_x(dve, done, read, gate, squares):
            sq, sq_done, sq_added = squares

            def add_square(n, b):
                dve.wait_ge(sq_done, n + 1)
                dve.wait_ge(sq_added, n + 2)
                dve.tensor_tensor(sq_sum[:], sq_sum[:], sq[:, 1 - b, :], ALU.add).then_inc(sq_added, 1)

            with dve.Fori(0, DT // 2) as i:
                for b in range(2):
                    dve.wait_ge(done[b], i + 2)
                    xn = x[:, bass.ds(2 * i + b, 1), :].rearrange("p a s -> p (a s)")
                    if gate is None:
                        ins = dve.tensor_tensor(xn, banks(4 * b), xn, ALU.add)
                    else:
                        ins = dve.scalar_tensor_tensor(out=xn, in0=banks(4 * b), scalar=gate[:, bass.ds(2 * i + b, 1)],
                                                       in1=xn, op0=ALU.mult, op1=ALU.add)
                    ins.then_inc(read[b], 1)
                    add_square(2 * i + b, b)
            add_square(DT, 0)

        def experts_part(l, gain, shift, gate):
            with ExitStack() as ctx:
                slots = sb("slots", [P, EXPERTS], U32, ctx)
                slot_gate = sb("slot_gate", [P, EXPERTS], F32, ctx)
                with ExitStack() as running:
                    raw = [sb(f"ex_raw{i}", [P, 4, HALF], F32, running) for i in range(RAW)]
                    hi, lo = ([sb(f"ex_{n}{i}", [P, 4, HALF], F32R, running) for i in range(SPLIT_EARLY)] for n in ("hi", "lo"))
                    loaded = [sem(f"ex_loaded{i}") for i in range(RAW)]
                    w_hi, w_lo = sem("ex_w_hi"), sem("ex_w_lo")
                    pieces = (expert_pieces(l), raw, hi, lo, loaded, w_hi, w_lo)
                    route(l, gain, shift, slots, slot_gate, pieces)
                    run_experts(slots, slot_gate, pieces)
                combine(gate)

        def load_ahead(sp, e, j, pieces):
            load_piece, raw, _, _, loaded, _, w_lo = pieces
            split = sp.snap(sp.to_reg(PIECES * e + j + 1))
            sp.wait_ge(w_lo, 1)
            sp.wait_ge(w_lo, split)
            ahead = j + RAW
            load_piece(sp, raw[j % RAW], e + ahead // PIECES, ahead % PIECES).then_inc(loaded[j % RAW], 16)

        def route(l, gain, shift, slots, slot_gate, pieces):
            load_piece, raw, hi, lo, loaded, w_hi, w_lo = pieces
            with ExitStack() as ctx:
                h = sb("rt_h", [P, DT, S], F32, ctx)
                rows = sb("rt_rows", [P, 2, D], F32, ctx)
                t = norm_tensors("n2", ctx, rows[:, 0, :])
                w_r = sb("w_r", [P, DT, EXPERTS], F32, ctx)
                logit = sq_sum[0:EXPERTS, :]
                aff = sb("aff", [P, TB, EXPERTS], F32, ctx)
                stat = sb("rt_stat", [P, 3, TB], F32, ctx)
                assert CAP == P and S // 2 == HALF
                halves = sb("rt_halves", [P, TB // 2, 2, EXPERTS], F32, ctx)
                aff_t = sq_sum[0:2 * EXPERTS, 0:HALF]
                best = sb("best", [2 * EXPERTS, CAP], F32, ctx)
                place = sb("place", [2 * EXPERTS, CAP], U32, ctx)
                place_f = sb("place_f", [2 * EXPERTS, CAP], F32, ctx)
                chosen = sb("chosen", [P, 2, 2, EXPERTS], F32, ctx)
                pick = sb("rt_pick", [P, 3, EXPERTS], F32, ctx)
                part = sb("rt_part", [P, 2, DT, P], F32, ctx)
                names = ("w_in", "scaled", "h_ready", "logits", "logit_copied", "turned", "soft", "exp_done", "aff_done",
                         "aff_turned", "aff_copied", "step", "place_done", "back", "chosen", "flipped", "slots_done", "zeroed", "rows_out")
                (w_in, scaled, h_ready, logits, logit_copied, turned, soft, exp_done, aff_done, aff_turned, aff_copied, step,
                 place_done, back, chosen_done, flipped, slots_done, zeroed, rows_out) = [sem("rt_" + n) for n in names]
                part_in = [sem(f"rt_part_in{b}") for b in range(2)]
                row_turned = [sem(f"rt_row_turned{b}") for b in range(2)]
                row_copied = [sem(f"rt_row_copied{b}") for b in range(2)]
                flip_psum = psum[:, 4, 0:4 * EXPERTS].rearrange("p (a b e) -> p a b e", a=2, b=2)
                soft_psum = psum[:, 4, 0:TB * EXPERTS].rearrange("p (t e) -> p t e", e=EXPERTS)
                with nc.Block() as block:
                    @block.sync
                    def _(sp):
                        sp.dma_start(w_r[:], A["w_router"][bass.ds(l, 1)].rearrange("a (k p) e -> p (a k) e", p=P)).then_inc(w_in, 16)
                        sp.sem_inc(rows_out, 32)
                        with sp.Fori(0, TB) as i:
                            sp.dma_start(moe_rows[bass.ds(i * P, P), :], zero_row[:]).then_inc(zeroed, 16)
                        for j in range(RAW):
                            load_piece(sp, raw[j], 0, j).then_inc(loaded[j], 16)
                        for j in range(SPLIT_EARLY):
                            load_ahead(sp, 0, j, pieces)
                        with sp.Fori(0, TB // 2) as i:
                            for b in range(2):
                                sp.wait_ge(row_copied[b], i + 2)
                                sp.dma_start(h2_rows[bass.ds((2 * i + b) * P, P), :], rows[:, b, :]).then_inc(rows_out, 16)
                        sp.wait_ge(zeroed, 16 * TB)
                        sp.wait_ge(rows_out, 16 * TB + 32)

                    @block.gpsimd
                    def _(pool):
                        for j in range(SPLIT_EARLY):
                            pool.wait_ge(w_hi, j + 1)
                            pool.tensor_tensor(lo[j][:], raw[j][:], hi[j][:].bitcast(F32), ALU.subtract).then_inc(w_lo, 1)
                        pool.wait_ge(h_ready, DT)
                        with pool.Fori(0, TB // 2) as i:
                            for b in range(2):
                                pool.wait_ge(row_turned[b], i + 1)
                                pool.tensor_copy(part[:, b, :, :], h[:, :, bass.ds((2 * i + b) * P, P)]).then_inc(part_in[b], 1)

                    @block.scalar
                    def _(act):
                        for b in range(2):
                            act.sem_inc(row_copied[b], 1)
                        norm_act(act, t)
                        for k in range(DT):
                            act.wait_ge(scaled, k + 1)
                            act.activation(h[:, k, :], h[:, k, :], ACT.Identity, scale=gain[:, 1, k:k + 1],
                                           bias=shift[:, k:k + 1]).then_inc(h_ready, 1)
                        for j in range(SPLIT_EARLY):
                            act.wait_ge(loaded[j], 16)
                            act.copy(hi[j][:], raw[j][:]).then_inc(w_hi, 1)
                        act.wait_ge(logits, 1)
                        act.copy(logit, banks(0)[0:EXPERTS, :]).then_inc(logit_copied, 1)
                        act.wait_ge(soft, 2)
                        act.activation(aff[:], aff[:], ACT.Exp).then_inc(exp_done, 1)
                        act.wait_ge(aff_turned, 1)
                        act.copy(aff_t, bank(0)[0:2 * EXPERTS, :]).then_inc(aff_copied, 1)
                        with act.Fori(0, TB // 2) as i:
                            for b in range(2):
                                act.wait_ge(row_turned[b], i + 2)
                                act.wait_ge(rows_out, 32 * i + 32)
                                act.copy(rows[:, b, :], banks(2 + 4 * b)).then_inc(row_copied[b], 1)

                    @block.vector
                    def _(dve):
                        norm_dve(dve, t)
                        for k in range(DT):
                            dve.tensor_tensor(h[:, k, :], x[:, k, :], banks(2), ALU.mult).then_inc(scaled, 1)
                        dve.wait_ge(turned, 1)
                        dve.tensor_reduce(stat[:, 0, :], soft_psum, AX.X, ALU.max).then_inc(soft, 1)
                        dve.wait_ge(soft, 1)
                        dve.tensor_tensor(aff[:], soft_psum, stat[:, 0, :].unsqueeze(2).to_broadcast([P, TB, EXPERTS]),
                                          ALU.subtract).then_inc(soft, 1)
                        dve.wait_ge(exp_done, 1)
                        dve.tensor_reduce(stat[:, 1, :], aff[:], AX.X, ALU.add).then_inc(soft, 1)
                        dve.wait_ge(soft, 3)
                        dve.reciprocal(stat[:, 2, :], stat[:, 1, :]).then_inc(soft, 1)
                        dve.wait_ge(soft, 4)
                        for half in range(2):
                            blocks = slice(half * TB // 2, (half + 1) * TB // 2)
                            dve.tensor_tensor(halves[:, :, half, :], aff[:, blocks, :], stat[:, 2, blocks].unsqueeze(2).to_broadcast(
                                [P, TB // 2, EXPERTS]), ALU.mult).then_inc(aff_done, 1)
                        dve.wait_ge(aff_copied, 1)
                        ch = Chain(dve, step)
                        for r in range(CAP // 8):
                            at = slice(8 * r, 8 * r + 8)
                            ch.step(dve.max(best[:, at], aff_t))
                            ch.step(dve.max_index(place[:, at], best[:, at], aff_t))
                            ch.step(dve.match_replace(aff_t, best[:, at], aff_t, -1.0))
                        dve.tensor_copy(place_f[:], place[:]).then_inc(place_done, 1)
                        dve.wait_ge(back, 1)
                        dve.tensor_copy(chosen[:].rearrange("p a b e -> p (a b e)"), psum[:, 5, 0:4 * EXPERTS]).then_inc(chosen_done, 1)
                        dve.wait_ge(flipped, 1)
                        first, token, take = (pick[:, i, :] for i in range(3))
                        dve.tensor_tensor(slot_gate[:], chosen[:, 1, 0, :], flip_psum[:, 1, 1, :], ALU.max).then_inc(slots_done, 1)
                        ch.step(dve.tensor_tensor(first, chosen[:, 1, 0, :], flip_psum[:, 1, 1, :], ALU.is_ge))
                        ch.step(dve.tensor_scalar(token, flip_psum[:, 0, 1, :], float(HALF), None, ALU.add))
                        ch.step(dve.tensor_tensor(take, chosen[:, 0, 0, :], token, ALU.subtract))
                        ch.step(dve.tensor_tensor(take, take, first, ALU.mult))
                        ch.step(dve.tensor_tensor(token, token, take, ALU.add))
                        dve.tensor_copy(slots[:], token).then_inc(slots_done, 1)

                    @block.tensor
                    def _(pe):
                        for b in range(2):
                            pe.sem_inc(row_turned[b], 1)
                        norm_pe(pe, t)
                        pe.wait_ge(w_in, 16)
                        for k in range(DT):
                            pe.wait_ge(h_ready, k + 1)
                            for half in range(2):
                                mm = pe.matmul(bank(half)[0:EXPERTS, :], w_r[:, k, :], h[:, k, half * HALF:(half + 1) * HALF],
                                               start=k == 0, stop=k == DT - 1)
                        mm.then_inc(logits, 1)
                        pe.wait_ge(logit_copied, 1)
                        for b in range(TB):
                            mm = pe.transpose(soft_psum[:, b, :], logit[:, b * P:(b + 1) * P], ident[0:EXPERTS, 0:EXPERTS])
                        mm.then_inc(turned, 1)
                        pe.wait_ge(aff_done, 2)
                        for b in range(TB // 2):
                            mm = pe.transpose(bank(0)[0:2 * EXPERTS, b * P:(b + 1) * P], halves[:, b, :, :].rearrange("p h e -> p (h e)"),
                                              ident)
                        mm.then_inc(aff_turned, 1)
                        with pe.Fori(0, TB // 2) as i:
                            for b in range(2):
                                pe.wait_ge(part_in[b], i + 1)
                                pe.wait_ge(row_copied[b], i + 1)
                                for k in range(DT):
                                    mm = pe.transpose(banks(2 + 4 * b)[:, k * P:(k + 1) * P], part[:, b, k, :], ident)
                                mm.then_inc(row_turned[b], 1)
                        pe.wait_ge(place_done, 1)
                        both = ident[0:2 * EXPERTS, 0:2 * EXPERTS]
                        pe.transpose(psum[:, 5, 0:2 * EXPERTS], place_f[:], both)
                        pe.transpose(psum[:, 5, 2 * EXPERTS:4 * EXPERTS], best[:], both).then_inc(back, 1)
                        pe.wait_ge(chosen_done, 1)
                        pe.matmul(flip_psum.rearrange("p a b e -> p (a b e)"), flip[:], chosen[:].rearrange("p a b e -> p (a b e)"),
                                  start=True, stop=True).then_inc(flipped, 1)

        def expert_pieces(l):
            raw = [A["w_gate"], A["w_up"], A["w_down"]]

            def piece(e, j):
                one = bass.ds(l * EXPERTS + e, 1)
                if j < 8:
                    f, n, half = j // 4, j // 2 % 2, j % 2
                    return raw[n][one, half * HALF:(half + 1) * HALF, f * HALF:(f + 1) * HALF].rearrange("a (k p) n -> p (a k) n", p=P)
                rows = slice((j - 8) * 2 * P, (j - 7) * 2 * P)
                return raw[2][one, rows, :].rearrange("a (k p) n -> p (a k) n", p=P)

            def room(buf, j):
                return buf[:] if j < 8 else buf[:].rearrange("p (k o) n -> p k (o n)", o=2)

            return lambda sp, buf, e, j: sp.dma_start(room(buf, j), piece(e, j))

        def run_experts(slots, slot_gate, pieces):
            _, raw, hi, lo, loaded, w_hi, w_lo = pieces
            with ExitStack() as ctx:
                hi, lo = (early + [sb(f"ex_{n}{i}", [P, 4, HALF], F32R, ctx) for i in range(SPLIT_EARLY, PARTS)]
                          for n, early in (("hi", hi), ("lo", lo)))
                idx_in = sb("idx_in", [P, 1], U32, ctx)
                idx_out = sb("idx_out", [P, 1], U32, ctx)
                xe = sb("xe", [P, D], F32, ctx)
                xe_hi, xe_lo = (sb("xe_" + n, [P, DT, P], F32R, ctx) for n in ("hi", "lo"))
                act_g = sb("act_g", [P, 2, HALF], F32, ctx)
                hid = sb("hid", [P, 2, HALF], F32, ctx)
                hid_hi, hid_lo = (sb("hid_" + n, [P, FT, P], F32R, ctx) for n in ("hi", "lo"))
                ye = sb("ye", [P, D], F32, ctx)
                names = ("idx_in", "gathered", "idx_out", "scattered", "w_used", "silu", "hid", "xe_turned",
                         "xe_hi", "xe_lo", "hid_turned", "hid_hi", "hid_lo", "ye", "ye_free")
                (idx_in_done, gathered, idx_out_done, scattered, w_used, silu_done, hid_done, xe_turned, xe_hi_done, xe_lo_done,
                 hid_turned, hid_hi_done, hid_lo_done, ye_done, ye_free) = [sem("ex_" + n) for n in names]
                last = EXPERTS - 1
                turn_bank = (5, 4)
                hid_bank = (4, 5)

                def in_bank(i):
                    return bank(i).rearrange("p (k m) -> p k m", m=P)

                def four(b):
                    return slice(4 * b, 4 * b + 4)

                with nc.Block() as block:
                    @block.sync
                    def _(sp):
                        for j in range(SPLIT_EARLY, PIECES):
                            load_ahead(sp, 0, j, pieces)
                        with sp.Fori(1, last) as e:
                            for j in range(PIECES):
                                load_ahead(sp, e, j, pieces)
                        for j in range(PIECES - RAW):
                            load_ahead(sp, last, j, pieces)

                    @block.gpsimd
                    def _(pool):
                        def gather(e, count):
                            pool.tensor_copy(idx_in[:], slots[:, bass.ds(e, 1)]).then_inc(idx_in_done, 1)
                            pool.wait_ge(idx_in_done, 1)
                            pool.wait_ge(idx_in_done, count)
                            pool.indirect_dma_start(xe[:], None, h2_rows, bass.IndirectOffsetOnAxis(ap=idx_in[:, 0:1], axis=0)).then_inc(gathered, 16)

                        def scatter(e, count, written, left):
                            pool.tensor_copy(idx_out[:], slots[:, bass.ds(e, 1)]).then_inc(idx_out_done, 1)
                            pool.wait_ge(idx_out_done, 1)
                            pool.wait_ge(idx_out_done, count)
                            pool.wait_ge(ye_done, written)
                            pool.indirect_dma_start(moe_rows, bass.IndirectOffsetOnAxis(ap=idx_out[:, 0:1], axis=0), ye[:], None,
                                                    compute_op=ALU.add).then_inc(scattered, 16)
                            pool.wait_ge(scattered, left)
                            pool.sem_inc(ye_free, 1)

                        pool.sem_inc(ye_free, 1)
                        gather(0, 1)
                        pool.wait_ge(xe_turned, 2)
                        gather(1, 2)
                        with pool.Fori(0, EXPERTS - 2) as e:
                            reg = [pool.snap(pool.to_reg(v)) for v in (2 * e + 4, e + 3, e + 1, 2 * e + 4, 16 * e + 16)]
                            pool.wait_ge(gathered, 32)
                            pool.wait_ge(xe_turned, reg[0])
                            gather(e + 2, reg[1])
                            scatter(e, *reg[2:])
                        for e in (last - 1, last):
                            scatter(e, e + 1, 2 * e + 4, 16 * e + 16)

                    @block.tensor
                    def _(pe):
                        def turn_rows(e):
                            pe.wait_ge(gathered, 16 * e + 16)
                            for b in range(2):
                                for k in range(4):
                                    mm = pe.transpose(psum[:, turn_bank[b], k * P:(k + 1) * P], xe[:, (4 * b + k) * P:(4 * b + k + 1) * P], ident)
                                mm.then_inc(xe_turned, 1)

                        def turn_hidden(e, f):
                            pe.wait_ge(hid_done, 2 * e + f + 1)
                            for k in range(4):
                                mm = pe.transpose(psum[:, hid_bank[f], k * P:(k + 1) * P], hid[:, f, k * P:(k + 1) * P], ident)
                            mm.then_inc(hid_turned, 1)

                        def take(e, j, steps):
                            pe.wait_ge(w_lo, PIECES * e + j + 1)
                            h, r = hi[j % PARTS], lo[j % PARTS]
                            for out, x_hi, x_lo, k, first, end in steps:
                                pe.matmul(bank(out), x_hi, h[:, k, :], start=first, stop=False)
                                pe.matmul(bank(out), x_hi, r[:, k, :], start=False, stop=False)
                                mm = pe.matmul(bank(out), x_lo, h[:, k, :], start=False, stop=end)
                            mm.then_inc(w_used, 1)

                        def expert(e, more):
                            for j in range(8):
                                f, n, half = j // 4, j // 2 % 2, j % 2
                                if j < 2:
                                    pe.wait_ge(xe_lo_done, 2 * e + half + 1)
                                if j == 6:
                                    turn_hidden(e, 0)
                                take(e, j, [(2 * f + n, xe_hi[:, 4 * half + k, :], xe_lo[:, 4 * half + k, :], k,
                                             half == 0 and k == 0, half == 1 and k == 3) for k in range(4)])
                            pe.wait_ge(hid_lo_done, 2 * e + 1)
                            if more:
                                turn_rows(e + 1)
                            for j in range(8, PIECES):
                                if j == 8:
                                    pe.wait_ge(ye_done, 2 * e + 2)
                                if j == 10:
                                    if more:
                                        pe.wait_ge(xe_lo_done, 2 * e + 3)
                                    turn_hidden(e, 1)
                                    pe.wait_ge(hid_lo_done, 2 * e + 2)
                                at = 2 * (j - 8)
                                take(e, j, [(6 + o, hid_hi[:, at + k, :], hid_lo[:, at + k, :], 2 * k + o,
                                             at + k == 0, at + k == FT - 1) for k in range(2) for o in range(2)])

                        turn_rows(0)
                        with pe.Fori(0, last) as e:
                            expert(e, True)
                        expert(last, False)

                    @block.scalar
                    def _(act):
                        def split_hi(e, j):
                            n = PIECES * e + j
                            act.wait_ge(loaded[j % RAW], 16 * ((PIECES // RAW) * e + j // RAW + 1))
                            if not isinstance(n, int) or n >= PARTS:
                                act.wait_ge(w_used, n - PARTS + 1)
                            act.copy(hi[j % PARTS][:], raw[j % RAW][:]).then_inc(w_hi, 1)

                        def rows_hi(e):
                            for b in range(2):
                                act.wait_ge(xe_turned, 2 * e + b + 1)
                                act.copy(xe_hi[:, four(b), :], in_bank(turn_bank[b])).then_inc(xe_hi_done, 1)

                        def hidden_hi(e, f):
                            act.wait_ge(hid_turned, 2 * e + f + 1)
                            act.copy(hid_hi[:, four(f), :], in_bank(hid_bank[f])).then_inc(hid_hi_done, 1)

                        def silu(e, f):
                            act.wait_ge(w_used, PIECES * e + 4 * f + 2)
                            act.activation(act_g[:, f, :], bank(2 * f), ACT.Silu).then_inc(silu_done, 1)

                        def expert(e, more):
                            for j in range(PARTS, PIECES + PARTS):
                                if j < PIECES or more:
                                    split_hi(e, j)
                                if j == 4:
                                    silu(e, 0)
                                if j == 8:
                                    silu(e, 1)
                                    hidden_hi(e, 0)
                                if j == 10 and more:
                                    rows_hi(e + 1)
                                if j == 12:
                                    hidden_hi(e, 1)

                        rows_hi(0)
                        for j in range(SPLIT_EARLY, PARTS):
                            split_hi(0, j)
                        with act.Fori(0, last) as e:
                            expert(e, True)
                        expert(last, False)

                    @block.vector
                    def _(dve):
                        def split_lo(e, j):
                            dve.wait_ge(w_hi, PIECES * e + j + 1)
                            dve.tensor_tensor(lo[j % PARTS][:], raw[j % RAW][:], hi[j % PARTS][:].bitcast(F32), ALU.subtract).then_inc(w_lo, 1)

                        def rows_lo(e):
                            for b in range(2):
                                dve.wait_ge(xe_hi_done, 2 * e + b + 1)
                                dve.tensor_tensor(xe_lo[:, four(b), :], in_bank(turn_bank[b]), xe_hi[:, four(b), :].bitcast(F32),
                                                  ALU.subtract).then_inc(xe_lo_done, 1)

                        def hidden(e, f):
                            dve.wait_ge(silu_done, 2 * e + f + 1)
                            dve.wait_ge(w_used, PIECES * e + 4 * f + 4)
                            dve.tensor_tensor(hid[:, f, :], act_g[:, f, :], bank(2 * f + 1), ALU.mult).then_inc(hid_done, 1)

                        def hidden_lo(e, f):
                            dve.wait_ge(hid_hi_done, 2 * e + f + 1)
                            dve.tensor_tensor(hid_lo[:, four(f), :], in_bank(hid_bank[f]), hid_hi[:, four(f), :].bitcast(F32),
                                              ALU.subtract).then_inc(hid_lo_done, 1)

                        def output(e):
                            dve.wait_ge(w_used, PIECES * e + PIECES)
                            dve.wait_ge(ye_free, e + 1)
                            for o in range(2):
                                dve.tensor_scalar(ye[:, o * HALF:(o + 1) * HALF], bank(6 + o), slot_gate[:, bass.ds(e, 1)], None,
                                                  ALU.mult).then_inc(ye_done, 1)

                        def expert(e, more):
                            for j in range(PARTS, PIECES + PARTS):
                                if j < PIECES or more:
                                    split_lo(e, j)
                                if j == 6:
                                    hidden(e, 0)
                                if j == 8:
                                    hidden_lo(e, 0)
                                if j == 10:
                                    hidden(e, 1)
                                    if more:
                                        rows_lo(e + 1)
                                if j == 12:
                                    hidden_lo(e, 1)
                                if j == 14:
                                    output(e)

                        dve.sem_inc(ye_done, 2)
                        rows_lo(0)
                        for j in range(SPLIT_EARLY, PARTS):
                            split_lo(0, j)
                        with dve.Fori(0, last) as e:
                            expert(e, True)
                        expert(last, False)

        def combine(gate):
            with ExitStack() as ctx:
                rows = [sb(f"cb_rows{b}", [P, TB, 2 * P], F32, ctx) for b in range(2)]
                loaded = [sem(f"cb_loaded{b}") for b in range(2)]
                turned = [sem(f"cb_turned{b}") for b in range(2)]
                read = [sem(f"cb_read{b}") for b in range(2)]
                sq = sb("cb_sq", [P, 2, S], F32, ctx)
                sq_done, sq_added = sem("cb_sq_done"), sem("cb_sq_added")
                with nc.Block() as block:
                    @block.sync
                    def _(sp):
                        for n in range(DT // 2):
                            if n >= 2:
                                sp.wait_ge(turned[1], n)
                            sp.dma_start(rows[n % 2][:], moe_rows[:, 2 * n * P:2 * (n + 1) * P].rearrange(
                                "(t p) m -> p t m", p=P)).then_inc(loaded[n % 2], 16)

                    @block.tensor
                    def _(pe):
                        for j in range(2):
                            pe.sem_inc(turned[j], 1)
                        with pe.Fori(0, DT // 4) as i:
                            for b in range(2):
                                pe.wait_ge(loaded[b], 16 * i + 16)
                                for j in range(2):
                                    pe.wait_ge(read[j], 2 * i + b + 1)
                                    for t in range(TB):
                                        mm = pe.transpose(banks(4 * j)[:, t * P:(t + 1) * P], rows[b][:, t, j * P:(j + 1) * P], ident)
                                    mm.then_inc(turned[j], 1)

                    @block.gpsimd
                    def _(pool):
                        clear_squares(pool, sq, sq_added)

                    @block.scalar
                    def _(act):
                        square_added(act, read, sq, sq_done, sq_added)

                    @block.vector
                    def _(dve):
                        for b in range(2):
                            dve.sem_inc(read[b], 1)
                        add_to_x(dve, turned, read, gate, (sq, sq_done, sq_added))

        def second(out):
            def s2(name):
                return scols[:, SC[name][0]:SC[name][1]]

            with ExitStack() as ctx:
                mix = sb("mix2", [P, DT, S], F32, ctx)
                with ExitStack() as before:
                    qfg = sb("qfg", [P, 3, HG, S], F32, before)
                    last = sb("hg_last", [P, HG, NCH], F32, before)
                    lru, v, lru_x, kd = x[:, 0:LT, :], x[:, LT:LT + HG, :], mix[:, 0:LT, :], mix[:, LT:LT + HG, :]
                    project2(mix, qfg, lru_x, lru, v, kd, last, s2)
                    mixers(mix, qfg, lru_x, lru, v, kd, last, s2)
                mix_out("so", tile_of(A["w_out_2"]), lambda k: mix[:, k, :] if k < HG else lru[:, k - HG, :],
                        lambda sp: sp.dma_start(x[:], x_rows.rearrange("(k p) s -> p k s", p=P)))
            feed_forward(s2("ffn_norm"))
            final_norm(out, s2("final"))

        def scale_rows(dve, dst, gain, done):
            for k in range(DT):
                dve.scalar_tensor_tensor(out=dst[:, k, :], in0=x[:, k, :], scalar=gain[:, k:k + 1], in1=banks(2),
                                         op0=ALU.mult, op1=ALU.mult).then_inc(done, 1)

        def split_norm_act(act, full, hi, scaled, hi_done):
            for k in range(DT):
                act.wait_ge(scaled, k + 1)
                act.copy(hi[:, k, :], full[:, k % 2, :]).then_inc(hi_done, 1)

        def split_norm_dve(dve, full, gain, hi, lo, scaled, hi_done, lo_done):
            def low_part(k):
                dve.wait_ge(hi_done, k + 1)
                dve.tensor_tensor(lo[:, k, :], full[:, k % 2, :], hi[:, k, :].bitcast(F32), ALU.subtract).then_inc(lo_done, 1)

            for k in range(DT):
                if k >= 2:
                    low_part(k - 2)
                    dve.wait_ge(lo_done, k - 1)
                dve.scalar_tensor_tensor(out=full[:, k % 2, :], in0=x[:, k, :], scalar=gain[:, k:k + 1], in1=banks(2),
                                         op0=ALU.mult, op1=ALU.mult).then_inc(scaled, 1)
            low_part(DT - 2)
            low_part(DT - 1)

        def project2(mix, qfg, lru_x, lru_g, v, kd, last, s2):
            q, f, g = (qfg[:, i, :, :] for i in range(3))
            with ExitStack() as ctx:
                xn_hi, xn_lo = (sb("xn_" + n, [P, DT, S], F32R, ctx) for n in ("hi", "lo"))
                t = norm_tensors("n3", ctx, mix[:, 4, :])
                full = mix[:, 0:2, :]
                cum, diff = g[:, 0:2, :], g[:, 2:4, :]
                lb = sb("hg_lb", [P, 3, HG], F32, ctx)
                reset = mix[:, 3, :]
                w = split_tensors("p2", DT, ctx)
                done, read = w["done"], w["read"]
                names = ("scaled", "hi_done", "lo_done", "x_out", "lb", "lb_act", "reset", "keys", "logs", "cums", "grow",
                         "shrink", "diffs", "tail", "q_dec", "k_state", "k_dec")
                (scaled, hi_done, lo_done, x_out, lbs, lb_act, reset_done, keys, logs, cums, grow, shrink, diffs, tail, q_dec,
                 k_state, k_dec) = [sem("p2_" + n) for n in names]
                groups = [(ACT.Sigmoid, f), (ACT.Silu, q), (ACT.Copy, lru_x), (ACT.Copy, v), (ACT.Gelu_apprx_tanh, lru_g), (ACT.Silu, g)]
                n_pairs = len(groups) * HG // 2
                with nc.Block() as block:
                    @block.sync
                    def _(sp):
                        stream_tiles(sp, tile_of(A["w_in_2"]), w, n_pairs, lambda: sp.dma_start(
                            x_rows.rearrange("(k p) s -> p k s", p=P), x[:]).then_inc(x_out, 16))
                        sp.wait_ge(x_out, 16)

                    @block.gpsimd
                    def _(pool):
                        pool.memset(reset, 1.0).then_inc(reset_done, 1)
                        pool.wait_ge(reset_done, 1)
                        pool.memset(reset.rearrange("p (c t) -> p c t", t=CHUNK)[:, :, 0:1], 0.0).then_inc(reset_done, 1)
                        split_tiles(pool, w, n_pairs)

                    @block.tensor
                    def _(pe):
                        norm_pe(pe, t)
                        linear(pe, xn_hi, xn_lo, DT, w, n_pairs, lo_done)

                    @block.scalar
                    def _(act):
                        def take(n):
                            func, dst = groups[n // HG]
                            act.wait_ge(done[n % 2], n // 2 + 2)
                            act.activation(dst[:, n % HG, :], banks(4 * (n % 2)), func).then_inc(read[n % 2], 1)

                        def decays(h):
                            b = h % 2
                            act.wait_ge(cums, h + 1)
                            act.activation(f[:, h, :], cum[:, b, :], ACT.Exp).then_inc(grow, 1)
                            act.wait_ge(diffs, h + 1)
                            act.wait_ge(grow, h + 1)
                            act.activation(cum[:, b, :], cum[:, b, :], ACT.Exp, scale=-1.0).then_inc(shrink, 1)
                            act.activation(diff[:, b, :], diff[:, b, :], ACT.Exp).then_inc(tail, 1)

                        for b in range(2):
                            act.sem_inc(read[b], 1)
                        norm_act(act, t)
                        split_norm_act(act, full, xn_hi, scaled, hi_done)
                        act.wait_ge(lbs, 1)
                        act.activation(lb[:, 1, :], lb[:, 0, :], ACT.Sigmoid).then_inc(lb_act, 1)
                        for n in range(HG):
                            take(n)
                        for h in range(HG):
                            act.wait_ge(keys, 2 * h + 2)
                            act.activation(f[:, h, :], f[:, h, :], ACT.Ln).then_inc(logs, 1)
                        for pair in range(HG // 2):
                            for h in (2 * pair, 2 * pair + 1):
                                take(HG + h)
                            for h in (2 * pair, 2 * pair + 1):
                                decays(h)
                        act.wait_ge(lo_done, DT)
                        act.wait_ge(x_out, 16)
                        for n in range(2 * HG, 5 * HG):
                            take(n)
                        act.wait_ge(k_dec, HG)
                        for n in range(5 * HG, 6 * HG):
                            take(n)

                    @block.vector
                    def _(dve):
                        dve.tensor_tensor(lb[:, 0, :], s2("lb0"), s2("lb1"), ALU.subtract).then_inc(lbs, 1)
                        norm_dve(dve, t)
                        split_norm_dve(dve, full, s2("mix_norm"), xn_hi, xn_lo, scaled, hi_done, lo_done)
                        dve.wait_ge(lb_act, 1)
                        dve.tensor_scalar(lb[:, 2, :], lb[:, 1, :], -1.0, 1.0, ALU.mult, ALU.add).then_inc(lbs, 1)
                        dve.wait_ge(lbs, 2)
                        for h in range(HG):
                            dve.wait_ge(read[h % 2], h // 2 + 2)
                            dve.tensor_scalar(f[:, h, :], f[:, h, :], lb[:, 2, h:h + 1], lb[:, 1, h:h + 1], ALU.mult, ALU.add).then_inc(keys, 1)
                            dve.wait_ge(keys, 2 * h + 1)
                            dve.tensor_scalar(kd[:, h, :], f[:, h, :], -1.0, 1.0, ALU.mult, ALU.add).then_inc(keys, 1)
                        dve.wait_ge(reset_done, 2)

                        def sums(h):
                            b = h % 2
                            dve.wait_ge(logs, h + 1)
                            if h >= 2:
                                dve.wait_ge(k_dec, h - 1)
                                dve.wait_ge(k_state, h - 1)
                            dve.tensor_tensor_scan(cum[:, b, :], reset, f[:, h, :], 0.0, ALU.mult, ALU.add).then_inc(cums, 1)
                            dve.wait_ge(cums, h + 1)
                            by_chunk = cum[:, b, :].rearrange("p (c t) -> p c t", t=CHUNK)
                            dve.tensor_tensor(diff[:, b, :].rearrange("p (c t) -> p c t", t=CHUNK),
                                              by_chunk[:, :, CHUNK - 1:CHUNK].to_broadcast([P, NCH, CHUNK]), by_chunk, ALU.subtract).then_inc(diffs, 1)

                        def times(h):
                            b = h % 2
                            dve.wait_ge(read[h % 2], (HG + h) // 2 + 2)
                            dve.wait_ge(grow, h + 1)
                            dve.tensor_tensor(q[:, h, :], q[:, h, :], f[:, h, :], ALU.mult).then_inc(q_dec, 1)
                            dve.tensor_copy(last[:, h, :].unsqueeze(2), f[:, h, :].rearrange("p (c t) -> p c t", t=CHUNK)[:, :, CHUNK - 1:CHUNK]).then_inc(q_dec, 1)
                            dve.wait_ge(tail, h + 1)
                            dve.wait_ge(q_dec, 2 * h + 2)
                            dve.tensor_tensor(f[:, h, :], kd[:, h, :], diff[:, b, :], ALU.mult).then_inc(k_state, 1)
                            dve.wait_ge(k_state, h + 1)
                            dve.tensor_tensor(kd[:, h, :], kd[:, h, :], cum[:, b, :], ALU.mult).then_inc(k_dec, 1)

                        for pair in range(HG // 2):
                            for h in (2 * pair, 2 * pair + 1):
                                sums(h)
                            for h in (2 * pair, 2 * pair + 1):
                                times(h)

        def mixers(mix, qfg, lru_x, lru, v, kd, last, s2):
            q, ks, g = (qfg[:, i, :, :] for i in range(3))
            with ExitStack() as ctx:
                kd_s, ks_s, v_s = (sb(n, [P, HG, P], F32, ctx) for n in ("kd_s", "ks_s", "v_s"))
                q_s = sb("q_s", [P, 2, HG, P], F32, ctx)
                last_s = sb("last_s", [P, 2, HG, CPB], F32, ctx)
                ks_t = sb("ks_t", [P, 2, HG, P], F32, ctx)
                v_t = sb("v_t", [P, 2, HG, P], F32, ctx)
                sc_t = sb("sc_t", [P, 2, HG, P], F32, ctx)
                state = sb("hc_state", [P, 2 * CPB, HG, P], F32, ctx)
                causal = sb("causal", [P, HG, P], U32, ctx)
                sq = sb("hc_sq", [P, HG, P], F32, ctx)
                block_ss = sb("hc_block_ss", [P, HG], F32, ctx)
                ss = sb("hc_ss", [P, TB, HG], F32, ctx)
                root = sb("hc_root", [P, TB, HG], F32, ctx)
                rstd = sb("hc_rstd", [P, TB, HG], F32, ctx)
                names = ("init", "staged", "q_staged", "scores", "ks_turned", "v_turned", "masked", "ks_copied", "v_copied",
                         "update", "state", "inter", "out_copied", "summed", "root", "rstd")
                (init, staged, q_staged, scores, ks_turned, v_turned, masked, ks_copied, v_copied, update, state_done, inter,
                 out_copied, summed, rooted, inverted) = [sem("hc_" + n) for n in names]
                scaled = [sem(f"hc_scaled{b}") for b in range(2)]
                out_turned = [sem(f"hc_out_turned{b}") for b in range(2)]
                gated = [sem(f"hc_gated{b}") for b in range(2)]
                w_a, w_x = (sb(n, [P, LT, P], F32, ctx) for n in ("w_a", "w_x"))
                wa_s, wx_s = (sb(n, [P, P], F32, ctx) for n in ("wa_s", "wx_s"))
                xc, r, ig, a, th, wide = (sb("lru_" + n, [P, S], F32, ctx) for n in ("xc", "r", "ig", "a", "th", "wide"))
                sp_col = sb("lru_sp", [P, 8, LT], F32, ctx)
                names = ("zeroed", "w_in", "col", "col_act", "w_staged", "conv", "prod", "gates", "decay", "step", "rooted")
                zeroed, w_in, col, col_act, w_staged, conv, prod, gates, decay, lru_step, lru_rooted = [sem("ru_" + n) for n in names]
                absneg, u, w1, lnw, d, rd, zero, rate = (sp_col[:, i, :] for i in range(8))
                STATE = HG * CPB
                N_LRU = 6
                score_bank, ks_bank, v_bank, update_bank, out_bank = 0, 1, 2, 3, 7
                rows_s = [ks_t[:, b, :, :] for b in range(2)]
                gate_banks = (3, 5)

                def heads_of(i):
                    return bank(i).rearrange("p (h m) -> p h m", m=P)

                with nc.Block() as block:
                    @block.sync
                    def _(sp):
                        sp.wait_ge(zeroed, 2)
                        for w, name in ((w_a, "lru_wa"), (w_x, "lru_wx")):
                            for half in range(2):
                                at = slice(half * 64, half * 64 + 64)
                                sp.dma_start(w[at, :, at], A[name].rearrange("(n two) d e -> two d n e", two=2)[half]).then_inc(w_in, 16)

                    @block.gpsimd
                    def _(pool):
                        def stage(t):
                            at = block_of(t)
                            pool.tensor_copy(kd_s[:], kd[:, :, at]).then_inc(staged, 1)
                            pool.tensor_copy(ks_s[:], ks[:, :, at]).then_inc(staged, 1)
                            pool.tensor_copy(v_s[:], v[:, :, at]).then_inc(staged, 1)

                        def stage_q(t, slot):
                            pool.tensor_copy(q_s[:, slot, :, :], q[:, :, block_of(t)]).then_inc(q_staged, 1)
                            chunks = slice(t * CPB, (t + 1) * CPB) if isinstance(t, int) else bass.ds(t * CPB, CPB)
                            pool.tensor_copy(last_s[:, slot, :, :], last[:, :, chunks]).then_inc(q_staged, 1)

                        def stage_weights(j):
                            pool.tensor_copy(wa_s[:], w_a[:, j, :] if isinstance(j, int) else w_a[:, bass.ds(j, 1), :].rearrange("p a m -> p (a m)")).then_inc(w_staged, 1)
                            pool.tensor_copy(wx_s[:], w_x[:, j, :] if isinstance(j, int) else w_x[:, bass.ds(j, 1), :].rearrange("p a m -> p (a m)")).then_inc(w_staged, 1)

                        pool.memset(w_a[:], 0.0).then_inc(zeroed, 1)
                        pool.memset(w_x[:], 0.0).then_inc(zeroed, 1)
                        stage(0)
                        pool.wait_ge(w_in, 64)
                        stage_weights(0)
                        for t in range(2):
                            stage_q(t, t)
                        for done in (scores, ks_turned, v_turned):
                            pool.wait_ge(done, 1)
                        stage(1)
                        with pool.Fori(0, LT) as j:
                            for slot in range(2):
                                t = 2 * j + slot
                                ahead = pool.snap(pool.to_reg((t + 2) % TB))
                                taken, used, stated, multiplied = [pool.snap(pool.to_reg(n)) for n in (
                                    t + 2, CPB * t + 2 * CPB, STATE * t + STATE + 1, 2 * j + 2)]
                                pool.wait_ge(scores, 1)
                                for done in (scores, ks_turned, v_turned):
                                    pool.wait_ge(done, taken)
                                stage(ahead)
                                if slot == 0:
                                    pool.wait_ge(prod, 1)
                                    pool.wait_ge(prod, multiplied)
                                    stage_weights(pool.snap(pool.to_reg((j + 1) % LT)))
                                pool.wait_ge(inter, 1)
                                pool.wait_ge(inter, used)
                                pool.wait_ge(state_done, stated)
                                stage_q(ahead, slot)
                        with pool.Fori(0, TB // 2) as i:
                            for b in range(2):
                                t = 2 * i + b
                                freed = pool.snap(pool.to_reg(i + 1))
                                pool.wait_ge(inverted, 1)
                                pool.wait_ge(out_turned[b], freed)
                                pool.tensor_tensor(rows_s[b], v[:, :, block_of(t)], rstd[:, bass.ds(t, 1), :].rearrange(
                                    "p a h -> p (a h)").unsqueeze(2).to_broadcast([P, HG, P]), ALU.mult).then_inc(scaled[b], 1)

                    @block.tensor
                    def _(pe):
                        def turn(t):
                            pe.wait_ge(staged, 3 * t + 3)
                            if not isinstance(t, int):
                                pe.wait_ge(masked, t)
                                pe.wait_ge(ks_copied, t)
                                pe.wait_ge(v_copied, t)
                            at = block_of(t if isinstance(t, int) else t % TB)
                            for h in range(HG):
                                mm = pe.matmul(psum[:, score_bank, h * P:(h + 1) * P], kd_s[:, h, :], q[:, h, at], start=True, stop=True)
                            mm.then_inc(scores, 1)
                            for h in range(HG):
                                mm = pe.transpose(psum[:, ks_bank, h * P:(h + 1) * P], ks_s[:, h, :], ident)
                            mm.then_inc(ks_turned, 1)
                            for h in range(HG):
                                mm = pe.transpose(psum[:, v_bank, h * P:(h + 1) * P], v_s[:, h, :], ident)
                            mm.then_inc(v_turned, 1)

                        for done in (inter, update):
                            pe.sem_inc(done, CPB)
                        for b in range(2):
                            pe.sem_inc(out_turned[b], 1)
                        turn(0)
                        pe.wait_ge(init, 2 + HG)
                        with pe.Fori(0, LT) as j:
                            pe.wait_ge(conv, LTAPS * j + LTAPS)
                            pe.wait_ge(w_staged, 2 * j + 2)
                            pe.wait_ge(state_done, 2 * STATE * j + 1)
                            for n, w in ((0, wa_s), (1, wx_s)):
                                for half in range(2):
                                    mm = pe.matmul(bank(gate_banks[n] + half), w[:], xc[:, half * HALF:(half + 1) * HALF], start=True, stop=True)
                                mm.then_inc(prod, 1)
                            for slot in range(2):
                                t = 2 * j + slot
                                turn(t + 1)
                                pe.wait_ge(ks_copied, t + 1)
                                pe.wait_ge(v_copied, t + 1)
                                pe.wait_ge(state_done, STATE * t + 1)
                                if slot == 0:
                                    pe.wait_ge(gates, 2 * j + 2)
                                for c in range(CPB):
                                    at = slice(c * CHUNK, (c + 1) * CHUNK)
                                    for h in range(HG):
                                        mm = pe.matmul(psum[:, update_bank + c, h * P:(h + 1) * P], ks_t[at, slot, h, :], v_t[at, slot, h, :],
                                                       start=True, stop=True, tile_position=(c * CHUNK, 0))
                                    mm.then_inc(update, 1)
                                pe.wait_ge(masked, t + 1)
                                pe.wait_ge(out_copied, t + 1)
                                for h in range(HG):
                                    pe.matmul(psum[:, out_bank, h * P:(h + 1) * P], sc_t[:, slot, h, :], v_t[:, slot, h, :],
                                              start=h == 0, stop=False, skip_group_check=True)
                                pe.wait_ge(q_staged, 2 * t + 2)
                                for c in range(CPB):
                                    at = slice(c * CHUNK, (c + 1) * CHUNK)
                                    pe.wait_ge(state_done, STATE * t + HG * c + 1)
                                    for h in range(HG):
                                        mm = pe.matmul(psum[at, out_bank, h * P:(h + 1) * P], q_s[:, slot, h, at], state[:, slot * CPB + c, h, :],
                                                       start=False, stop=True, skip_group_check=True, tile_position=(0, c * CHUNK))
                                    mm.then_inc(inter, 1)
                        with pe.Fori(0, TB // 2) as i:
                            for b in range(2):
                                pe.wait_ge(scaled[b], i + 1)
                                pe.wait_ge(gated[b], i + 1)
                                for h in range(HG):
                                    mm = pe.transpose(psum[:, b, h * P:(h + 1) * P], rows_s[b][:, h, :], ident)
                                mm.then_inc(out_turned[b], 1)

                    @block.scalar
                    def _(act):
                        def copies(t, slot):
                            act.wait_ge(ks_turned, t + 1)
                            if not isinstance(t, int):
                                act.wait_ge(update, CPB * t)
                            act.copy(ks_t[:, slot, :, :], heads_of(ks_bank)).then_inc(ks_copied, 1)
                            act.wait_ge(v_turned, t + 1)
                            if not isinstance(t, int):
                                act.wait_ge(inter, CPB * t - CPB + 1)
                            act.copy(v_t[:, slot, :, :], heads_of(v_bank)).then_inc(v_copied, 1)

                        def outputs(t):
                            act.wait_ge(inter, CPB * t + 2 * CPB)
                            act.copy(v[:, :, block_of(t)], heads_of(out_bank)).then_inc(summed, 1)
                            for h in range(HG):
                                act.activation(sq[:, h, :], psum[:, out_bank, h * P:(h + 1) * P], ACT.Square,
                                               accum_out=block_ss[:, h:h + 1]).then_inc(summed, 1)
                            act.wait_ge(summed, (1 + HG) * t + 1 + HG)
                            act.copy(ss[:, bass.ds(t, 1), :].rearrange("p a h -> p (a h)"), block_ss[:]).then_inc(out_copied, 1)

                        act.sem_inc(out_copied, 1)
                        copies(0, 0)
                        act.wait_ge(col, 2)
                        act.activation(rate, absneg, ACT.Exp).then_inc(col_act, 1)
                        act.wait_ge(col, 3)
                        act.activation(lnw, w1, ACT.Ln).then_inc(col_act, 1)
                        act.wait_ge(col, 13)
                        with act.Fori(0, LT) as j:
                            one = bass.ds(j, 1)
                            act.wait_ge(prod, 2 * j + 1)
                            act.wait_ge(lru_step, N_LRU * j + 1)
                            act.activation(r[:], banks(gate_banks[0]), ACT.Sigmoid, bias=s2("ba")[:, one]).then_inc(gates, 1)
                            act.wait_ge(prod, 2 * j + 2)
                            act.activation(ig[:], banks(gate_banks[1]), ACT.Sigmoid, bias=s2("bx")[:, one]).then_inc(gates, 1)
                            copies(2 * j + 1, 1)
                            act.wait_ge(gates, 2 * j + 1)
                            act.activation(a[:], r[:], ACT.Exp, scale=zero[:, one]).then_inc(decay, 1)
                            act.activation(th[:], r[:], ACT.Tanh, scale=d[:, one]).then_inc(decay, 1)
                            outputs(2 * j)
                            copies(2 * j + 2, 0)
                            act.wait_ge(lru_step, N_LRU * j + 4)
                            act.activation(wide[:], wide[:], ACT.Sqrt).then_inc(lru_rooted, 1)
                            outputs(2 * j + 1)
                        act.wait_ge(out_copied, TB + 1)
                        act.activation(root[:], ss[:], ACT.Sqrt, bias=EPS, scale=1.0 / P).then_inc(rooted, 1)

                    @block.vector
                    def _(dve):
                        def mask(t, slot):
                            scored = t + 1 if isinstance(t, int) else dve.snap(dve.to_reg(t + 1))
                            used = None if isinstance(t, int) else dve.snap(dve.to_reg(CPB * t - CPB + 1))
                            dve.wait_ge(init, 2 + HG)
                            if used is not None:
                                dve.wait_ge(inter, used)
                            dve.wait_ge(scores, scored)
                            dve.copy_predicated(sc_t[:, slot, :, :].rearrange("p h m -> p (h m)"), causal[:].rearrange("p h m -> p (h m)"),
                                                bank(score_bank)).then_inc(masked, 1)

                        def states(t, slot):
                            dve.wait_ge(q_staged, 2 * t + 2)
                            for c in range(CPB):
                                dve.wait_ge(update, CPB * t + c + CPB + 1)
                                dve.wait_ge(state_done, STATE * t + HG * c + 1)
                                n = slot * CPB + c
                                for h in range(HG):
                                    dve.scalar_tensor_tensor(out=state[:, (n + 1) % (2 * CPB), h, :], in0=state[:, n, h, :],
                                                             scalar=last_s[:, slot, h, c:c + 1], in1=psum[:, update_bank + c, h * P:(h + 1) * P],
                                                             op0=ALU.mult, op1=ALU.add).then_inc(state_done, 1)

                        def convolve(j, backs):
                            cw, cb = s2("conv_w"), s2("conv_b")
                            one = (lambda n: slice(n, n + 1)) if isinstance(j, int) else (lambda n: bass.ds(n, 1))
                            for back in backs:
                                tap = cw[:, one(j * LTAPS + LTAPS - 1 - back)]
                                src = lru_x[:, one(j), 0:S - back].rearrange("p a s -> p (a s)")
                                if back == 0:
                                    ins = dve.tensor_scalar(xc[:], src, tap, cb[:, one(j)], ALU.mult, ALU.add)
                                else:
                                    ins = dve.scalar_tensor_tensor(out=xc[:, back:], in0=src, scalar=tap, in1=xc[:, back:],
                                                                   op0=ALU.mult, op1=ALU.add)
                                yield ins.then_inc(conv, 1)

                        dve.memset(state[:, 0, :, :], 0.0).then_inc(init, 1)
                        dve.memset(sc_t[:], 0.0).then_inc(init, 1)
                        for h in range(HG):
                            dve.tensor_copy(causal[:, h, :], cc("causal")).then_inc(init, 1)
                        dve.sem_inc(state_done, 1)
                        dve.sem_inc(lru_step, 1)
                        for b in range(2):
                            dve.sem_inc(gated[b], 1)
                        for back, _ in enumerate(convolve(0, range(LTAPS))):
                            dve.wait_ge(conv, back + 1)
                        mask(0, 0)
                        cs = Chain(dve, col)
                        la = s2("lru_a")
                        cs.step(dve.tensor_scalar(u, la, -1.0, None, ALU.mult))
                        cs.step(dve.tensor_tensor(absneg, la, u, ALU.min))
                        dve.wait_ge(col_act, 1)
                        cs.step(dve.tensor_scalar(w1, rate, 1.0, None, ALU.add))
                        cs.step(dve.tensor_scalar(d, w1, -1.0, None, ALU.add))
                        cs.step(dve.tensor_scalar(zero, d, 0.0, None, ALU.is_equal))
                        cs.step(dve.tensor_scalar(d, d, 1e-30, None, ALU.max))
                        cs.step(dve.reciprocal(rd, d))
                        dve.wait_ge(col_act, 2)
                        cs.step(dve.tensor_tensor(rd, rd, lnw, ALU.mult))
                        cs.step(dve.tensor_tensor(rd, rd, zero, ALU.add))
                        cs.step(dve.tensor_tensor(rd, rd, rate, ALU.mult))
                        cs.step(dve.scalar_tensor_tensor(out=u, in0=u, scalar=0.0, in1=rd, op0=ALU.max, op1=ALU.add))
                        cs.step(dve.tensor_scalar(d, u, LRU_C, None, ALU.mult))
                        cs.step(dve.tensor_scalar(zero, u, -LRU_C, None, ALU.mult))
                        with dve.Fori(0, LT) as j:
                            nxt = (j + 1) % LT
                            step = N_LRU * j + 1
                            mask(2 * j + 1, 1)
                            states(2 * j, 0)
                            dve.wait_ge(gates, 2 * j + 2)
                            dve.tensor_tensor(ig[:], ig[:], xc[:], ALU.mult).then_inc(lru_step, 1)
                            dve.wait_ge(decay, 2 * j + 2)
                            dve.tensor_tensor(wide[:], a[:], a[:], ALU.mult).then_inc(lru_step, 1)
                            dve.wait_ge(lru_step, step + 2)
                            dve.scalar_tensor_tensor(out=wide[:], in0=wide[:], scalar=1.0, in1=th[:], op0=ALU.add, op1=ALU.mult).then_inc(lru_step, 1)
                            for back, _ in enumerate(convolve(nxt, range(2))):
                                dve.wait_ge(conv, LTAPS * j + LTAPS + back + 1)
                            mask(2 * j + 2, 0)
                            states(2 * j + 1, 1)
                            for back, _ in enumerate(convolve(nxt, range(2, LTAPS))):
                                dve.wait_ge(conv, LTAPS * j + LTAPS + 3 + back)
                            dve.wait_ge(lru_rooted, j + 1)
                            dve.tensor_tensor(wide[:], wide[:], ig[:], ALU.mult).then_inc(lru_step, 1)
                            dve.wait_ge(lru_step, step + 4)
                            dve.tensor_tensor_scan(r[:], a[:], wide[:], 0.0, ALU.mult, ALU.add).then_inc(lru_step, 1)
                            dve.wait_ge(lru_step, step + 5)
                            tile = lru[:, bass.ds(j, 1), :].rearrange("p a s -> p (a s)")
                            dve.tensor_tensor(tile, r[:], tile, ALU.mult).then_inc(lru_step, 1)
                        dve.wait_ge(rooted, 1)
                        dve.reciprocal(rstd[:].rearrange("p t h -> p (t h)"), root[:].rearrange("p t h -> p (t h)")).then_inc(inverted, 1)
                        with dve.Fori(0, TB // 2) as i:
                            for b in range(2):
                                at = block_of(2 * i + b)
                                dve.wait_ge(out_turned[b], i + 2)
                                dve.scalar_tensor_tensor(out=mix[:, 0:HG, at], in0=heads_of(b), scalar=s2("hg_norm"), in1=g[:, :, at],
                                                         op0=ALU.mult, op1=ALU.mult).then_inc(gated[b], 1)

        def feed_forward(gain):
            G = 2
            groups = FFT // G
            per_group = DT // 2
            with ExitStack() as ctx:
                hn_hi, hn_lo = (sb("hn_" + n, [P, DT, S], F32R, ctx) for n in ("hi", "lo"))
                hid_hi, hid_lo = (sb("ff_hid_" + n, [P, 2 * G, S], F32R, ctx) for n in ("hi", "lo"))
                full = sb("ff_full", [P, 2, S], F32, ctx)
                sil, prod = full[:, 0, :], full[:, 1, :]
                t = norm_tensors("n4", ctx)
                w = split_tensors("up", DT, ctx)
                wd_raw = sb("wd_raw", [P, G, D], F32, ctx)
                wd_hi, wd_lo = (sb("wd_" + n, [P, G, D], F32R, ctx) for n in ("hi", "lo"))
                last_down = {n: [w[n][j].rearrange("p k m -> p (k m)") for j in range(G)] for n in ("hi", "lo")}
                names = ("scaled", "hi_done", "lo_done", "hid_hi_done", "hid_done", "wd_loaded", "wd_split", "sq_done", "sq_added")
                scaled, hi_done, lo_done, hid_hi_done, hid_done, wd_loaded, wd_split, sq_done, sq_added = [sem("ff_" + n) for n in names]
                down_done = [sem(f"ff_down_done{b}") for b in range(2)]
                down_read = [sem(f"ff_down_read{b}") for b in range(2)]
                done, read = w["done"], w["read"]
                gate_banks, up_banks, down_banks = 0, 4, (2, 6)

                with nc.Block() as block:
                    @block.sync
                    def _(sp):
                        tiles = tile_of(A["w_gate_up"])

                        def load_up(g):
                            for j in range(G):
                                for b in range(2):
                                    sp.wait_ge(w["split"][b], 2 * (G * g + j) + 1)
                                    sp.dma_start(w["raw"][b][:], tiles(2 * G * g + 2 * j + b)).then_inc(w["loaded"][b], 16)

                        def load_down(g):
                            sp.wait_ge(wd_split, 2 * g + 1)
                            sp.dma_start(wd_raw[:], A["w_down_2"][bass.ds(g * G * P, G * P), :].rearrange(
                                "(k p) n -> p k n", p=P)).then_inc(wd_loaded, 16)

                        load_up(0)
                        with sp.Fori(0, groups - 1) as g:
                            load_up(g + 1)
                            load_down(g)
                        load_down(groups - 1)

                    @block.gpsimd
                    def _(pool):
                        def split_up(g):
                            for j in range(G):
                                for b in range(2):
                                    split_tile(pool, w, b, G * g + j)

                        def split_down(g):
                            loaded, used = pool.snap(pool.to_reg(16 * g + 16)), pool.snap(pool.to_reg(per_group * g + 2 * per_group))
                            pool.wait_ge(wd_loaded, 16)
                            pool.wait_ge(wd_loaded, loaded)
                            pool.wait_ge(down_done[1], used)
                            pool.tensor_scalar(wd_hi[:], wd_raw[:], 1.0, None, ALU.mult).then_inc(wd_split, 1)
                            pool.wait_ge(wd_split, 2 * g + 2)
                            pool.tensor_tensor(wd_lo[:], wd_raw[:], wd_hi[:].bitcast(F32), ALU.subtract).then_inc(wd_split, 1)

                        for b in range(2):
                            pool.sem_inc(w["split"][b], 1)
                        pool.sem_inc(wd_split, 1)
                        split_up(0)
                        with pool.Fori(0, groups - 1) as g:
                            split_up(g + 1)
                            split_down(g)
                        last = groups - 1
                        pool.wait_ge(wd_loaded, 16 * groups)
                        for j in range(G):
                            pool.wait_ge(done[j], G * groups + 1)
                            pool.tensor_scalar(last_down["hi"][j], wd_raw[:, j, :], 1.0, None, ALU.mult).then_inc(wd_split, 1)
                        for j in range(G):
                            pool.wait_ge(wd_split, 2 * last + 2 + j)
                            pool.tensor_tensor(last_down["lo"][j], wd_raw[:, j, :], last_down["hi"][j].bitcast(F32),
                                               ALU.subtract).then_inc(wd_split, 1)

                    @block.tensor
                    def _(pe):
                        def first_up():
                            for part in range(2):
                                for b, out in ((0, gate_banks), (1, up_banks)):
                                    if part == 0:
                                        pe.wait_ge(w["split"][b], 3)
                                        pe.wait_ge(read[b], 1)
                                    for k in range(part * DT // 2, (part + 1) * DT // 2):
                                        pe.wait_ge(lo_done, k + 1)
                                        mm = products(pe, out, w["hi"][b][:, k, :], w["lo"][b][:, k, :], hn_hi[:, k, :],
                                                      hn_lo[:, k, :], k == 0, k == DT - 1)
                                    if part:
                                        mm.then_inc(done[b], 1)

                        def up(g, tiles=range(G)):
                            for j in tiles:
                                for b, out in ((0, gate_banks), (1, up_banks)):
                                    pe.wait_ge(w["split"][b], 2 * (G * g + j) + 3)
                                    pe.wait_ge(read[b], G * g + j + 1)
                                    for k in range(DT):
                                        mm = products(pe, out, w["hi"][b][:, k, :], w["lo"][b][:, k, :], hn_hi[:, k, :],
                                                      hn_lo[:, k, :], k == 0, k == DT - 1)
                                    mm.then_inc(done[b], 1)

                        def down(g, slot, split, w_hi, w_lo):
                            pe.wait_ge(wd_split, split)
                            pe.wait_ge(hid_done, G * g + G + 1)
                            for o in range(DT):
                                b = o % 2
                                pe.wait_ge(down_read[b], per_group * g + o // 2 + 1)
                                at = slice(o * P, (o + 1) * P)
                                for j in range(G):
                                    mm = products(pe, down_banks[b], w_hi[j][:, at], w_lo[j][:, at], slot(hid_hi, j), slot(hid_lo, j),
                                                  j == 0, j == G - 1)
                                mm.then_inc(down_done[b], 1)

                        for b in range(2):
                            pe.sem_inc(done[b], 1)
                        for b in range(2):
                            pe.sem_inc(down_done[b], 2 * per_group)
                        norm_pe(pe, t)
                        first_up()
                        up(0, range(1, G))
                        with pe.Fori(0, groups - 1) as g:
                            up(g + 1)
                            down(g, lambda part, j: part[:, bass.ds(G * (g % 2) + j, 1), :].rearrange("p a s -> p (a s)"), 2 * g + 3,
                                 *([part[:, j, :] for j in range(G)] for part in (wd_hi, wd_lo)))
                        last = groups - 1
                        down(last, lambda part, j: part[:, G * (last % 2) + j, :], 2 * last + 2 * G + 1, last_down["hi"], last_down["lo"])

                    @block.scalar
                    def _(act):
                        def gates(g, slot):
                            for j in range(G):
                                n = G * g + j
                                act.wait_ge(done[0], n + 2)
                                act.wait_ge(read[1], n + 1)
                                act.activation(sil, banks(gate_banks), ACT.Silu).then_inc(read[0], 1)
                                act.wait_ge(read[1], n + 2)
                                act.wait_ge(down_done[1], per_group * g + per_group)
                                act.copy(slot(hid_hi, j), prod).then_inc(hid_hi_done, 1)

                        act.sem_inc(read[0], 1)
                        norm_act(act, t)
                        split_norm_act(act, full, hn_hi, scaled, hi_done)
                        act.wait_ge(lo_done, DT)
                        with act.Fori(0, groups) as g:
                            gates(g, lambda part, j: part[:, bass.ds(G * (g % 2) + j, 1), :].rearrange("p a s -> p (a s)"))
                        for o in range(DT):
                            act.wait_ge(down_read[o % 2], per_group * (groups - 1) + o // 2 + 2)
                            if o >= 2:
                                act.wait_ge(sq_added, max(1, o - 2))
                            act.activation(full[:, o % 2, :], x[:, o, :], ACT.Square).then_inc(sq_done, 1)

                    @block.vector
                    def _(dve):
                        def hidden(g, slot):
                            for j in range(G):
                                n = G * g + j
                                dve.wait_ge(done[1], n + 2)
                                dve.wait_ge(read[0], n + 2)
                                dve.wait_ge(hid_done, n + 1)
                                dve.tensor_tensor(prod, banks(up_banks), sil, ALU.mult).then_inc(read[1], 1)
                                dve.wait_ge(hid_hi_done, n + 1)
                                dve.tensor_tensor(slot(hid_lo, j), prod, slot(hid_hi, j).bitcast(F32), ALU.subtract).then_inc(hid_done, 1)

                        def add_square(o):
                            dve.wait_ge(sq_done, o + 1)
                            if o > 1:
                                dve.wait_ge(sq_added, o - 1)
                            dve.tensor_tensor(sq_sum[:], full[:, 0, :] if o == 1 else sq_sum[:], full[:, o % 2, :],
                                              ALU.add).then_inc(sq_added, 1)

                        def add(g, square=False):
                            for o in range(DT):
                                b = o % 2
                                dve.wait_ge(down_done[b], per_group * (g + 2) + o // 2 + 1)
                                dve.tensor_tensor(x[:, o, :], banks(down_banks[b]), x[:, o, :], ALU.add).then_inc(down_read[b], 1)
                                if square and o >= 2:
                                    add_square(o - 1)
                            if square:
                                add_square(DT - 1)

                        dve.sem_inc(read[1], 1)
                        dve.sem_inc(hid_done, 1)
                        for b in range(2):
                            dve.sem_inc(down_read[b], 1)
                        norm_dve(dve, t)
                        split_norm_dve(dve, full, gain, hn_hi, hn_lo, scaled, hi_done, lo_done)
                        slot = lambda g: lambda part, j: part[:, bass.ds(G * (g % 2) + j, 1), :].rearrange("p a s -> p (a s)")
                        hidden(0, lambda part, j: part[:, j, :])
                        with dve.Fori(0, groups - 1) as g:
                            hidden(g + 1, slot(g + 1))
                            add(g)
                        add(groups - 1, True)

        def final_norm(out, gain):
            with ExitStack() as ctx:
                res = sb("res", [P, DT, S], F32, ctx)
                t = norm_tensors("n5", ctx)
                scaled, stored = sem("fn_scaled"), sem("fn_stored")
                with nc.Block() as block:
                    @block.tensor
                    def _(pe):
                        norm_pe(pe, t)

                    @block.scalar
                    def _(act):
                        norm_act(act, t)

                    @block.vector
                    def _(dve):
                        norm_dve(dve, t)
                        scale_rows(dve, res, gain, scaled)

                    @block.sync
                    def _(sp):
                        for k in range(DT):
                            sp.wait_ge(scaled, k + 1)
                            sp.dma_start(out[k * P:(k + 1) * P, :], res[:, k, :]).then_inc(stored, 16)
                        sp.wait_ge(stored, 16 * DT)

        with own_semaphores():
            setup()
        with nc.Fori(0, DEPTH) as l:
            layer(l)
        first_only.close()
        second(A["out"])
    return sem_names


def host_arrays(inputs):
    f = {n: np.asarray(a) for n, a in inputs.items()}

    def cols(v, rows=P):
        v = np.asarray(v)
        return np.ascontiguousarray(v.reshape(-1, rows).T)

    def tiles(w):
        k, n = w.shape
        return np.ascontiguousarray(w.reshape(k // P, P, n // P, P).transpose(2, 1, 0, 3).reshape(n // P, P, k))

    o2 = Q_RANK + KV_RANK
    o3 = o2 + ROPE
    w_in, layer_cols, w_uq, w_uk, w_uv = [], [], [], [], []
    for l in range(DEPTH):
        w = f["w_in"][l]
        rope = w[:, o2:o3]
        val, gat = w[:, o3:o3 + CONV_CH], w[:, o3 + CONV_CH:]
        pairs = [p for j in range(CT) for p in (gat[:, j * P:(j + 1) * P], val[:, j * P:(j + 1) * P])]
        w_in.append(tiles(np.concatenate(pairs + [w[:, :o2], rope, rope], axis=1)))
        uq = f["w_uq"][l].reshape(Q_RANK, HEADS, QK)
        uq = np.concatenate([uq[:, :, :NOPE].reshape(Q_RANK, -1), uq[:, :, NOPE:].reshape(Q_RANK, -1)], axis=1)
        w_uq.append(tiles(uq).transpose(1, 0, 2).reshape(P, -1))
        ukv = f["w_ukv"][l].reshape(KV_RANK, HEADS, NOPE + VD)
        w_uk.append(ukv[:, :, :NOPE].reshape(KV_RANK, -1))
        w_uv.append(ukv[:, :, NOPE:].reshape(KV_RANK, -1))
        conv_w = np.zeros((TAPS_PAD, CONV_CH), f["conv_w"].dtype)
        conv_w[:TAPS] = f["conv_w"][l]
        qg, kg = f["q_head_g"][l], f["k_head_g"][l]
        layer_cols.append(np.concatenate([
            cols(f["norm1_g"][l]), cols(f["norm2_g"][l]), cols(f["q_latent_g"][l]), cols(f["kv_latent_g"][l]),
            cols(qg[:NOPE]), cols(np.concatenate([qg[NOPE:], qg[NOPE:]])),
            cols(kg[:NOPE]), cols(np.concatenate([kg[NOPE:], kg[NOPE:]])),
            conv_w.reshape(TAPS_PAD, CT, P).transpose(2, 1, 0).reshape(P, -1),
            cols(f["conv_b"][l]), cols(f["conv_norm_g"][l]), cols(f["conv_norm_b"][l])], axis=1))
    w2 = f["w_in_2"][0]
    hw = HG * P
    w2_tiled = np.concatenate([w2[:, n * hw:(n + 1) * hw] for n in (1, 0, 4, 2, 5, 3)], axis=1)
    gu = f["w_gate_up_2"][0]
    gu = np.stack([gu[:, :DFF].reshape(D, FFT, P), gu[:, DFF:].reshape(D, FFT, P)], axis=2).reshape(D, 2 * DFF)
    second_cols = np.concatenate([
        cols(f["mix_norm_w_2"][0]), cols(f["hg_lb_2"][0]), cols(f["hg_lb_2"][1]), cols(f["hg_norm_w_2"][0]),
        f["conv_w_2"][0].reshape(LTAPS, LT, P).transpose(2, 1, 0).reshape(P, -1), cols(f["conv_b_2"][0]),
        cols(f["lru_ba_2"][0]), cols(f["lru_bx_2"][0]), cols(f["lru_a_2"][0]), cols(f["ffn_norm_w_2"][0]),
        cols(f["final_norm_w_2"])], axis=1)

    consts = np.zeros((P, N_CONST), np.float32)
    n = np.arange(P)
    consts[:, CC["ident"][0]:CC["ident"][1]] = np.eye(P)
    for r in range(2 * ADA_BUFS):
        consts[r, CC["fold"][0] + r % ADA_BUFS] = 1
    consts[:, CC["flip"][0]:CC["flip"][1]] = np.eye(P)[::-1]
    consts[:, CC["ones"][0]:CC["ones"][1]] = 1
    m = n % ROPE
    for r in range(P):
        if m[r] < ROPE // 2:
            consts[r + ROPE // 2, CC["turn"][0] + r] = -1
        else:
            consts[r - ROPE // 2, CC["turn"][0] + r] = 1
    consts[:, CC["causal"][0]:CC["causal"][1]] = (n[:, None] // CHUNK == n[None, :] // CHUNK) & (n[:, None] <= n[None, :])
    sel = np.zeros((P, 11, 2 * HEADS), np.float32)
    for h in range(HEADS):
        sel[:, h, h] = 1
        sel[:, 6 + h, HEADS + h] = 1
        sel[(h % 2) * ROPE:(h % 2 + 1) * ROPE, HEADS + h // 2, h] = 1
        sel[:ROPE, 10, HEADS + h] = 1
    consts[:, CC["sel"][0]:CC["sel"][1]] = sel.reshape(P, -1)
    consts[:, CC["inv_freq"][0]] = (np.float32(1) / (10000.0 ** (np.arange(0, ROPE, 2) / ROPE)).astype(np.float32))[n % (ROPE // 2)]
    return {
        "x_t": np.ascontiguousarray(f["x"][0].T), "c_cols": cols(f["c"][0]), "consts": consts,
        "positions": np.ascontiguousarray(f["positions"]),
        "b_ada_cols": cols(f["b_ada"]),
        "w_ada": np.ascontiguousarray(f["w_ada"].reshape(DEPTH, D, N_MOD * D // HALF, HALF).transpose(0, 2, 1, 3).reshape(-1, D, HALF)),
        "layer_cols": np.ascontiguousarray(np.stack(layer_cols)),
        "w_in": np.concatenate(w_in), "w_uq": np.ascontiguousarray(np.stack(w_uq)), "w_uk": np.ascontiguousarray(np.stack(w_uk)),
        "w_uv": np.ascontiguousarray(np.stack(w_uv)),
        "w_out": np.concatenate([tiles(f["w_out"][l]) for l in range(DEPTH)]),
        "w_router": np.ascontiguousarray(f["w_router"]),
        "w_gate": f["w_gate"].reshape(-1, D, FF), "w_up": f["w_up"].reshape(-1, D, FF), "w_down": f["w_down"].reshape(-1, FF, D),
        "second_cols": np.ascontiguousarray(second_cols),
        "w_in_2": tiles(w2_tiled),
        "lru_wa": np.ascontiguousarray(f["lru_wa_2"][0]), "lru_wx": np.ascontiguousarray(f["lru_wx_2"][0]),
        "w_out_2": tiles(f["w_out_2"][0]), "w_gate_up": tiles(gu), "w_down_2": np.ascontiguousarray(f["w_down_2"][0]),
    }


def kernel(**inputs):
    import concourse.bacc as bacc
    from concourse.bass_utils import run_bass_kernel_spmd

    nc = bacc.Bacc("TRN2", target_bir_lowering=False, num_devices=1)
    arrays = host_arrays(inputs)
    aps = {n: nc.dram_tensor(n + "_dram", a.shape, mybir.dt.from_np(a.dtype), kind="ExternalInput").ap() for n, a in arrays.items()}
    aps["out"] = nc.dram_tensor("out_t", (D, S), F32, kind="ExternalOutput").ap()
    build(nc, aps)
    r = run_bass_kernel_spmd(nc, [{n + "_dram": a for n, a in arrays.items()}], core_ids=[0])
    return np.ascontiguousarray(r.results[0]["out_t"].T).reshape(1, S, D)
```
